# Optimizing a Trainium2 kernel written in Bass

```python
import jax
import jax.numpy as jnp
from jax import lax
import numpy as np

D_MODEL = 1024
BATCH = 1
SEQ = 128
DEPTH = 2
DEC_BATCH = 1
DEC_SEQ = 256
PAST_LEN = 128

GRID_W = 64
HEAD_DIM = 64
ROPE_BASE = 10000.0
QBLOCK = 128
A_HEADS = 8
A_KV_HEADS = 2
WINDOW = 128
B_HEADS = 8
B_DK = 64
B_DV = 64
RET_CHUNK = 128
C_HEADS = 16
NB_ROWS = 8
NB_COLS = 16
D_FF = 2816
N_EXPERTS = 8
TOP_K = 2
D_FF_EXPERT = 2816
N_EVEN = (DEPTH + 1) // 2
N_ODD = DEPTH // 2
EPS = 1e-6
NEG = -1e30
A_Q = A_HEADS * HEAD_DIM
A_KV = A_KV_HEADS * HEAD_DIM
B_QK = B_HEADS * B_DK
B_V = B_HEADS * B_DV
IN_EVEN = A_Q + 2 * A_KV + 2 * B_QK + 2 * B_V
MIX_EVEN = A_Q + B_V
C_W = C_HEADS * HEAD_DIM

kernel_name = 'hybrid_diffusion_prefix_step'

def _rmsnorm(x, g):
    xf = x.astype(jnp.float32)
    y = xf * lax.rsqrt(jnp.mean(xf * xf, axis=-1, keepdims=True) + EPS)
    return (y * g.astype(jnp.float32)).astype(x.dtype)

def _adaln(cvec, w, b):
    m = (jax.nn.silu(cvec) @ w + b).reshape(-1, 1, 6 * D_MODEL)
    return jnp.split(m, 6, axis=-1)

def _modulate(h, shift, scale):
    return h * (1 + scale) + shift

def _rotate_half(x, ang):
    f = ang.shape[-1]
    xf = x.astype(jnp.float32)
    x1, x2 = xf[..., :f], xf[..., f:]
    cos = jnp.cos(ang)[:, None, :]
    sin = jnp.sin(ang)[:, None, :]
    return jnp.concatenate([x1 * cos - x2 * sin, x1 * sin + x2 * cos], axis=-1).astype(x.dtype)

def _rope2d(x):
    T = x.shape[1]
    half = HEAD_DIM // 2
    nf = half // 2
    t = jnp.arange(T)
    row = (t // GRID_W).astype(jnp.float32)
    col = (t % GRID_W).astype(jnp.float32)
    inv = ROPE_BASE ** (-jnp.arange(nf, dtype=jnp.float32) / nf)
    return jnp.concatenate([_rotate_half(x[..., :half], row[:, None] * inv),
                            _rotate_half(x[..., half:], col[:, None] * inv)], axis=-1)

def _softmax_sink(s, sink):
    if sink is None:
        return jax.nn.softmax(s, axis=-1)
    col = jnp.broadcast_to(sink, s.shape[:-1] + (1,))
    return jax.nn.softmax(jnp.concatenate([col, s], axis=-1), axis=-1)[..., 1:]

def _context_attention(q, k, v, sink):
    B, L, H, d = q.shape
    G = k.shape[2]
    rep = H // G
    nb = L // QBLOCK
    qb = q.reshape(B, nb, QBLOCK, G, rep, d).transpose(1, 0, 2, 3, 4, 5)
    sink_b = None if sink is None else sink.astype(jnp.float32).reshape(1, G, rep, 1, 1)

    def block(qblk):
        s = jnp.einsum('bqgrd,bkgd->bgrqk', qblk, k, preferred_element_type=jnp.float32) * d ** -0.5
        p = _softmax_sink(s, sink_b)
        return jnp.einsum('bgrqk,bkgd->bqgrd', p.astype(v.dtype), v)

    o = lax.map(block, qb)
    return o.transpose(1, 0, 2, 3, 4, 5).reshape(B, L, H * d)

def _window_attention(q, k, v, ck, cv, sink):
    B, T, H, d = q.shape
    G = k.shape[2]
    rep = H // G
    nb = T // QBLOCK
    Lc = ck.shape[1]

    def band(x):
        xp = jnp.pad(x, ((0, 0), (QBLOCK, QBLOCK), (0, 0), (0, 0))).reshape(B, nb + 2, QBLOCK, G, d)
        return jnp.concatenate([xp[:, :-2], xp[:, 1:-1], xp[:, 2:]], axis=2)

    kb, vb = band(k), band(v)
    qb = q.reshape(B, nb, QBLOCK, G, rep, d)
    scale = d ** -0.5
    s_loc = jnp.einsum('bnqgrd,bnkgd->bngrqk', qb, kb, preferred_element_type=jnp.float32) * scale
    s_ctx = jnp.einsum('bnqgrd,bkgd->bngrqk', qb, ck, preferred_element_type=jnp.float32) * scale
    n = jnp.arange(nb)[:, None, None]
    qpos = n * QBLOCK + jnp.arange(QBLOCK)[None, :, None]
    kpos = n * QBLOCK - QBLOCK + jnp.arange(3 * QBLOCK)[None, None, :]
    mask = (jnp.abs(kpos - qpos) <= WINDOW) & (kpos >= 0) & (kpos < T)
    s_loc = jnp.where(mask[None, :, None, None], s_loc, NEG)
    sink_b = sink.astype(jnp.float32).reshape(1, 1, G, rep, 1, 1)
    p = _softmax_sink(jnp.concatenate([s_ctx, s_loc], axis=-1), sink_b).astype(v.dtype)
    o = (jnp.einsum('bngrqk,bkgd->bnqgrd', p[..., :Lc], cv)
         + jnp.einsum('bngrqk,bnkgd->bnqgrd', p[..., Lc:], vb))
    return o.reshape(B, T, H * d)

def _retention_scan(q, k, v, log_g, s0):
    B, H, T, dk = q.shape
    dv = v.shape[-1]
    C = RET_CHUNK
    n = T // C
    idx = jnp.arange(C, dtype=jnp.float32)
    lg = log_g[:, None]
    q_dec = jnp.exp(lg * (idx + 1.0))[:, :, None]
    k_dec = jnp.exp(lg * (C - 1.0 - idx))[:, :, None]
    diff = idx[:, None] - idx[None, :]
    dmask = jnp.where(diff >= 0, jnp.exp(log_g[:, None, None] * jnp.maximum(diff, 0.0)), 0.0)
    chunk_dec = jnp.exp(log_g * C)[:, None, None]

    def chunks(x):
        return x.reshape(B, H, n, C, x.shape[-1]).transpose(2, 0, 1, 3, 4)

    def step(S, inp):
        qc, kc, vc = inp
        att = jnp.einsum('bhqd,bhkd->bhqk', qc, kc) * dmask
        o = jnp.einsum('bhqk,bhkv->bhqv', att, vc) + jnp.einsum('bhqd,bhdv->bhqv', qc * q_dec, S)
        S = S * chunk_dec + jnp.einsum('bhkd,bhkv->bhdv', kc * k_dec, vc)
        return S, o

    S, o = lax.scan(step, s0, (chunks(q), chunks(k), chunks(v)))
    return o.transpose(1, 2, 0, 3, 4).reshape(B, H, T, dv), S

def _retention_branch(qr, kr, vr, gr, lg_f, lg_b, s0f, s0b):
    B, L, _ = qr.shape

    def heads(x, dh):
        return x.reshape(B, L, B_HEADS, dh).transpose(0, 2, 1, 3).astype(jnp.float32)

    q = heads(qr, B_DK)
    k = heads(kr, B_DK) * B_DK ** -0.5
    v = heads(vr, B_DV)
    lf = jax.nn.log_sigmoid(lg_f.astype(jnp.float32))
    lb = jax.nn.log_sigmoid(lg_b.astype(jnp.float32))
    of, sf = _retention_scan(q, k, v, lf, s0f.astype(jnp.float32))
    ob, sb = _retention_scan(q[:, :, ::-1], k[:, :, ::-1], v[:, :, ::-1], lb, s0b.astype(jnp.float32))
    o = of + ob[:, :, ::-1]
    mu = jnp.mean(o, axis=-1, keepdims=True)
    var = jnp.mean(jnp.square(o - mu), axis=-1, keepdims=True)
    o = (o - mu) * lax.rsqrt(var + EPS)
    o = o.transpose(0, 2, 1, 3).reshape(B, L, B_V).astype(gr.dtype)
    return jax.nn.silu(gr) * o, sf.astype(qr.dtype), sb.astype(qr.dtype)

def _even_project(h, w_in):
    B, L, _ = h.shape
    sizes = [A_Q, A_KV, A_KV, B_QK, B_QK, B_V, B_V]
    offs = [int(o) for o in np.cumsum(sizes)[:-1]]
    qa, ka, va, qr, kr, vr, gr = jnp.split(h @ w_in, offs, axis=-1)
    qa = qa.reshape(B, L, A_HEADS, HEAD_DIM)
    ka = ka.reshape(B, L, A_KV_HEADS, HEAD_DIM)
    va = va.reshape(B, L, A_KV_HEADS, HEAD_DIM)
    return qa, ka, va, qr, kr, vr, gr

def _even_mixer_context(h, w_in, w_out, sink, lg_f, lg_b):
    B = h.shape[0]
    qa, ka, va, qr, kr, vr, gr = _even_project(h, w_in)
    oa = _context_attention(qa, ka, va, sink)
    zero = jnp.zeros((B, B_HEADS, B_DK, B_DV), jnp.float32)
    orr, sf, sb = _retention_branch(qr, kr, vr, gr, lg_f, lg_b, zero, zero)
    out = jnp.concatenate([oa, orr], axis=-1) @ w_out
    return out, ka, va, sf, sb

def _even_mixer_latent(h, ck, cv, s0f, s0b, w_in, w_out, sink, lg_f, lg_b):
    qa, ka, va, qr, kr, vr, gr = _even_project(h, w_in)
    oa = _window_attention(_rope2d(qa), _rope2d(ka), va, ck, cv, sink)
    orr, _, _ = _retention_branch(qr, kr, vr, gr, lg_f, lg_b, s0f, s0b)
    return jnp.concatenate([oa, orr], axis=-1) @ w_out

def _odd_project(h, w_qkv):
    B, L, _ = h.shape
    q, k, v = jnp.split(h @ w_qkv, 3, axis=-1)
    shp = (B, L, C_HEADS, HEAD_DIM)
    return q.reshape(shp), k.reshape(shp), v.reshape(shp)

def _odd_mixer_context(h, w_qkv, w_out):
    q, k, v = _odd_project(h, w_qkv)
    return _context_attention(q, k, v, None) @ w_out, k, v

def _neighborhood_attention(q, k, v, ck, cv, rpb):
    B, T, H, d = q.shape
    R = T // GRID_W
    WR = min(NB_ROWS, R)
    Lc = ck.shape[1]
    r = jnp.arange(R)
    krow = jnp.clip(r - WR // 2, 0, R - WR)[:, None] + jnp.arange(WR)[None, :]
    cq = jnp.arange(GRID_W)
    cstart = jnp.clip(cq - NB_COLS // 2, 0, GRID_W - NB_COLS)
    col_ok = (cq[None, :] >= cstart[:, None]) & (cq[None, :] < cstart[:, None] + NB_COLS)
    qg = q.reshape(B, R, GRID_W, H, d)
    kg = k.reshape(B, R, GRID_W, H, d)[:, krow]
    vg = v.reshape(B, R, GRID_W, H, d)[:, krow]
    scale = d ** -0.5
    s_nb = jnp.einsum('brqhd,brjkhd->brhqjk', qg, kg, preferred_element_type=jnp.float32) * scale
    dr = krow - r[:, None] + NB_ROWS - 1
    dc = jnp.clip(cq[None, :] - cq[:, None], 1 - NB_COLS, NB_COLS - 1) + NB_COLS - 1
    bias = rpb.astype(jnp.float32)[:, dr[:, None, :, None], dc[None, :, None, :]]
    s_nb = s_nb + bias.transpose(1, 0, 2, 3, 4)[None]
    s_nb = jnp.where(col_ok[:, None, :], s_nb, NEG).reshape(B, R, H, GRID_W, WR * GRID_W)
    s_ctx = jnp.einsum('brqhd,bkhd->brhqk', qg, ck, preferred_element_type=jnp.float32) * scale
    p = jax.nn.softmax(jnp.concatenate([s_ctx, s_nb], axis=-1), axis=-1).astype(v.dtype)
    p_nb = p[..., Lc:].reshape(B, R, H, GRID_W, WR, GRID_W)
    o = (jnp.einsum('brhqk,bkhd->brqhd', p[..., :Lc], cv)
         + jnp.einsum('brhqjk,brjkhd->brqhd', p_nb, vg))
    return o.reshape(B, T, H * d)

def _odd_mixer_latent(h, ck, cv, w_qkv, w_out, rpb):
    q, k, v = _odd_project(h, w_qkv)
    return _neighborhood_attention(q, k, v, ck, cv, rpb) @ w_out

def _swiglu(h, w_gu, w_down):
    g, u = jnp.split(h @ w_gu, 2, axis=-1)
    return (jax.nn.silu(g) * u) @ w_down

def _moe(h, w_router, w_gu, w_down):
    logits = jnp.einsum('bld,de->ble', h, w_router, preferred_element_type=jnp.float32)
    top_v, top_i = lax.top_k(logits, TOP_K)
    gates = jax.nn.softmax(top_v, axis=-1)
    comb = jnp.sum(jax.nn.one_hot(top_i, N_EXPERTS, dtype=jnp.float32) * gates[..., None], axis=-2)
    comb = comb.astype(h.dtype)
    out = jnp.zeros_like(h)
    for e in range(N_EXPERTS):
        out = out + comb[..., e:e + 1] * _swiglu(h, w_gu[e], w_down[e])
    return out

def setup_inputs(seed: int = 0) -> dict:
    key = jax.random.key(seed)
    ks = jax.random.split(key, 32)

    def nrm(i, shape, scale):
        return jax.random.normal(ks[i], shape, jnp.float32) * scale

    D = D_MODEL
    base = jnp.asarray(np.log(2.0 ** (5 + np.arange(B_HEADS)) - 1.0), jnp.float32)
    return {
        'x_prompt': nrm(0, (BATCH, SEQ, D), 1.0),
        'x_sample': nrm(1, (DEC_BATCH, DEC_SEQ, D), 1.0),
        'cache_a_k': nrm(2, (DEC_BATCH, N_EVEN, PAST_LEN, A_KV_HEADS, HEAD_DIM), 1.0),
        'cache_a_v': nrm(3, (DEC_BATCH, N_EVEN, PAST_LEN, A_KV_HEADS, HEAD_DIM), 1.0),
        'state_ret_fwd': nrm(4, (DEC_BATCH, N_EVEN, B_HEADS, B_DK, B_DV), 1.0),
        'state_ret_bwd': nrm(5, (DEC_BATCH, N_EVEN, B_HEADS, B_DK, B_DV), 1.0),
        'cache_c_k': nrm(6, (DEC_BATCH, N_ODD, PAST_LEN, C_HEADS, HEAD_DIM), 1.0),
        'cache_c_v': nrm(7, (DEC_BATCH, N_ODD, PAST_LEN, C_HEADS, HEAD_DIM), 1.0),
        'c': nrm(8, (DEC_BATCH, D), 1.0),
        'c_ctx': nrm(9, (D,), 1.0),
        'mod_w': nrm(10, (DEPTH, D, 6 * D), D ** -0.5),
        'mod_b': nrm(11, (DEPTH, 6 * D), 0.02),
        'norm1_g': 1.0 + nrm(12, (DEPTH, D), 0.02),
        'norm2_g': 1.0 + nrm(13, (DEPTH, D), 0.02),
        'final_g': 1.0 + nrm(14, (D,), 0.02),
        'ev_w_in': nrm(15, (N_EVEN, D, IN_EVEN), D ** -0.5),
        'ev_w_out': nrm(16, (N_EVEN, MIX_EVEN, D), MIX_EVEN ** -0.5),
        'ev_sink': nrm(17, (N_EVEN, A_HEADS), 0.5),
        'ev_ret_logit_fwd': base + nrm(18, (N_EVEN, B_HEADS), 0.1),
        'ev_ret_logit_bwd': base + nrm(19, (N_EVEN, B_HEADS), 0.1),
        'ev_ffn_w_gu': nrm(20, (N_EVEN, D, 2 * D_FF), D ** -0.5),
        'ev_ffn_w_down': nrm(21, (N_EVEN, D_FF, D), D_FF ** -0.5),
        'od_w_qkv': nrm(22, (N_ODD, D, 3 * C_W), D ** -0.5),
        'od_w_out': nrm(23, (N_ODD, C_W, D), C_W ** -0.5),
        'od_rpb': nrm(24, (N_ODD, C_HEADS, 2 * NB_ROWS - 1, 2 * NB_COLS - 1), 0.1),
        'od_w_router': nrm(25, (N_ODD, D, N_EXPERTS), D ** -0.5),
        'od_moe_w_gu': nrm(26, (N_ODD, N_EXPERTS, D, 2 * D_FF_EXPERT), D ** -0.5),
        'od_moe_w_down': nrm(27, (N_ODD, N_EXPERTS, D_FF_EXPERT, D), D_FF_EXPERT ** -0.5),
    }

def reference(x_prompt, x_sample, cache_a_k, cache_a_v, state_ret_fwd, state_ret_bwd, cache_c_k, cache_c_v,
              c, c_ctx, mod_w, mod_b, norm1_g, norm2_g, final_g, ev_w_in, ev_w_out, ev_sink,
              ev_ret_logit_fwd, ev_ret_logit_bwd, ev_ffn_w_gu, ev_ffn_w_down, od_w_qkv, od_w_out, od_rpb,
              od_w_router, od_moe_w_gu, od_moe_w_down):
    xp, xs = x_prompt, x_sample
    a_k, a_v, r_f, r_b, c_k, c_v = [], [], [], [], [], []
    for i in range(DEPTH):
        j = i // 2
        mp = _adaln(c_ctx, mod_w[i], mod_b[i])
        ms = _adaln(c, mod_w[i], mod_b[i])
        hp = _modulate(_rmsnorm(xp, norm1_g[i]), mp[0], mp[1])
        hs = _modulate(_rmsnorm(xs, norm1_g[i]), ms[0], ms[1])
        if i % 2 == 0:
            op, ka, va, sf, sb = _even_mixer_context(hp, ev_w_in[j], ev_w_out[j], ev_sink[j],
                                                     ev_ret_logit_fwd[j], ev_ret_logit_bwd[j])
            os_ = _even_mixer_latent(hs, cache_a_k[:, j], cache_a_v[:, j], state_ret_fwd[:, j],
                                     state_ret_bwd[:, j], ev_w_in[j], ev_w_out[j], ev_sink[j],
                                     ev_ret_logit_fwd[j], ev_ret_logit_bwd[j])
            a_k.append(ka)
            a_v.append(va)
            r_f.append(sf)
            r_b.append(sb)
        else:
            op, kc, vc = _odd_mixer_context(hp, od_w_qkv[j], od_w_out[j])
            os_ = _odd_mixer_latent(hs, cache_c_k[:, j], cache_c_v[:, j], od_w_qkv[j], od_w_out[j], od_rpb[j])
            c_k.append(kc)
            c_v.append(vc)
        xp = xp + mp[2] * op
        xs = xs + ms[2] * os_
        hp = _modulate(_rmsnorm(xp, norm2_g[i]), mp[3], mp[4])
        hs = _modulate(_rmsnorm(xs, norm2_g[i]), ms[3], ms[4])
        if i % 2 == 0:
            fp = _swiglu(hp, ev_ffn_w_gu[j], ev_ffn_w_down[j])
            fs = _swiglu(hs, ev_ffn_w_gu[j], ev_ffn_w_down[j])
        else:
            fp = _moe(hp, od_w_router[j], od_moe_w_gu[j], od_moe_w_down[j])
            fs = _moe(hs, od_w_router[j], od_moe_w_gu[j], od_moe_w_down[j])
        xp = xp + mp[5] * fp
        xs = xs + ms[5] * fs
    y_prompt = _rmsnorm(xp, final_g)
    y_sample = _rmsnorm(xs, final_g)
    new_a_k = jnp.stack(a_k, axis=1)
    new_a_v = jnp.stack(a_v, axis=1)
    new_ret_fwd = jnp.stack(r_f, axis=1)
    new_ret_bwd = jnp.stack(r_b, axis=1)
    new_c_k = jnp.stack(c_k, axis=1)
    new_c_v = jnp.stack(c_v, axis=1)
    return (y_prompt, y_sample, new_a_k, new_a_v, new_ret_fwd, new_ret_bwd, new_c_k, new_c_v)


_drawn_inputs = setup_inputs


def setup_inputs(seed=0):
    import zlib

    import numpy as np

    out = dict(_drawn_inputs(seed))
    spreads = {}
    factors = {'final_g': 7.888, 'ev_sink': 8.0, 'od_rpb': 3.055}
    for name, (base, spread) in spreads.items():
        noise = np.random.default_rng([zlib.crc32(name.encode()), seed]).standard_normal(out[name].shape)
        drawn = base * np.exp(spread * noise) if base else spread * noise
        out[name] = jnp.asarray(drawn.astype(out[name].dtype))
    for name, factor in factors.items():
        out[name] = (out[name] * factor).astype(out[name].dtype)
    return out
```

```python
from contextlib import ExitStack

import numpy as np

import concourse.bass as bass
from concourse import mybir

F32 = mybir.dt.float32
F32R = mybir.dt.float32r
I32 = mybir.dt.int32
U32 = mybir.dt.uint32
ALU = mybir.AluOpType
ACT = mybir.ActivationFunctionType
AX = mybir.AxisListType.X

P = 128
D = 1024
KD = D // P
T = 3
DH = 64
GRID_W = 64
A_HEADS, A_KV_HEADS, B_HEADS, C_HEADS = 8, 2, 8, 16
A_Q, A_KV, B_W = A_HEADS * DH, A_KV_HEADS * DH, B_HEADS * DH
NB_ROWS, NB_COLS = 8, 16
C_W = C_HEADS * DH
IN_EVEN = A_Q + 2 * A_KV + 4 * B_W
O_QA, O_KA, O_VA = 0, A_Q, A_Q + A_KV
O_QR = O_VA + A_KV
O_KR, O_VR, O_GR = O_QR + B_W, O_QR + 2 * B_W, O_QR + 3 * B_W
FF = 2816
E = 8
EPS = 1e-6
NEG = -1e30
SCALE = DH ** -0.5

RAW = 6
HL = 3
BLK = 1024
SB = 4
FS = 512
NS = -(-FF // FS)
FF_PH = []
for _s in range(NS):
    for _g in range(2):
        _n = min(FS, FF - _s * FS)
        _j = FF_PH[-1][2] + FF_PH[-1][3] if FF_PH else 0
        FF_PH.append((_s, _g, _j, KD * _n // BLK, _s * FS, _n))
GB = FF_PH[-1][2] + FF_PH[-1][3]
DB = FF // P
EB = GB + DB
MOD_CH, MOD_STEP = 24, 3
B_MOD = 0
B_IN = B_MOD + MOD_CH * SB
IN_FULL = IN_EVEN // 512
B_OUT0 = B_IN + IN_FULL * SB + 2
B_FFN = B_OUT0 + 2 * SB
B_QKV = B_FFN + EB
B_OUT1 = B_QKV + 6 * SB
B_MOE = B_OUT1 + 2 * SB
assert IN_EVEN % 512 == 256 and EB % RAW == 0 and EB % HL == 0 and (MOD_STEP * SB) % RAW == 0
PADW = 127
DR = 7

CONSTS = {}
_at = 0
for _name, _n in (("ident", P), ("ones", P), ("before", P), ("slots", T * P), ("experts", E), ("sel", 4 * P),
                  ("ropec", 2 * DH), ("ropes", 2 * DH), ("mask0", 2 * 3 * P), ("ahead", P), ("behind", P),
                  ("is_ahead", P), ("is_behind", P), ("decay_at", 2 * P), ("kcol", 2), ("cmask", GRID_W)):
    CONSTS[_name] = (_at, _n)
    _at += _n
NCONST = _at


def constants():
    c = np.zeros((P, NCONST), np.float32)

    def put(name, a):
        o, n = CONSTS[name]
        c[:, o:o + n] = np.asarray(a, np.float64).reshape(P, n)

    i = np.arange(P)
    put("ident", np.eye(P))
    put("ones", np.ones((P, P)))
    put("before", i[:, None] < i[None, :])
    put("slots", np.tile(np.arange(T * P), (P, 1)))
    put("experts", np.tile(np.arange(E), (P, 1)))
    sel = np.zeros((4, 32, 4, P))
    for m, rows in enumerate(((0, 2, 4), (1, 3, 4), (0, 2, 4, 5), (1, 3, 4, 5))):
        for r in rows:
            sel[:, r, m] = 1
    put("sel", sel.reshape(P, 4 * P))
    nf = DH // 4
    inv = 10000.0 ** (-np.arange(nf, dtype=np.float32) / np.float32(nf))
    t = np.arange(2 * P)
    ang = np.stack([(t // GRID_W)[:, None] * inv, (t % GRID_W)[:, None] * inv], 1).astype(np.float32)
    cos, sin = np.cos(ang), np.sin(ang)
    put("ropec", np.concatenate([cos, cos], -1).reshape(2, P, DH).transpose(1, 0, 2))
    put("ropes", np.concatenate([-sin, sin], -1).reshape(2, P, DH).transpose(1, 0, 2))
    m0 = np.zeros((P, 2, 3 * P))
    m0[:, 0, 2 * P:] = np.where(i[None, :] + P - i[:, None] <= P, 0, NEG)
    m0[:, 1, P:2 * P] = np.where(i[:, None] + P - i[None, :] <= P, 0, NEG)
    put("mask0", m0)
    d = i[None, :] - i[:, None]
    put("ahead", np.maximum(d, 0))
    put("behind", np.maximum(-d, 0))
    put("is_ahead", d >= 0)
    put("is_behind", d <= 0)
    put("decay_at", np.tile(np.concatenate([i + 1, P - i]), (P, 1)))
    put("kcol", np.stack([P - 1 - i, i], 1))
    cq = i % GRID_W
    ck = np.arange(GRID_W)
    start = np.clip(cq - NB_COLS // 2, 0, GRID_W - NB_COLS)
    ok = (ck[None] >= start[:, None]) & (ck[None] < start[:, None] + NB_COLS)
    put("cmask", np.where(ok, 0, NEG))
    return c


def build(nc, a, outs):
    (x_prompt, x_sample, cache_a_k, cache_a_v, st_f, st_b, cache_c_k, cache_c_v, c_in, c_ctx, mod_w, mod_b,
     norm1_g, norm2_g, final_g, w_in, w_out0, sink, lg_f, lg_b, w_gu, w_down, w_qkv, w_out1, rpb, w_router,
     moe_gu, moe_down, const) = a
    y_prompt, y_sample, new_a_k, new_a_v, new_f, new_b, new_c_k, new_c_v = outs

    mods = nc.dram_tensor("mods_scratch", [4, MOD_CH * 512], F32).ap()
    padded = nc.dram_tensor("rpb_scratch", [C_HEADS * DR, PADW], F32).ap()

    with ExitStack() as ctx:
        def sem(name):
            return ctx.enter_context(nc.semaphore(name))

        top = [0]

        def sb(name, shape, dt=F32, at=None):
            n = 4 * int(np.prod(shape[1:]))
            n = (n + 31) // 32 * 32
            o = top[0] if at is None else at
            h = nc.alloc_sbuf_tensor_at(name, shape, dt, offset=o)
            if at is None:
                top[0] = o + n
            return h

        first = ctx.enter_context(nc.sbuf_tensor("first", [P, 8], F32))
        top[0] = (nc.sbuf_base + 63) // 32 * 32
        x = sb("x", [P, T, D])
        keep = sb("keep", [P, CONSTS["ropec"][0]])
        rawb = sb("rawb", [P, RAW, BLK])
        whi = sb("whi", [P, HL, BLK], F32R)
        wlo = sb("wlo", [P, HL, BLK], F32R)
        hT_hi = sb("hT_hi", [P, KD, T * P], F32R)
        hT_lo = sb("hT_lo", [P, KD, T * P], F32R)
        mrow = sb("mrow", [P, D])
        gate = sb("gate", [P, 2, D])
        gbc = sb("gbc", [P, D])
        st = sb("st", [P, 64])
        comb = sb("comb", [P, T, E])
        posm = sb("posm", [P, T, E])
        counts = sb("counts", [1, E], I32)
        region = top[0]
        top[0] = region
        h = sb("h", [P, T, D])
        act_at = top[0]
        acc = sb("acc", [P, T, D])
        fT_hi = sb("fT_hi", [P, DB, T * P], F32R)
        fT_lo = sb("fT_lo", [P, DB, T * P], F32R)
        sg = sb("sg", [P, T, FS])
        oh = sb("oh", [P, T, T * P])
        ohT = sb("ohT", [P, T * P], F32R)
        ff_top = top[0]
        top[0] = act_at + 12 * 1024
        wr = sb("wr", [P, KD, E])
        wr_hi = sb("wr_hi", [P, KD, E], F32R)
        wr_lo = sb("wr_lo", [P, KD, E], F32R)
        logits = sb("logits", [P, T, E])
        best = sb("best", [P, T, 8])
        best_i = sb("best_i", [P, T, 8], U32)
        best_f = sb("best_f", [P, T, 8])
        m1 = sb("m1", [P, T, E])
        m2 = sb("m2", [P, T, E])
        msk = sb("msk", [P, T, E])
        rt = sb("rt", [P, 8, T])
        top[0] = act_at
        crow = sb("crow", [16, P])
        ccol = sb("ccol", [P, 16])
        cs4 = sb("cs4", [P, KD, P], F32R)
        mst = sb("mst", [4, MOD_STEP, 512])
        padrow = sb("padrow", [C_HEADS * DR, PADW])
        top[0] = region
        s_sc = sb("s_sc", [P, 2, 3 * P])
        s_p = sb("s_p", [P, 2, 3 * P])
        s_pT = sb("s_pT", [P, 2, 3 * P])
        a_neg = sb("a_neg", [P, 2, 2])
        a_sum = sb("a_sum", [P, 2, 2])
        a_es = sb("a_es", [P, 2, 2])
        a_rec = sb("a_rec", [P, 2, 2])
        assert top[0] <= act_at
        top[0] = act_at
        kT = sb("kT", [P, 2, 4 * P])
        qT = sb("qT", [P, 2, T * P])
        shared = top[0]
        proj0 = sb("proj0", [P, T, IN_EVEN])
        more = sb("more", [P, NCONST - CONSTS["ropec"][0]])
        ck0 = sb("ck0", [P, A_KV])
        cv0 = sb("cv0", [P, A_KV])
        kdup = sb("kdup", [P, 4, 2 * A_KV])
        sinks = sb("sinks", [P, 2, A_HEADS])
        lg = sb("lg", [P, 3, 8])
        lgt = sb("lgt", [P, 3, 8])
        logd = sb("logd", [P, 3, 8])
        dm = sb("dm", [P, B_HEADS, P])
        dq = sb("dq", [P, 2, 4, P])
        kdec = sb("kdec", [P, 2, 8])
        cdec = sb("cdec", [P, 2, 4])
        S0 = sb("S0", [P, 2, 4, DH])
        SS = sb("SS", [P, 2, 4, DH])
        up = sb("up", [P, 2, 4, DH])
        gst = sb("gst", [P, 4, T, 8])
        kd_at = top[0]
        kd = sb("kd", [P, 4, B_W])
        rqT = sb("rqT", [P, 2, T * P])
        rkT = sb("rkT", [P, 2, T * P])
        rqd = sb("rqd", [P, 2, 2, 2 * P])
        rat = sb("rat", [P, 2, T * P])
        top0 = top[0]
        rot = sb("rot", [P, 2, 640], at=kd_at)
        dm2 = sb("dm2", [P, B_HEADS, P], at=kd_at + 8 * 1024)
        gn = sb("gn", [P, T, B_W], at=kd_at)
        gn2 = sb("gn2", [P, T, B_W], at=kd_at + 4 * T * B_W)
        tmp_w = sb("tmp_w", [P, T, D], at=region)
        top[0] = shared
        proj1 = sb("proj1", [P, T, 3 * C_W])
        ck1 = sb("ck1", [P, C_W])
        cv1 = sb("cv1", [P, C_W])
        bm = sb("bm", [P, 2, 2, 2, 3 * P])
        bmr = sb("bmr", [P, 2, 4, 4, GRID_W])
        cm = sb("cm", [P, GRID_W])
        assert max(ff_top, top0, top[0]) <= nc.sbuf_usable_end, (ff_top, top0, top[0], nc.sbuf_usable_end)

        ps = ctx.enter_context(nc.psum_tensor("ps", [P, 8, 512], F32))

        def cst(name):
            o, n = CONSTS[name]
            base = CONSTS["ropec"][0]
            return keep[:, o:o + n] if o < base else more[:, o - base:o - base + n]

        ident = cst("ident")

        w_loaded = [sem(f"w_loaded{i}") for i in range(RAW)]
        hi_done = sem("hi_done")
        lo_done = sem("lo_done")
        pe_used = sem("pe_used")
        x_in = sem("x_in")
        keep_in = sem("keep_in")
        more_in = sem("more_in")
        crow_in = sem("crow_in")
        g_in = sem("g_in")
        m_in = sem("m_in")
        ones_in = sem("ones_in")
        cc_t = sem("cc_t")
        cc_silu = sem("cc_silu")
        cs_zero = sem("cs_zero")
        cs_hi = sem("cs_hi")
        cs_lo = sem("cs_lo")
        mod_ev = sem("mod_ev")
        mst_free = sem("mst_free")
        mod_out = sem("mod_out")
        nsq = sem("nsq")
        nms = sem("nms")
        nsd = sem("nsd")
        nrs = sem("nrs")
        bc_ps = sem("bc_ps")
        h_rows = sem("h_rows")
        gate_ps = sem("gate_ps")
        gate_ev = sem("gate_ev")
        tin_ps = sem("tin_ps")
        tin_hi = sem("tin_hi")
        tin_lo = sem("tin_lo")
        gm_ev = sem("gm_ev")
        res_t = sem("res_t")
        x_upd = sem("x_upd")
        dch = sem("dch")
        ach = sem("ach")
        rope_done = sem("rope_done")
        at_trk = sem("at_trk")
        at_trq = sem("at_trq")
        at_kT = sem("at_kT")
        at_qT = sem("at_qT")
        at_s = sem("at_s")
        at_sc = sem("at_sc")
        at_m = sem("at_m")
        at_e = sem("at_e")
        at_pt = sem("at_pt")
        at_ptev = sem("at_ptev")
        at_o = sem("at_o")
        at_es = sem("at_es")
        at_zs = sem("at_zs")
        at_done = sem("at_done")
        kv_in = sem("kv_in")
        lg_in = sem("lg_in")
        s0_in = sem("s0_in")
        tb_a = sem("tb_a")
        tb_v = sem("tb_v")
        kd_v = sem("kd_v")
        kdup_v = sem("kdup_v")
        u_ps = sem("u_ps")
        up_ev = sem("up_ev")
        ss_v = sem("ss_v")
        r_tr = sem("r_tr")
        r_q = sem("r_q")
        r_qd = sem("r_qd")
        r_at_ps = sem("r_at_ps")
        r_at_v = sem("r_at_v")
        r_o = sem("r_o")
        gn_v = sem("gn_v")
        gn_a = sem("gn_a")
        mix_done = sem("mix_done")
        pad_z = sem("pad_z")
        pad_in = sem("pad_in")
        pad_out = sem("pad_out")
        cm_in = sem("cm_in")
        bm_z = sem("bm_z")
        bm_in = [sem("bm_in0"), sem("bm_in1")]
        bm_ok = sem("bm_ok")
        c1_in = sem("c1_in")
        sg_a = sem("sg_a")
        gu_v = sem("gu_v")
        ft_ps = sem("ft_ps")
        ft_hi = sem("ft_hi")
        ft_lo = sem("ft_lo")
        y_hi = sem("y_hi")
        y_lo = sem("y_lo")
        wr_in = sem("wr_in")
        wr_v = sem("wr_v")
        lo_ps = sem("lo_ps")
        rt_v = sem("rt_v")
        rt_a = sem("rt_a")
        pos_ps = sem("pos_ps")
        routed = sem("routed")
        acc_z = sem("acc_z")
        oh_v = sem("oh_v")
        ga_ps = sem("ga_ps")
        ga_hi = sem("ga_hi")
        ga_lo = sem("ga_lo")
        oht_ps = sem("oht_ps")
        oht_ev = sem("oht_ev")
        sc_ps = sem("sc_ps")
        sc_v = sem("sc_v")
        stored = sem("stored")
        stored_sp = sem("stored_sp")

        def slot_h(b):
            return (b if b < B_MOE else b - B_MOE) % HL

        def slot_r(b):
            return (b if b < B_MOE else b - B_MOE) % RAW

        def conv_hi(act, b, n=None, loads=None):
            s, r = slot_r(b), slot_h(b)
            act.wait_ge(w_loaded[s], 16 * (b // RAW + 1) if loads is None else loads)
            act.wait_ge(pe_used, (b if n is None else n) + 1)
            nc.scalar.activation(whi[:, r, :], rawb[:, s, :], ACT.Copy).then_inc(hi_done, 1)

        def conv_lo(dve, b, n=None, loads=None):
            s, r = slot_r(b), slot_h(b)
            dve.wait_ge(hi_done, (b if n is None else n) + 1)
            nc.vector.tensor_tensor(wlo[:, r, :], rawb[:, s, :], whi[:, r, :].bitcast(F32),
                                    ALU.subtract).then_inc(lo_done, 1)

        class Ahead:

            def __init__(self, eng, conv, start):
                self.eng, self.conv, self.b = eng, conv, start

            def to(self, end):
                while self.b < end:
                    self.conv(self.eng, self.b)
                    self.b += 1

        class Chain:

            def __init__(self, eng, s):
                self.eng, self.s, self.n = eng, s, 0

            def __call__(self, ins):
                self.n += 1
                ins.then_inc(self.s, 1)
                self.eng.wait_ge(self.s, self.n)

        def mm3(out, l_hi, l_lo, r_hi, r_lo, start, stop):
            nc.tensor.matmul(out, l_hi, r_hi, start=start, stop=False)
            nc.tensor.matmul(out, l_hi, r_lo, start=False, stop=False)
            return nc.tensor.matmul(out, l_lo, r_hi, start=False, stop=stop)

        def wblk(buf, b, cols):
            return buf[:, slot_h(b), :].rearrange("p (k n) -> p k n", n=cols)

        def tiles_of(ap):
            return ap.rearrange("(t p) d -> p t d", p=P)

        def kn(w):
            return w.rearrange("(k p) n -> p k n", p=P)

        def chunks(b0, ncols):
            out = []
            b = b0
            for o in range(0, ncols, 512):
                n = min(512, ncols - o)
                k = KD * n // BLK
                out.append((b, k, o, n))
                b += k
            return out

        IN_CH = chunks(B_IN, IN_EVEN)
        QKV_CH = chunks(B_QKV, 3 * C_W)
        OUT_CH = [chunks(B_OUT0, D), chunks(B_OUT1, D)]
        BEFORE = [sum(b % RAW == s for b in range(B_MOE)) for s in range(RAW)]

        def y_of(buf):
            return buf[:, :, :].rearrange("p a n -> p (a n)")[:, 0:D]

        GM_DONE = [0, T * len(IN_CH)]

        block = ctx.enter_context(nc.Block())

        @block.sync
        def _(sp):
            def load(b, src, n=None):
                sp.wait_ge(lo_done, (b if n is None else n) + 1)
                view = rawb[:, slot_r(b), :]
                if len(src.shape) == 3:
                    view = view.rearrange("p (k n) -> p k n", n=src.shape[2])
                sp.dma_start(view, src).then_inc(w_loaded[slot_r(b)], 16)

            def load_chunks(ch, w):
                for b, k, o, n in ch:
                    rows = BLK // n
                    for i in range(k):
                        load(b + i, kn(w)[:, i * rows:(i + 1) * rows, o:o + n])

            def load_ff(b0, gu, down, n0=None):
                guv = kn(gu)
                for s, g, j, k, o, n in FF_PH:
                    rows = BLK // n
                    for i in range(k):
                        load(b0 + j + i, guv[:, i * rows:(i + 1) * rows, g * FF + o:g * FF + o + n],
                             None if n0 is None else n0 + (j + i))
                for j in range(DB):
                    load(b0 + GB + j, down[j * P:(j + 1) * P, :], None if n0 is None else n0 + (GB + j))

            mw = mod_w.rearrange("l (k p) n -> p k l n", p=P)
            with sp.Fori(0, MOD_CH // MOD_STEP) as it:
                for c in range(MOD_STEP):
                    for i in range(SB):
                        j = c * SB + i
                        lay = it // (MOD_CH // MOD_STEP // 2)
                        col = (it % (MOD_CH // MOD_STEP // 2)) * (MOD_STEP * 512) + c * 512
                        sp.wait_ge(lo_done, it * (MOD_STEP * SB) + (j + 1))
                        sp.dma_start(rawb[:, j % RAW, :].rearrange("p (k n) -> p k n", n=512),
                                     mw[:, 2 * i:2 * i + 2, bass.ds(lay, 1), bass.ds(col, 512)]
                                     .rearrange("p k l n -> p k (l n)")).then_inc(w_loaded[j % RAW], 16)
            load_chunks(IN_CH, w_in[0])
            load_chunks(OUT_CH[0], w_out0[0])
            load_ff(B_FFN, w_gu[0], w_down[0])
            load_chunks(QKV_CH, w_qkv[0])
            load_chunks(OUT_CH[1], w_out1[0])
            sp.wait_ge(lo_done, B_MOE + RAW)
            with sp.Fori(0, E) as e:
                load_ff(B_MOE, moe_gu[0, bass.ds(e, 1)].rearrange("e d n -> (e d) n"),
                        moe_down[0, bass.ds(e, 1)].rearrange("e d n -> (e d) n"), n0=e * EB + B_MOE)


        @block.gpsimd
        def _(pool):
            pool.dma_start(crow[0:8, :], c_ctx.rearrange("(k p) -> k p", p=P)).then_inc(crow_in, 16)
            pool.dma_start(crow[8:16, :], c_in[0].rearrange("(k p) -> k p", p=P)).then_inc(crow_in, 16)
            nkeep = CONSTS["ropec"][0]
            pool.dma_start(keep[:, :], const[:, 0:nkeep]).then_inc(keep_in, 16)
            nc.gpsimd.memset(padrow[:, :], 0.0).then_inc(pad_z, 1)
            pool.dma_start(x[:, 0, :], x_prompt[0]).then_inc(x_in, 16)
            pool.dma_start(x[:, 1:3, :], tiles_of(x_sample[0])).then_inc(x_in, 16)
            o1 = CONSTS["ones"][0]
            for q in range(3):
                pool.dma_start(mrow[32 * q + 5:32 * q + 6, :].rearrange("p (a b) -> p a b", b=P),
                               const[0:8, o1:o1 + P].unsqueeze(0)).then_inc(ones_in, 16)
            pool.dma_start(more[:, :], const[:, nkeep:NCONST]).then_inc(more_in, 16)
            pool.dma_start(ck0[:, :], cache_a_k[0, 0].rearrange("t h d -> t (h d)")).then_inc(kv_in, 16)
            pool.dma_start(cv0[:, :], cache_a_v[0, 0].rearrange("t h d -> t (h d)")).then_inc(kv_in, 16)
            pool.dma_start(sinks[:, 0, :], sink[0].partition_broadcast(P)).then_inc(kv_in, 16)
            for d, src in enumerate((lg_f, lg_b)):
                pool.dma_start(lg[:, 1 + d, :], src[0].partition_broadcast(P)).then_inc(lg_in, 16)
                for u in range(2):
                    pool.dma_start(lg[DH * u:DH * (u + 1), 0, 4 * d:4 * d + 4],
                                   src[0].rearrange("(i u) -> u i", u=2)[u].partition_broadcast(DH),
                                   allow_slow_non_contiguous=True).then_inc(lg_in, 16)
            for d, src in enumerate((st_f, st_b)):
                for u in range(2):
                    pool.dma_start(S0[DH * u:DH * (u + 1), d, :, :],
                                   src[0, 0].rearrange("(i u) k v -> u k i v", u=2)[u]).then_inc(s0_in, 16)
            pool.wait_ge(pad_z, 1)
            pool.dma_start(padded, padrow[:, :]).then_inc(pad_out, 16)
            pool.wait_ge(pad_out, 16)
            pool.dma_start(padded.rearrange("(h r) c -> h r c", r=DR)[:, :, 48:48 + 2 * NB_COLS - 1],
                           rpb[0][:, NB_ROWS - 4:NB_ROWS + 3, :]).then_inc(pad_in, 16)

            with pool.Fori(0, MOD_CH // MOD_STEP) as it:
                pool.wait_ge(mod_ev, it * MOD_STEP + 2 * MOD_STEP)
                pool.dma_start(mods[:, bass.ds(it * (MOD_STEP * 512), MOD_STEP * 512)],
                               mst[:, :, :].rearrange("p a b -> p (a b)")).then_inc(mod_out, 16)
                pool.wait_ge(mod_out, it * 16 + 16)
                pool.sem_inc(mst_free, 1)

            def norm_rows(n):
                lay, half = n // 2, n % 2
                if n:
                    pool.wait_ge(gate_ps, n)
                    pool.wait_ge(h_rows, T * n)
                else:
                    pool.wait_ge(mod_out, 16 * (MOD_CH // MOD_STEP))
                g = (norm1_g, norm2_g)[half]
                pool.dma_start(gbc[:, :], g[lay].partition_broadcast(P)).then_inc(g_in, 16)
                for q in range(3):
                    c0 = (3 * half + q) * D
                    pool.dma_start(mrow[32 * q:32 * q + 4, :], mods[:, lay * 6 * D + c0:lay * 6 * D + c0 + D])\
                        .then_inc(m_in, 16)
                    pool.dma_start(mrow[32 * q + 4:32 * q + 5, :], mod_b[lay:lay + 1, c0:c0 + D]).then_inc(m_in, 16)

            norm_rows(0)
            norm_rows(1)
            pool.wait_ge(gm_ev, GM_DONE[1])
            pool.dma_start(new_a_k[0, 0].rearrange("t h d -> t (h d)"), proj0[:, 0, O_KA:O_KA + A_KV]).then_inc(stored, 16)
            pool.dma_start(new_a_v[0, 0].rearrange("t h d -> t (h d)"), proj0[:, 0, O_VA:O_VA + A_KV]).then_inc(stored, 16)
            pool.wait_ge(up_ev, 2)
            for d, dst in enumerate((new_f, new_b)):
                for u in range(2):
                    pool.dma_start(dst[0, 0].rearrange("(i u) k v -> u k i v", u=2)[u],
                                   up[DH * u:DH * (u + 1), d, :, :]).then_inc(stored, 16)
            norm_rows(2)
            pool.wait_ge(x_upd, 12)
            pool.dma_start(ck1[:, :], cache_c_k[0, 0].rearrange("t h d -> t (h d)")).then_inc(c1_in, 16)
            pool.dma_start(cv1[:, :], cache_c_v[0, 0].rearrange("t h d -> t (h d)")).then_inc(c1_in, 16)
            oc = CONSTS["cmask"][0]
            pool.dma_start(cm[:, :], const[:, oc:oc + GRID_W]).then_inc(cm_in, 16)
            for r in range(2):
                nc.gpsimd.memset(bm[:, r, :, :, 0:P], 0.0).then_inc(bm_z, 1)
            pool.wait_ge(pad_in, 16)
            pool.wait_ge(cm_in, 16)

            def bias_load(i):
                if i >= 2:
                    pool.wait_ge(bm_ok, i - 1)
                for qt in range(2):
                    for rq in range(2):
                        for u in range(2):
                            row = (2 * i + u) * DR + 3 - (2 * qt + rq)
                            src = bass.AP(padded.tensor, row * PADW, [[1, GRID_W], [PADW, 4], [1, GRID_W]])
                            pool.dma_start(bmr[GRID_W * rq:GRID_W * (rq + 1), i % 2, 2 * qt + u, :, :], src)\
                                .then_inc(bm_in[i % 2], 16)

            bias_load(0)
            for i in range(8):
                if i < 7:
                    bias_load(i + 1)
                pool.wait_ge(bm_in[i % 2], 128 * (i // 2 + 1))
                if i >= 2:
                    pool.wait_ge(at_sc, 24 + 6 * (i - 1))
                v = bm[:, i % 2, :, :, P:].rearrange("p a b (k c) -> p (a b) k c", c=GRID_W)
                m = cm[:, :].unsqueeze(1).unsqueeze(1).to_broadcast([P, 4, 4, GRID_W])
                nc.gpsimd.tensor_tensor(v, bmr[:, i % 2, :, :, ::-1], m, ALU.add).then_inc(bm_ok, 1)
            pool.dma_start(new_c_k[0, 0].rearrange("t h d -> t (h d)"), proj1[:, 0, C_W:2 * C_W]).then_inc(stored, 16)
            pool.dma_start(new_c_v[0, 0].rearrange("t h d -> t (h d)"), proj1[:, 0, 2 * C_W:]).then_inc(stored, 16)
            norm_rows(3)
            pool.wait_ge(stored, 16 * 8)
            pool.wait_ge(x_upd, 18)
            pool.dma_start(wr[:, :, :], kn(w_router[0]), allow_slow_non_contiguous=True).then_inc(wr_in, 16)
            nc.gpsimd.memset(acc[:, :, :], 0.0).then_inc(acc_z, 1)
            pool.wait_ge(h_rows, 12)
            pool.dma_start(gbc[:, :], final_g.partition_broadcast(P)).then_inc(g_in, 16)
            for t in range(T):
                pool.wait_ge(h_rows, 13 + t)
                dst = y_prompt[0] if t == 0 else y_sample[0, (t - 1) * P:t * P, :]
                pool.dma_start(dst, h[:, t, :]).then_inc(stored, 16)
            pool.wait_ge(stored, 16 * 11)

        @block.tensor
        def _(pe):
            def norm_bc(n):
                pe.wait_ge(m_in, 96 * (n + 1))
                if n:
                    pe.wait_ge(x_upd, 6 * n)
                for kind in range(2):
                    for part, m in ((1, 2 + kind), (0, kind)):
                        for half in range(2):
                            q = 32 * part
                            mm = nc.tensor.matmul(ps[:, 4 * kind + 2 * (1 - part) + half, :],
                                                  cst("sel")[q:q + 6, m * P:(m + 1) * P],
                                                  mrow[q:q + 6, 512 * half:512 * (half + 1)], start=True, stop=True)
                    mm.then_inc(bc_ps, 1)

            def norm_gate(n):
                for kind in range(2):
                    for half in range(2):
                        mm = nc.tensor.matmul(ps[:, 4 + 2 * kind + half, :], cst("sel")[64:70, kind * P:(kind + 1) * P],
                                              mrow[64:70, 512 * half:512 * (half + 1)], start=True, stop=True)
                mm.then_inc(gate_ps, 1)

            def turn_in(n, src, ready):
                for t in range(T):
                    ready(t)
                    if t == 2:
                        pe.wait_ge(tin_lo, 6 * n + 2)
                    for kh in range(2):
                        for k in range(4):
                            mm = nc.tensor.transpose(ps[:, (2 * t) % 4 + kh, k * P:(k + 1) * P],
                                                     src(t, 4 * kh + k), ident)
                        mm.then_inc(tin_ps, 1)

            def norm(n, turn):
                norm_bc(n)
                turn_in(turn, lambda t, k: h[:, t, k * P:(k + 1) * P], lambda t: pe.wait_ge(h_rows, T * n + t + 1))
                norm_gate(n)
                pe.wait_ge(tin_lo, 6 * (turn + 1))
                pe.wait_ge(gate_ev, n + 1)

            def dense(ch, base):
                for c, (b, nb, o, n) in enumerate(ch):
                    rows = BLK // n
                    for i in range(nb):
                        pe.wait_ge(lo_done, b + i + 1 + RAW)
                        for kk in range(rows):
                            k = i * rows + kk
                            for t in range(T):
                                idx = T * c + t
                                if k == 0 and idx >= 6 and base is not None:
                                    pe.wait_ge(gm_ev, base + idx - 5)
                                mm = mm3(ps[:, idx % 6, 0:n], hT_hi[:, k, t * P:(t + 1) * P],
                                         hT_lo[:, k, t * P:(t + 1) * P], wblk(whi, b + i, n)[:, kk, :],
                                         wblk(wlo, b + i, n)[:, kk, :], k == 0, k == KD - 1)
                        mm.then_inc(pe_used, 1)

            def attention(lay):
                npair, u0, p0, m0 = (4, 0, 0, 0) if lay == 0 else (8, 24, 4, 12)
                proj = proj0 if lay == 0 else proj1

                def prep(i):
                    if lay == 1 or i % 2 == 0:
                        ki = i // 2 if lay == 0 else 2 + i
                        if ki:
                            pe.wait_ge(at_kT, ki)
                        for c in range(4):
                            if lay == 0:
                                src = kdup[:, c, P * ki:P * (ki + 1)]
                            else:
                                src = (ck1[:, P * i:P * (i + 1)], proj[:, 1, C_W + P * i:C_W + P * (i + 1)],
                                       proj[:, 2, C_W + P * i:C_W + P * (i + 1)],
                                       proj[:, 0, C_W + P * i:C_W + P * (i + 1)])[c]
                            mm = nc.tensor.transpose(ps[:, 4, c * P:(c + 1) * P], src, ident)
                        mm.then_inc(at_trk, 1)
                    if p0 + i:
                        pe.wait_ge(at_qT, p0 + i)
                    for t in range(T):
                        mm = nc.tensor.transpose(ps[:, 5, t * P:(t + 1) * P], proj[:, t, P * i:P * (i + 1)], ident)
                    mm.then_inc(at_trq, 1)

                def unit(n):
                    return n // 6, n % 6 // 2, n % 2

                def scores(n):
                    i, t, u = unit(n)
                    g = u0 + n
                    if n % 6 == 0:
                        pe.wait_ge(at_qT, p0 + i + 1)
                        pe.wait_ge(at_kT, i // 2 + 1 if lay == 0 else 2 + i + 1)
                    if g >= 2:
                        pe.wait_ge(at_sc, g - 1)
                    sl = (i // 2) % 2 if lay == 0 else i % 2
                    r = slice(DH * u, DH * (u + 1))
                    lo, hi = (3 * P, 4 * P) if t == 0 else (0, 3 * P)
                    nc.tensor.matmul(ps[:, g % 2, 0:hi - lo], qT[r, i % 2, t * P:(t + 1) * P], kT[r, sl, lo:hi],
                                     start=True, stop=True).then_inc(at_s, 1)

                def turn_p(n):
                    g = u0 + n
                    nk = 1 if unit(n)[1] == 0 else 3
                    pe.wait_ge(at_e, g + 1)
                    if g >= 2:
                        pe.wait_ge(at_ptev, g - 1)
                    for c in range(nk):
                        mm = nc.tensor.transpose(ps[:, 2 + g % 2, c * P:(c + 1) * P],
                                                 s_p[:, g % 2, c * P:(c + 1) * P], ident)
                    mm.then_inc(at_pt, 1)

                def values(n):
                    i, t, u = unit(n)
                    g, m = u0 + n, m0 + 3 * i + t
                    head = 2 * i + u
                    pe.wait_ge(at_ptev, g + 1)
                    if u == 0 and m >= 2:
                        pe.wait_ge(at_done, m - 1)
                    if lay == 0:
                        o = DH * (head // 4)
                        vs = [proj[:, 0, O_VA + o:O_VA + o + DH]] if t == 0 else \
                             [cv0[:, o:o + DH]] + [proj[:, c, O_VA + o:O_VA + o + DH] for c in (1, 2)]
                    else:
                        o = DH * head
                        vs = [proj[:, 0, 2 * C_W + o:2 * C_W + o + DH]] if t == 0 else \
                             [cv1[:, o:o + DH]] + [proj[:, c, 2 * C_W + o:2 * C_W + o + DH] for c in (1, 2)]
                    for c, v in enumerate(vs):
                        mm = nc.tensor.matmul(ps[:, 6 + m % 2, DH * u:DH * (u + 1)], s_pT[:, g % 2, c * P:(c + 1) * P],
                                              v, start=(c == 0), stop=(c == len(vs) - 1))
                    if u == 1:
                        mm.then_inc(at_o, 1)

                N = 6 * npair
                prep(0)
                for n in range(N + 2):
                    if n < N:
                        scores(n)
                    if 1 <= n <= N:
                        turn_p(n - 1)
                    if n >= 2:
                        values(n - 2)
                    if n % 6 == 3 and n // 6 + 1 < npair:
                        prep(n // 6 + 1)

            def retention():
                pe.wait_ge(at_done, 12)
                pe.wait_ge(kd_v, 4)
                for z, t in enumerate((0, 1, 0, 2)):
                    for head in range(8):
                        i, u = head // 2, head % 2
                        mm = nc.tensor.matmul(ps[DH * u:DH * (u + 1), z, i * DH:(i + 1) * DH],
                                              kd[:, z, head * DH:(head + 1) * DH],
                                              proj0[:, t, O_VR + head * DH:O_VR + (head + 1) * DH], start=True, stop=True)
                    mm.then_inc(u_ps, 1)

                def turn(i):
                    if i:
                        pe.wait_ge(r_q, 2 * i)
                        pe.wait_ge(r_qd, i)
                    for o, bank in ((O_QR, 0), (O_KR, 1)):
                        for t in range(T):
                            mm = nc.tensor.transpose(ps[:, bank, t * P:(t + 1) * P],
                                                     proj0[:, t, o + P * i:o + P * (i + 1)], ident)
                    mm.then_inc(r_tr, 1)

                def att(j):
                    i, u = j // 2, j % 2
                    r = slice(DH * u, DH * (u + 1))
                    if u == 0:
                        pe.wait_ge(r_q, 2 * (i + 1))
                    if j >= 2:
                        pe.wait_ge(r_at_v, j - 1)
                    for t in range(T):
                        mm = nc.tensor.matmul(ps[:, 2 + j % 2, t * P:(t + 1) * P], rkT[r, i % 2, t * P:(t + 1) * P],
                                              rqT[r, i % 2, t * P:(t + 1) * P], start=True, stop=True)
                    mm.then_inc(r_at_ps, 1)

                def out(j):
                    i, u = j // 2, j % 2
                    r = slice(DH * u, DH * (u + 1))
                    pe.wait_ge(r_at_v, j + 1)
                    if u == 0:
                        pe.wait_ge(r_qd, i + 1)
                    for t in range(T):
                        o = ps[:, 5 + t, DH * j:DH * (j + 1)]
                        mm = nc.tensor.matmul(o, rat[:, j % 2, t * P:(t + 1) * P],
                                              proj0[:, t, O_VR + DH * j:O_VR + DH * (j + 1)], start=True, stop=(t == 0))
                        if t:
                            sf, sb_ = (S0, SS) if t == 1 else (SS, S0)
                            c = (t - 1) * P
                            if t == 1 and j:
                                pe.wait_ge(r_o, j)
                            nc.tensor.matmul(o, rqd[r, i % 2, 0, c:c + P], sf[r, 0, i, :], start=False, stop=False)
                            mm = nc.tensor.matmul(o, rqd[r, i % 2, 1, c:c + P], sb_[r, 1, i, :], start=False, stop=True)
                    mm.then_inc(r_o, 1)

                pe.wait_ge(up_ev, 2)
                pe.wait_ge(ss_v, 2)
                turn(0)
                for j in range(9):
                    if j < 8:
                        att(j)
                        if j % 2 == 1 and j < 7:
                            turn(j // 2 + 1)
                    if j >= 1:
                        out(j - 1)

            def feed(nt, b0, n0, u):
                def at(per, v):
                    return v if u is None else u * per + v

                def inc(t, per=1):
                    return per if t < nt - 1 else per * (T - nt + 1)

                def blk(j):
                    return b0 + j + 1 + RAW if n0 is None else n0 + (j + 1 + RAW)

                def turn(s, n):
                    for t in range(nt):
                        q = s * nt + t
                        pe.wait_ge(gu_v, at(3 * NS, 3 * s + t + 1))
                        if q >= 2:
                            ls, lt = divmod(q - 2, nt)
                            pe.wait_ge(ft_lo, at(3 * NS, 3 * ls + lt + 1))
                        for c in range(n // P):
                            mm = nc.tensor.transpose(ps[:, 6 + q % 2, c * P:(c + 1) * P], sg[:, t, c * P:(c + 1) * P], ident)
                        mm.then_inc(ft_ps, inc(t))

                for p, (s, g, j, nb, o, n) in enumerate(FF_PH):
                    rows = BLK // n
                    for i in range(nb):
                        pe.wait_ge(lo_done, blk(j + i))
                        for kk in range(rows):
                            k = i * rows + kk
                            for t in range(nt):
                                if k == 0 and s:
                                    pe.wait_ge(gu_v if g else sg_a, at(3 * NS, 3 * (s - 1) + t + 1))
                                mm = mm3(ps[:, 3 * g + t, 0:n], hT_hi[:, k, t * P:(t + 1) * P],
                                         hT_lo[:, k, t * P:(t + 1) * P], wblk(whi, b0 + j + i, n)[:, kk, :],
                                         wblk(wlo, b0 + j + i, n)[:, kk, :], k == 0, k == KD - 1)
                        mm.then_inc(pe_used, 1)
                    if g == 0 and s:
                        turn(s - 1, FS)
                turn(NS - 1, FF_PH[-1][5])
                for j in range(DB):
                    pe.wait_ge(lo_done, blk(GB + j))
                    w_hi, w_lo = (wblk(w, b0 + GB + j, 512) for w in (whi, wlo))
                    for t in range(nt):
                        if j % 4 == 0:
                            pe.wait_ge(ft_lo, at(3 * NS, 3 * (j // 4) + t + 1))
                        for half in range(2):
                            mm = mm3(ps[:, 2 * t + half, :], fT_hi[:, j, t * P:(t + 1) * P],
                                     fT_lo[:, j, t * P:(t + 1) * P], w_hi[:, half, :], w_lo[:, half, :],
                                     j == 0, j == DB - 1)
                    mm.then_inc(pe_used, 1)

            def expert(nt, e):
                pe.wait_ge(sc_v, e * 18 + 1)
                pe.wait_ge(oh_v, e + 1)
                for k in range(KD):
                    for m in range(T):
                        mm = nc.tensor.matmul(ps[:, k, 0:nt * P], h[:, m, k * P:(k + 1) * P], oh[:, m, 0:nt * P],
                                              start=(m == 0), stop=(m == T - 1))
                    mm.then_inc(ga_ps, 1)
                pe.wait_ge(ga_lo, e * KD + KD)
                feed(nt, B_MOE, e * EB + B_MOE, e + 1)
                banks = [b for b in range(2 * nt, 8) if b != 6]
                for t in range(nt):
                    if t == 0:
                        pe.wait_ge(ft_lo, (e + 1) * (3 * NS) + 3 * NS)
                    for m in range(T):
                        mm = nc.tensor.transpose(ps[:, 6, m * P:(m + 1) * P], oh[:, m, t * P:(t + 1) * P], ident)
                    mm.then_inc(oht_ps, 1 if t < nt - 1 else T - nt + 1)
                    pe.wait_ge(oht_ev, e * 3 + t + 1)
                    pe.wait_ge(y_lo, e * 3 + t + 1)
                    for m in range(T):
                        for half in range(2):
                            i = 6 * t + 2 * m + half
                            if i >= len(banks):
                                pe.wait_ge(sc_v, e * 18 + (i - len(banks) + 2))
                            o = ps[:, banks[i % len(banks)], :]
                            yc = slice(512 * half, 512 * (half + 1))
                            nc.tensor.matmul(o, ohT[:, m * P:(m + 1) * P], y_of(fT_hi)[:, yc], start=True, stop=False)
                            nc.tensor.matmul(o, ohT[:, m * P:(m + 1) * P], y_of(fT_lo)[:, yc], start=False, stop=True)\
                                .then_inc(sc_ps, 1 if i < 6 * nt - 1 else 6 * (T - nt) + 1)

            pe.wait_ge(crow_in, 32)
            pe.wait_ge(keep_in, 16)
            nc.tensor.transpose(ps[:, 6, 0:16], crow[:, :], ident[0:16, 0:16]).then_inc(cc_t, 1)
            pe.wait_ge(cs_lo, 1)
            with pe.Fori(0, MOD_CH // MOD_STEP) as it:
                for c in range(MOD_STEP):
                    for i in range(SB):
                        j = c * SB + i
                        pe.wait_ge(lo_done, it * (MOD_STEP * SB) + (j + 1 + RAW))
                        if i == 0:
                            pe.wait_ge(mod_ev, it * MOD_STEP + (c + 1))
                        for kk in range(2):
                            k = 2 * i + kk
                            nc.tensor.matmul(ps[:, c, :], cs4[:, k, :], wblk(whi, j, 512)[:, kk, :],
                                             start=(k == 0), stop=False)
                            mm = nc.tensor.matmul(ps[:, c, :], cs4[:, k, :], wblk(wlo, j, 512)[:, kk, :],
                                                  start=False, stop=(k == KD - 1))
                        mm.then_inc(pe_used, 1)
            pe.wait_ge(mod_ev, MOD_CH + MOD_STEP)
            pe.wait_ge(ones_in, 48)
            norm(0, 0)
            dense(IN_CH, 0)
            pe.wait_ge(gm_ev, GM_DONE[1])
            pe.wait_ge(rope_done, 2)
            pe.wait_ge(kdup_v, 4)
            pe.wait_ge(kv_in, 48)
            attention(0)
            retention()
            pe.wait_ge(at_done, 12)
            turn_in(1, lambda t, k: proj0[:, t, P * k:P * (k + 1)] if k < 4 else
                    proj0[:, t, O_QR + P * (k - 4):O_QR + P * (k - 3)], lambda t: pe.wait_ge(mix_done, t + 1))
            pe.wait_ge(tin_lo, 12)
            dense(OUT_CH[0], None)
            norm(1, 2)
            feed(T, B_FFN, None, None)
            norm(2, 3)
            dense(QKV_CH, GM_DONE[1])
            pe.wait_ge(gm_ev, GM_DONE[1] + T * len(QKV_CH))
            pe.wait_ge(c1_in, 32)
            attention(1)
            turn_in(4, lambda t, k: proj1[:, t, P * k:P * (k + 1)], lambda t: pe.wait_ge(at_done, 36))
            pe.wait_ge(tin_lo, 30)
            dense(OUT_CH[1], None)
            norm(3, 5)
            pe.wait_ge(wr_v, 2)
            for t in range(T):
                for k in range(KD):
                    mm = mm3(ps[:, t, 0:E], hT_hi[:, k, t * P:(t + 1) * P], hT_lo[:, k, t * P:(t + 1) * P],
                             wr_hi[:, k, :], wr_lo[:, k, :], k == 0, k == KD - 1)
                mm.then_inc(lo_ps, 1)
            pe.wait_ge(rt_v, 2)
            for t in range(T):
                for m in range(t + 1):
                    mm = nc.tensor.matmul(ps[:, 3 + t, 0:E], cst("before") if m == t else cst("ones"), msk[:, m, :],
                                          start=(m == 0), stop=(m == t))
            for m in range(T):
                mm = nc.tensor.matmul(ps[:, 6, 0:E], cst("ones"), msk[:, m, :], start=(m == 0), stop=(m == T - 1))
            mm.then_inc(pos_ps, 1)
            pe.wait_ge(routed, 1)
            with pe.Fori(0, E) as e:
                n_tok = pe.value_load(counts[0:1, bass.ds(e, 1)], min_val=0, max_val=T * P)
                with pe.If(n_tok < P + 1):
                    expert(1, e)
                with pe.Else():
                    with pe.If(n_tok < 2 * P + 1):
                        expert(2, e)
                    with pe.Else():
                        expert(3, e)
                    pe.nop()

        @block.scalar
        def _(act):
            chain = Chain(act, ach)

            def norm_stats(n):
                for t in range(T):
                    if n == 0 and t == 0:
                        act.wait_ge(x_in, 32)
                    elif n < 4 and t == 0:
                        act.wait_ge(x_upd, 6 * n)
                    elif n == 4:
                        act.wait_ge(x_upd, 18 + t + 1)
                    nc.scalar.activation(h[:, t, :], x[:, t, :], ACT.Square, accum_out=st[:, t:t + 1]).then_inc(nsq, 1)
                act.wait_ge(nms, n + 1)
                nc.scalar.activation(st[:, 6:9], st[:, 3:6], ACT.Sqrt).then_inc(nsd, 1)

            def turn_in(n):
                for t in range(T):
                    for kh in range(2):
                        act.wait_ge(tin_ps, 6 * n + 2 * t + kh + 1)
                        nc.scalar.activation(hT_hi[:, 4 * kh:4 * kh + 4, t * P:(t + 1) * P],
                                             ps[:, (2 * t) % 4 + kh, :].rearrange("p (k n) -> p k n", n=P), ACT.Copy)\
                            .then_inc(tin_hi, 1)

            def norm(n, turn):
                norm_stats(n)
                turn_in(turn)
                act.wait_ge(gate_ps, n + 1)
                nc.scalar.activation(gate[:, :, :], ps[:, 4:8, :].rearrange("p (a b) n -> p a (b n)", a=2), ACT.Copy)\
                    .then_inc(gate_ev, 1)

            def dense(ch, base, proj, extra=None):
                for c, (b, nb, o, n) in enumerate(ch):
                    ahead.to(min(b + nb + HL, B_MOE))
                    if proj is None:
                        continue
                    for t in range(T):
                        idx = T * c + t
                        act.wait_ge(pe_used, b + nb + HL)
                        nc.scalar.activation(proj[:, t, o:o + n], ps[:, idx % 6, 0:n], ACT.Copy).then_inc(gm_ev, 1)
                    if extra is not None and c == 1:
                        extra()

            def tables():
                act.wait_ge(tb_v, 1)
                chain(nc.scalar.activation(lgt[:, :, :], lgt[:, :, :], ACT.Exp, scale=-1.0))
                nc.scalar.activation(lgt[:, :, :], lgt[:, :, :], ACT.Ln, bias=1.0).then_inc(tb_a, 1)
                act.wait_ge(tb_v, 2)
                for hd in range(8):
                    nc.scalar.activation(dm[:, hd, :], cst("ahead"), ACT.Exp, scale=logd[:, 1, hd:hd + 1])
                    nc.scalar.activation(dm2[:, hd, :], cst("behind"), ACT.Exp, scale=logd[:, 2, hd:hd + 1])
                for d in range(2):
                    for i in range(4):
                        nc.scalar.activation(dq[:, d, i, :], cst("decay_at")[:, d * P:(d + 1) * P], ACT.Exp,
                                             scale=logd[:, 0, 4 * d + i:4 * d + i + 1])
                nc.scalar.activation(cdec[:, :, :], logd[:, 0, :].rearrange("p (a b) -> p a b", a=2), ACT.Exp,
                                     scale=float(P))
                nc.scalar.activation(kdec[:, :, :], kdec[:, :, :], ACT.Exp).then_inc(tb_a, 1)

            def attention(lay):
                npair, u0, p0, m0 = (4, 0, 0, 0) if lay == 0 else (8, 24, 4, 12)

                def prep(i):
                    if lay == 1 or i % 2 == 0:
                        ki = i // 2 if lay == 0 else 2 + i
                        sl = ki % 2 if lay == 0 else i % 2
                        act.wait_ge(at_trk, ki + 1)
                        nc.scalar.activation(kT[:, sl, :], ps[:, 4, :], ACT.Copy).then_inc(at_kT, 1)
                    act.wait_ge(at_trq, p0 + i + 1)
                    nc.scalar.activation(qT[:, i % 2, :], ps[:, 5, 0:T * P], ACT.Copy).then_inc(at_qT, 1)

                def exps(n):
                    t, u, g = n % 6 // 2, n % 2, u0 + n
                    m = m0 + n // 2
                    w = P if t == 0 else 3 * P
                    act.wait_ge(at_m, g + 1)
                    if g >= 2:
                        act.wait_ge(at_pt, g - 1)
                    if u == 0 and m >= 2:
                        act.wait_ge(at_done, m - 1)
                    nc.scalar.activation(s_p[:, g % 2, 0:w], s_sc[:, g % 2, 0:w], ACT.Exp, bias=a_neg[:, m % 2, u:u + 1],
                                         accum_out=a_sum[:, m % 2, u:u + 1]).then_inc(at_e, 1)

                def evac(n):
                    g = u0 + n
                    w = P if n % 6 // 2 == 0 else 3 * P
                    act.wait_ge(at_pt, g + 1)
                    nc.scalar.activation(s_pT[:, g % 2, 0:w], ps[:, 2 + g % 2, 0:w], ACT.Copy).then_inc(at_ptev, 1)

                N = 6 * npair
                prep(0)
                for n in range(N + 1):
                    if n < N:
                        exps(n)
                        if lay == 0 and n % 2 == 1:
                            m = n // 2
                            act.wait_ge(at_zs, m + 1)
                            nc.scalar.activation(a_es[:, m % 2, :], a_es[:, m % 2, :], ACT.Exp).then_inc(at_es, 1)
                    if n >= 1:
                        evac(n - 1)
                    if n % 6 == 3 and n // 6 + 1 < npair:
                        prep(n // 6 + 1)

            def retention():
                act.wait_ge(u_ps, 3)
                for d, z in ((0, 0), (1, 2)):
                    nc.scalar.activation(up[:, d, :, :], ps[:, z, 0:4 * DH].rearrange("p (a b) -> p a b", b=DH), ACT.Copy)\
                        .then_inc(up_ev, 1)
                for i in range(4):
                    act.wait_ge(r_tr, i + 1)
                    nc.scalar.activation(rqT[:, i % 2, :], ps[:, 0, 0:T * P], ACT.Copy).then_inc(r_q, 1)
                    nc.scalar.activation(rkT[:, i % 2, :], ps[:, 1, 0:T * P], ACT.Copy, scale=SCALE).then_inc(r_q, 1)
                for t in range(T):
                    nc.scalar.activation(proj0[:, t, O_GR:], proj0[:, t, O_GR:], ACT.Silu).then_inc(gn_a, 1)
                act.wait_ge(gn_v, 1)
                nc.scalar.activation(gst[:, 2, :, :], gst[:, 1, :, :], ACT.Sqrt).then_inc(gn_a, 1)

            def feed(nt, b0, n0, u, conv):
                def at(per, v):
                    return v if u is None else u * per + v

                def inc(t):
                    return 1 if t < nt - 1 else T - nt + 1

                def last(j):
                    return b0 + j + HL if n0 is None else n0 + (j + HL)

                def hi(s, n, tiles=range(nt)):
                    for t in tiles:
                        q = s * nt + t
                        act.wait_ge(ft_ps, at(3 * NS, 3 * s + t + 1))
                        nc.scalar.activation(fT_hi[:, 4 * s:4 * s + n // P, t * P:(t + 1) * P],
                                             ps[:, 6 + q % 2, 0:n].rearrange("p (c m) -> p c m", m=P), ACT.Copy)\
                            .then_inc(ft_hi, inc(t))

                for p, (s, g, j, nb, o, n) in enumerate(FF_PH):
                    conv(j + nb + HL)
                    if g == 0:
                        for t in range(nt):
                            act.wait_ge(pe_used, last(j + nb))
                            if s:
                                hi(s - 1, FS, [t])
                            nc.scalar.activation(sg[:, t, 0:n], ps[:, t, 0:n], ACT.Silu).then_inc(sg_a, inc(t))
                hi(NS - 1, FF_PH[-1][5])
                conv(EB)

            def loop_conv(e):
                done = [0]

                def to(end):
                    while done[0] < min(end, EB):
                        j = done[0]
                        conv_hi(act, B_MOE + j, e * EB + (B_MOE + j),
                                (e * (EB // RAW) + (BEFORE[j % RAW] + j // RAW + 1)) * 16)
                        done[0] += 1
                return to

            def expert(nt, e):
                conv = loop_conv(e)
                conv(HL)
                for k in range(KD):
                    act.wait_ge(ga_ps, e * KD + (k + 1))
                    nc.scalar.activation(hT_hi[:, k, 0:nt * P], ps[:, k, 0:nt * P], ACT.Copy).then_inc(ga_hi, 1)
                feed(nt, B_MOE, e * EB + B_MOE, e + 1, conv)
                for t in range(nt):
                    act.wait_ge(oht_ps, e * 3 + (t + 1))
                    if t:
                        act.wait_ge(sc_ps, e * 18 + 6 * t)
                    nc.scalar.activation(ohT[:, :], ps[:, 6, 0:T * P], ACT.Copy).then_inc(oht_ev, 1 if t < nt - 1 else T - nt + 1)
                    act.wait_ge(pe_used, e * EB + (B_MOE + EB + HL))
                    nc.scalar.activation(y_of(fT_hi), ps[:, 2 * t:2 * t + 2, :].rearrange("p a n -> p (a n)"), ACT.Copy)\
                        .then_inc(y_hi, 1 if t < nt - 1 else T - nt + 1)

            act.wait_ge(cc_t, 1)
            nc.scalar.activation(ccol[:, :], ps[:, 6, 0:16], ACT.Silu).then_inc(cc_silu, 1)
            act.wait_ge(cc_silu, 1)
            act.wait_ge(cs_zero, 1)
            nc.scalar.activation(cs4[:, :, 0:2], ccol[:, :].rearrange("p (a k) -> p k a", a=2), ACT.Copy).then_inc(cs_hi, 1)
            with act.Fori(0, MOD_CH // MOD_STEP) as it:
                def conv(j):
                    conv_hi(act, j, it * (MOD_STEP * SB) + j, (it * (MOD_STEP * SB // RAW) + (j // RAW + 1)) * 16)

                j = 0
                for c in range(MOD_STEP):
                    while j < min((c + 1) * SB + HL, MOD_STEP * SB):
                        conv(j)
                        j += 1
                    act.wait_ge(pe_used, it * (MOD_STEP * SB) + ((c + 1) * SB + HL))
                    if c == 0:
                        act.wait_ge(mst_free, it + 1)
                    nc.scalar.activation(mst[:, c, :], ps[0:4, c, :], ACT.Copy).then_inc(mod_ev, 1)
            ahead = Ahead(act, conv_hi, B_IN)
            norm(0, 0)
            dense(IN_CH, 0, proj0, tables)
            attention(0)
            retention()
            turn_in(1)
            dense(OUT_CH[0], None, None)
            norm(1, 2)
            act.wait_ge(stored, 16 * 6)
            feed(T, B_FFN, None, None, lambda end: ahead.to(min(B_FFN + end, B_MOE)))
            ahead.to(B_QKV + HL)
            norm(2, 3)
            dense(QKV_CH, GM_DONE[1], proj1)
            attention(1)
            turn_in(4)
            dense(OUT_CH[1], None, None)
            norm(3, 5)
            act.wait_ge(wr_in, 16)
            nc.scalar.activation(wr_hi[:, :, :], wr[:, :, :], ACT.Copy).then_inc(wr_v, 1)
            act.wait_ge(rt_v, 1)
            nc.scalar.activation(rt[:, 1, :], rt[:, 0, :], ACT.Exp).then_inc(rt_a, 1)
            act.wait_ge(pe_used, B_MOE + HL)
            act.wait_ge(routed, 1)
            with act.Fori(0, E) as e:
                n_tok = act.value_load(counts[0:1, bass.ds(e, 1)], min_val=0, max_val=T * P)
                with act.If(n_tok < P + 1):
                    expert(1, e)
                with act.Else():
                    with act.If(n_tok < 2 * P + 1):
                        expert(2, e)
                    with act.Else():
                        expert(3, e)
                    act.nop()
            norm_stats(4)

        @block.vector
        def _(dve):
            chain = Chain(dve, dch)

            def norm_rows(n):
                dve.wait_ge(nsq, T * (n + 1))
                nc.vector.tensor_scalar(st[:, 3:6], st[:, 0:3], 1.0 / D, EPS, ALU.mult, ALU.add).then_inc(nms, 1)
                dve.wait_ge(nsd, n + 1)
                chain(nc.vector.reciprocal(st[:, 9:12], st[:, 6:9]))
                dve.wait_ge(g_in, 16 * (n + 1))
                for t in range(T):
                    ins = nc.vector.scalar_tensor_tensor(out=h[:, t, :], in0=x[:, t, :], scalar=st[:, 9 + t:10 + t],
                                                         in1=gbc[:, :], op0=ALU.mult, op1=ALU.mult)
                    if n == 4:
                        ins.then_inc(h_rows, 1)
                        continue
                    chain(ins)
                    kind = min(t, 1)
                    dve.wait_ge(bc_ps, 2 * n + kind + 1)
                    chain(nc.vector.tensor_tensor(h[:, t, :], h[:, t, :], ps[:, 4 * kind:4 * kind + 2, :]
                                                  .rearrange("p a n -> p (a n)"), ALU.mult))
                    nc.vector.tensor_tensor(h[:, t, :], h[:, t, :], ps[:, 4 * kind + 2:4 * kind + 4, :]
                                            .rearrange("p a n -> p (a n)"), ALU.add).then_inc(h_rows, 1)

            def turn_in(n):
                for t in range(T):
                    for kh in range(2):
                        dve.wait_ge(tin_hi, 6 * n + 2 * t + kh + 1)
                        sl = (slice(None), slice(4 * kh, 4 * kh + 4), slice(t * P, (t + 1) * P))
                        nc.vector.tensor_tensor(hT_lo[sl], ps[:, (2 * t) % 4 + kh, :].rearrange("p (k n) -> p k n", n=P),
                                                hT_hi[sl].bitcast(F32), ALU.subtract).then_inc(tin_lo, 1)

            def norm(n, turn):
                norm_rows(n)
                turn_in(turn)

            def dense(ch, extra=None):
                for c, (b, nb, o, n) in enumerate(ch):
                    ahead.to(min(b + nb + HL, B_MOE))
                    if extra is not None and c == 1:
                        extra()

            def residual(ch, n):
                dve.wait_ge(gate_ev, n + 1)
                for c, (b, nb, o, w) in enumerate(ch):
                    for t in range(T):
                        idx = T * c + t
                        dve.wait_ge(pe_used, b + nb + HL)
                        add_to_x(t, slice(o, o + w), ps[:, idx, 0:w])

            def add_to_x(t, cols, src):
                chain(nc.vector.tensor_tensor(tmp_w[:, t, cols], src, gate[:, min(t, 1), cols], ALU.mult))
                nc.vector.tensor_tensor(x[:, t, cols], x[:, t, cols], tmp_w[:, t, cols], ALU.add).then_inc(x_upd, 1)

            def tables():
                dve.wait_ge(lg_in, 96)
                dve.wait_ge(more_in, 16)
                nc.vector.scalar_tensor_tensor(out=lgt[:, :, :], in0=lg[:, :, :], scalar=-1.0, in1=lg[:, :, :],
                                               op0=ALU.mult, op1=ALU.max).then_inc(tb_v, 1)
                chain(nc.vector.tensor_scalar(logd[:, :, :], lg[:, :, :], 0.0, None, ALU.min))
                dve.wait_ge(tb_a, 1)
                chain(nc.vector.tensor_tensor(logd[:, :, :], logd[:, :, :], lgt[:, :, :], ALU.subtract))
                for d in range(2):
                    ins = nc.vector.tensor_scalar(kdec[:, d, :], logd[:, 1 + d, :], cst("kcol")[:, d:d + 1], None, ALU.mult)
                ins.then_inc(tb_v, 1)
                dve.wait_ge(tb_a, 2)

                def over_heads(name):
                    return cst(name).unsqueeze(1).to_broadcast([P, B_HEADS, P])

                chain(nc.vector.tensor_tensor(dm[:, :, :], dm[:, :, :], over_heads("is_ahead"), ALU.mult))
                chain(nc.vector.tensor_tensor(dm2[:, :, :], dm2[:, :, :], over_heads("is_behind"), ALU.mult))
                chain(nc.vector.tensor_tensor(dm[:, :, :], dm[:, :, :], dm2[:, :, :], ALU.add))
                chain(nc.vector.tensor_scalar(kdec[:, :, :], kdec[:, :, :], SCALE, None, ALU.mult))
                dve.wait_ge(kv_in, 48)
                chain(nc.vector.tensor_scalar(sinks[:, 1, :], sinks[:, 0, :], -1.0, None, ALU.mult))

            def rotary():
                dve.wait_ge(gm_ev, GM_DONE[1])
                nh = (A_Q + A_KV) // DH
                for t in (1, 2):
                    v = proj0[:, t, 0:nh * DH].rearrange("p (n d) -> p n d", d=DH)
                    cos = cst("ropec").rearrange("p (t d) -> p t d", t=2)[:, t - 1].unsqueeze(1).to_broadcast([P, nh, DH])
                    chain(nc.vector.tensor_tensor(rot[:, 0, :].rearrange("p (n d) -> p n d", d=DH), v, cos, ALU.mult))
                    v4 = proj0[:, t, 0:nh * DH].rearrange("p (n a b) -> p n a b", a=4, b=DH // 4)
                    r4 = rot[:, 1, :].rearrange("p (n a b) -> p n a b", a=4, b=DH // 4)
                    s4 = cst("ropes").rearrange("p (t a b) -> p t a b", t=2, a=4)[:, t - 1]
                    for q in range(2):
                        sn = s4[:, q::2, :].unsqueeze(1).to_broadcast([P, nh, 2, DH // 4])
                        chain(nc.vector.tensor_tensor(r4[:, :, q::2, :], v4[:, :, 1 - q::2, :], sn, ALU.mult))
                    nc.vector.tensor_tensor(proj0[:, t, 0:nh * DH], rot[:, 0, :], rot[:, 1, :], ALU.add).then_inc(rope_done, 1)
                    dve.wait_ge(rope_done, t)
                for c, src in enumerate((ck0[:, :], proj0[:, 1, O_KA:O_VA], proj0[:, 2, O_KA:O_VA], proj0[:, 0, O_KA:O_VA])):
                    s3 = src.rearrange("p (g d) -> p g d", g=2)
                    nc.vector.tensor_copy(kdup[:, c, :].rearrange("p (g u d) -> p g u d", g=2, u=2),
                                          s3.unsqueeze(2).to_broadcast([P, 2, 2, DH])).then_inc(kdup_v, 1)

            def attention(lay):
                npair, u0, m0 = (4, 0, 0) if lay == 0 else (8, 24, 12)
                proj = proj0 if lay == 0 else proj1

                def scaled(n):
                    i, t, u = n // 6, n % 6 // 2, n % 2
                    g, m = u0 + n, m0 + n // 2
                    w = P if t == 0 else 3 * P
                    dve.wait_ge(at_s, g + 1)
                    if g >= 2:
                        dve.wait_ge(at_e, g - 1)
                    if t == 0:
                        nc.vector.tensor_scalar(s_sc[:, g % 2, 0:w], ps[:, g % 2, 0:w], SCALE, None, ALU.mult)\
                            .then_inc(at_sc, 1)
                    else:
                        if lay == 1 and t == 1 and u == 0:
                            dve.wait_ge(bm_ok, i + 1)
                        mask = cst("mask0").rearrange("p (t n) -> p t n", t=2)[:, t - 1] if lay == 0 else \
                            bm[:, i % 2, t - 1, u, :]
                        nc.vector.scalar_tensor_tensor(out=s_sc[:, g % 2, :], in0=ps[:, g % 2, 0:w], scalar=SCALE,
                                                       in1=mask, op0=ALU.mult, op1=ALU.add).then_inc(at_sc, 1)
                    dve.wait_ge(at_sc, g + 1)
                    ins = nc.vector.reduce_max(a_neg[:, m % 2, u:u + 1], s_sc[:, g % 2, 0:w], AX, negate=True)
                    if lay == 0:
                        chain(ins)
                        hd = 2 * i + u
                        ins = nc.vector.tensor_tensor(a_neg[:, m % 2, u:u + 1], a_neg[:, m % 2, u:u + 1],
                                                      sinks[:, 1, hd:hd + 1], ALU.min)
                    ins.then_inc(at_m, 1)
                    if lay == 0 and u == 1:
                        dve.wait_ge(at_m, g + 1)
                        nc.vector.tensor_tensor(a_es[:, m % 2, :], a_neg[:, m % 2, :], sinks[:, 0, 2 * i:2 * i + 2],
                                                ALU.add).then_inc(at_zs, 1)

                def finish(k):
                    i, t, m = k // 3, k % 3, m0 + k
                    tot = a_sum[:, m % 2, :]
                    if lay == 0:
                        dve.wait_ge(at_es, k + 1)
                        chain(nc.vector.tensor_tensor(a_rec[:, m % 2, :], tot, a_es[:, m % 2, :], ALU.add))
                        tot = a_rec[:, m % 2, :]
                    dve.wait_ge(at_o, m + 1)
                    chain(nc.vector.reciprocal(a_rec[:, m % 2, :], tot))
                    nc.vector.tensor_tensor(proj[:, t, P * i:P * (i + 1)].rearrange("p (u d) -> p u d", u=2),
                                            ps[:, 6 + m % 2, 0:P].rearrange("p (u d) -> p u d", u=2),
                                            a_rec[:, m % 2, :].unsqueeze(2).to_broadcast([P, 2, DH]), ALU.mult)\
                        .then_inc(at_done, 1)

                N = 6 * npair
                for n in range(N + 2):
                    if n < N:
                        scaled(n)
                    if n % 2 == 1 and n >= 3:
                        finish((n - 3) // 2)

            def retention():
                for z, (d, t) in enumerate(((0, 0), (0, 1), (1, 0), (1, 2))):
                    nc.vector.tensor_tensor(kd[:, z, :].rearrange("p (n d) -> p n d", d=DH),
                                            proj0[:, t, O_KR:O_VR].rearrange("p (n d) -> p n d", d=DH),
                                            kdec[:, d, :].unsqueeze(2).to_broadcast([P, 8, DH]), ALU.mult).then_inc(kd_v, 1)
                dve.wait_ge(s0_in, 64)
                chain(nc.vector.tensor_tensor(SS[:, :, :, :].rearrange("p a b d -> p (a b) d"),
                                              S0[:, :, :, :].rearrange("p a b d -> p (a b) d"),
                                              cdec[:, :, :].rearrange("p a b -> p (a b)").unsqueeze(2)
                                              .to_broadcast([P, 8, DH]), ALU.mult))
                dve.wait_ge(u_ps, 4)
                for d, z in ((0, 1), (1, 3)):
                    nc.vector.tensor_tensor(SS[:, d, :, :], SS[:, d, :, :],
                                            ps[:, z, 0:4 * DH].rearrange("p (a b) -> p a b", b=DH), ALU.add).then_inc(ss_v, 1)

                def queries(i):
                    dve.wait_ge(r_q, 2 * i + 2)
                    for d in range(2):
                        ins = nc.vector.tensor_tensor(rqd[:, i % 2, d, :].rearrange("p (t n) -> p t n", t=2),
                                                      ps[:, 0, P:3 * P].rearrange("p (t n) -> p t n", t=2),
                                                      dq[:, d, i, :].unsqueeze(1).to_broadcast([P, 2, P]), ALU.mult)
                    ins.then_inc(r_qd, 1)

                queries(0)
                for j in range(8):
                    dve.wait_ge(r_at_ps, j + 1)
                    nc.vector.tensor_tensor(rat[:, j % 2, :].rearrange("p (t n) -> p t n", t=T),
                                            ps[:, 2 + j % 2, 0:T * P].rearrange("p (t n) -> p t n", t=T),
                                            dm[:, j, :].unsqueeze(1).to_broadcast([P, T, P]), ALU.mult).then_inc(r_at_v, 1)
                    if j % 2 == 1 and j < 7:
                        queries(j // 2 + 1)
                dve.wait_ge(r_o, 8)

                def heads(ap):
                    return ap.rearrange("p (n d) -> p n d", d=DH)

                for t in range(T):
                    chain(nc.vector.tensor_reduce(gst[:, 0, t, :], heads(ps[:, 5 + t, :]), AX, ALU.add))
                chain(nc.vector.tensor_scalar(gst[:, 0, :, :], gst[:, 0, :, :], 1.0 / DH, None, ALU.mult))
                for t in range(T):
                    mean = gst[:, 0, t, :].unsqueeze(2).to_broadcast([P, 8, DH])
                    chain(nc.vector.tensor_tensor(heads(gn[:, t, :]), heads(ps[:, 5 + t, :]), mean, ALU.subtract))
                chain(nc.vector.tensor_tensor(gn2[:, :, :], gn[:, :, :], gn[:, :, :], ALU.mult))
                for t in range(T):
                    chain(nc.vector.tensor_reduce(gst[:, 1, t, :], heads(gn2[:, t, :]), AX, ALU.add))
                nc.vector.tensor_scalar(gst[:, 1, :, :], gst[:, 1, :, :], 1.0 / DH, EPS, ALU.mult, ALU.add).then_inc(gn_v, 1)
                dve.wait_ge(gn_a, 4)
                chain(nc.vector.reciprocal(gst[:, 3, :, :], gst[:, 2, :, :]))
                for t in range(T):
                    rs = gst[:, 3, t, :].unsqueeze(2).to_broadcast([P, 8, DH])
                    chain(nc.vector.tensor_tensor(heads(gn[:, t, :]), heads(gn[:, t, :]), rs, ALU.mult))
                    nc.vector.tensor_tensor(proj0[:, t, O_QR:O_KR], gn[:, t, :], proj0[:, t, O_GR:], ALU.mult)\
                        .then_inc(mix_done, 1)

            def feed(nt, n0, u, conv):
                def at(per, v):
                    return v if u is None else u * per + v

                def inc(t):
                    return 1 if t < nt - 1 else T - nt + 1

                def lo(s, n):
                    for t in range(nt):
                        q = s * nt + t
                        dve.wait_ge(ft_hi, at(3 * NS, 3 * s + t + 1))
                        sl = (slice(None), slice(4 * s, 4 * s + n // P), slice(t * P, (t + 1) * P))
                        nc.vector.tensor_tensor(fT_lo[sl], ps[:, 6 + q % 2, 0:n].rearrange("p (c m) -> p c m", m=P),
                                                fT_hi[sl].bitcast(F32), ALU.subtract).then_inc(ft_lo, inc(t))

                for p, (s, g, j, nb, o, n) in enumerate(FF_PH):
                    conv(j + nb + HL)
                    if g == 0 and s:
                        lo(s - 1, FS)
                    if g == 1:
                        for t in range(nt):
                            dve.wait_ge(pe_used, n0 + (j + nb + HL))
                            dve.wait_ge(sg_a, at(3 * NS, 3 * s + t + 1))
                            nc.vector.tensor_tensor(sg[:, t, 0:n], sg[:, t, 0:n], ps[:, 3 + t, 0:n], ALU.mult)\
                                .then_inc(gu_v, inc(t))
                lo(NS - 1, FF_PH[-1][5])
                conv(EB)

            def loop_conv(e):
                done = [0]

                def to(end):
                    while done[0] < min(end, EB):
                        conv_lo(dve, B_MOE + done[0], e * EB + (B_MOE + done[0]))
                        done[0] += 1
                return to

            def expert(nt, e):
                conv = loop_conv(e)
                for m in range(T):
                    ins = nc.vector.tensor_scalar(oh[:, m, 0:nt * P], cst("slots")[:, 0:nt * P],
                                                  posm[:, m, bass.ds(e, 1)], None, ALU.is_equal)
                ins.then_inc(oh_v, 1)
                conv(HL)
                for k in range(KD):
                    dve.wait_ge(ga_hi, e * KD + (k + 1))
                    nc.vector.tensor_tensor(hT_lo[:, k, 0:nt * P], ps[:, k, 0:nt * P], hT_hi[:, k, 0:nt * P].bitcast(F32),
                                            ALU.subtract).then_inc(ga_lo, 1)
                feed(nt, e * EB + B_MOE, e + 1, conv)
                banks = [b for b in range(2 * nt, 8) if b != 6]
                for t in range(nt):
                    dve.wait_ge(y_hi, e * 3 + (t + 1))
                    nc.vector.tensor_tensor(y_of(fT_lo), ps[:, 2 * t:2 * t + 2, :].rearrange("p a n -> p (a n)"),
                                            y_of(fT_hi).bitcast(F32), ALU.subtract).then_inc(y_lo, 1 if t < nt - 1 else T - nt + 1)
                    for m in range(T):
                        for half in range(2):
                            i = 6 * t + 2 * m + half
                            dve.wait_ge(sc_ps, e * 18 + (i + 1))
                            cols = slice(512 * half, 512 * (half + 1))
                            nc.vector.scalar_tensor_tensor(out=acc[:, m, cols], in0=ps[:, banks[i % len(banks)], :],
                                                           scalar=comb[:, m, bass.ds(e, 1)], in1=acc[:, m, cols],
                                                           op0=ALU.mult, op1=ALU.add)\
                                .then_inc(sc_v, 1 if i < 6 * nt - 1 else 6 * (T - nt) + 1)

            def route():
                dve.wait_ge(wr_v, 1)
                nc.vector.tensor_tensor(wr_lo[:, :, :], wr[:, :, :], wr_hi[:, :, :].bitcast(F32), ALU.subtract).then_inc(wr_v, 1)
                for t in range(T):
                    dve.wait_ge(lo_ps, t + 1)
                    chain(nc.vector.tensor_copy(logits[:, t, :], ps[:, t, 0:E]))
                    chain(nc.vector.max(best[:, t, :], logits[:, t, :]))
                    chain(nc.vector.max_index(best_i[:, t, :], best[:, t, :], logits[:, t, :]))
                chain(nc.vector.tensor_copy(best_f[:, :, :], best_i[:, :, :]))
                nc.vector.tensor_tensor(rt[:, 0, :], best[:, :, 1], best[:, :, 0], ALU.subtract).then_inc(rt_v, 1)
                for t in range(T):
                    chain(nc.vector.tensor_scalar(m1[:, t, :], cst("experts"), best_f[:, t, 0:1], None, ALU.is_equal))
                    chain(nc.vector.tensor_scalar(m2[:, t, :], cst("experts"), best_f[:, t, 1:2], None, ALU.is_equal))
                nc.vector.tensor_tensor(msk[:, :, :], m1[:, :, :], m2[:, :, :], ALU.add).then_inc(rt_v, 1)
                dve.wait_ge(rt_a, 1)
                chain(nc.vector.tensor_scalar(rt[:, 2, :], rt[:, 1, :], 1.0, None, ALU.add))
                chain(nc.vector.reciprocal(rt[:, 3, :], rt[:, 2, :]))
                chain(nc.vector.tensor_tensor(rt[:, 4, :], rt[:, 1, :], rt[:, 3, :], ALU.mult))
                for t in range(T):
                    chain(nc.vector.tensor_scalar(m1[:, t, :], m1[:, t, :], rt[:, 3, t:t + 1], None, ALU.mult))
                    chain(nc.vector.scalar_tensor_tensor(out=comb[:, t, :], in0=m2[:, t, :], scalar=rt[:, 4, t:t + 1],
                                                         in1=m1[:, t, :], op0=ALU.mult, op1=ALU.add))
                dve.wait_ge(pos_ps, 1)
                dve.wait_ge(rt_v, 2)
                for t in range(T):
                    chain(nc.vector.scalar_tensor_tensor(out=posm[:, t, :], in0=ps[:, 3 + t, 0:E], scalar=1.0,
                                                         in1=msk[:, t, :], op0=ALU.add, op1=ALU.mult))
                chain(nc.vector.tensor_scalar(posm[:, :, :], posm[:, :, :], -1.0, None, ALU.add))
                dve.wait_ge(acc_z, 1)
                chain(nc.vector.tensor_copy(counts[:, :], ps[0:1, 6, 0:E]))
                nc.vector.memset(first[:, 0:1], 0.0).then_inc(sc_v, 1)
                nc.vector.memset(first[:, 1:2], 0.0).then_inc(routed, 1)

            nc.vector.memset(first[:, 0:1], 0.0).then_inc(lo_done, RAW)
            nc.vector.memset(first[:, 1:2], 0.0).then_inc(pe_used, HL)
            nc.vector.memset(first[:, 2:3], 0.0).then_inc(mst_free, 1)
            nc.vector.memset(first[:, 3:4], 0.0).then_inc(mod_ev, MOD_STEP)
            nc.vector.memset(cs4[:, :, :].bitcast(F32), 0.0).then_inc(cs_zero, 1)
            dve.wait_ge(cs_hi, 1)
            nc.vector.tensor_tensor(cs4[:, :, 2:4], ccol[:, :].rearrange("p (a k) -> p k a", a=2),
                                    cs4[:, :, 0:2].bitcast(F32), ALU.subtract).then_inc(cs_lo, 1)
            with dve.Fori(0, MOD_CH // MOD_STEP) as it:
                for j in range(MOD_STEP * SB):
                    conv_lo(dve, j, it * (MOD_STEP * SB) + j)
            ahead = Ahead(dve, conv_lo, B_IN)
            norm(0, 0)
            dense(IN_CH, tables)
            rotary()
            attention(0)
            retention()
            turn_in(1)
            dense(OUT_CH[0])
            residual(OUT_CH[0], 0)
            norm(1, 2)
            dve.wait_ge(stored, 16 * 6)
            feed(T, B_FFN, None, lambda end: ahead.to(min(B_FFN + end, B_MOE)))
            ahead.to(B_QKV + HL)
            dve.wait_ge(gate_ev, 2)
            for t in range(T):
                for half in range(2):
                    dve.wait_ge(pe_used, B_FFN + EB + HL)
                    add_to_x(t, slice(512 * half, 512 * (half + 1)), ps[:, 2 * t + half, :])
            norm(2, 3)
            dense(QKV_CH)
            attention(1)
            turn_in(4)
            dense(OUT_CH[1])
            residual(OUT_CH[1], 2)
            norm(3, 5)
            route()
            with dve.Fori(0, E) as e:
                n_tok = dve.value_load(counts[0:1, bass.ds(e, 1)], min_val=0, max_val=T * P)
                with dve.If(n_tok < P + 1):
                    expert(1, e)
                with dve.Else():
                    with dve.If(n_tok < 2 * P + 1):
                        expert(2, e)
                    with dve.Else():
                        expert(3, e)
                    dve.nop()
            dve.wait_ge(gate_ev, 4)
            dve.wait_ge(sc_v, E * 18 + 1)
            for t in range(T):
                chain(nc.vector.tensor_tensor(acc[:, t, :], acc[:, t, :], gate[:, min(t, 1), :], ALU.mult))
                nc.vector.tensor_tensor(x[:, t, :], x[:, t, :], acc[:, t, :], ALU.add).then_inc(x_upd, 1)
            norm_rows(4)


_INS = ['x_prompt', 'x_sample', 'cache_a_k', 'cache_a_v', 'state_ret_fwd', 'state_ret_bwd', 'cache_c_k',
        'cache_c_v', 'c', 'c_ctx', 'mod_w', 'mod_b', 'norm1_g', 'norm2_g', 'final_g', 'ev_w_in', 'ev_w_out',
        'ev_sink', 'ev_ret_logit_fwd', 'ev_ret_logit_bwd', 'ev_ffn_w_gu', 'ev_ffn_w_down', 'od_w_qkv',
        'od_w_out', 'od_rpb', 'od_w_router', 'od_moe_w_gu', 'od_moe_w_down']
_OUTS = [(1, 128, 1024), (1, 256, 1024), (1, 1, 128, 2, 64), (1, 1, 128, 2, 64), (1, 1, 8, 64, 64),
         (1, 1, 8, 64, 64), (1, 1, 128, 16, 64), (1, 1, 128, 16, 64)]


def kernel(**inputs):
    import concourse.bacc as _bacc
    from concourse.bass_utils import run_bass_kernel_spmd as _run

    nc = _bacc.Bacc("TRN2", target_bir_lowering=False, num_devices=1)
    arrays, args = {}, []
    for name in _INS:
        a = inputs[name]
        arrays[f"in_{name}"] = np.ascontiguousarray(a[..., ::-1] if name == "od_rpb" else a)
    arrays["constants"] = constants()
    for name, a in arrays.items():
        args.append(nc.dram_tensor(name, a.shape, mybir.dt.from_np(a.dtype), kind="ExternalInput").ap())
    outs = [nc.dram_tensor(f"out_{i}", shape, F32, kind="ExternalOutput").ap() for i, shape in enumerate(_OUTS)]
    build(nc, args, outs)
    r = _run(nc, [arrays], core_ids=[0])
    return tuple(r.results[0][f"out_{i}"] for i in range(len(_OUTS)))
```

```python
from contextlib import ExitStack

import numpy as np

import concourse.bass as bass
from concourse import mybir

F32 = mybir.dt.float32
F32R = mybir.dt.float32r
I32 = mybir.dt.int32
U32 = mybir.dt.uint32
ALU = mybir.AluOpType
ACT = mybir.ActivationFunctionType
AX = mybir.AxisListType.X

P = 128
D = 1024
KD = D // P
T = 3
DH = 64
GRID_W = 64
A_HEADS, A_KV_HEADS, B_HEADS, C_HEADS = 8, 2, 8, 16
A_Q, A_KV, B_W = A_HEADS * DH, A_KV_HEADS * DH, B_HEADS * DH
NB_ROWS, NB_COLS = 8, 16
C_W = C_HEADS * DH
IN_EVEN = A_Q + 2 * A_KV + 4 * B_W
O_QA, O_KA, O_VA = 0, A_Q, A_Q + A_KV
O_QR = O_VA + A_KV
O_KR, O_VR, O_GR = O_QR + B_W, O_QR + 2 * B_W, O_QR + 3 * B_W
FF = 2816
E = 8
EPS = 1e-6
NEG = -1e30
SCALE = DH ** -0.5

RAW = 6
HL = 3
BLK = 1024
SB = 4
FS = 512
NS = -(-FF // FS)
FF_PH = []
for _s in range(NS):
    for _g in range(2):
        _n = min(FS, FF - _s * FS)
        _j = FF_PH[-1][2] + FF_PH[-1][3] if FF_PH else 0
        FF_PH.append((_s, _g, _j, KD * _n // BLK, _s * FS, _n))
GB = FF_PH[-1][2] + FF_PH[-1][3]
DB = FF // P
EB = GB + DB
MOD_CH, MOD_STEP = 24, 3
B_MOD = 0
B_IN = B_MOD + MOD_CH * SB
IN_FULL = IN_EVEN // 512
B_OUT0 = B_IN + IN_FULL * SB + 2
B_FFN = B_OUT0 + 2 * SB
B_QKV = B_FFN + EB
B_OUT1 = B_QKV + 6 * SB
B_MOE = B_OUT1 + 2 * SB
assert IN_EVEN % 512 == 256 and EB % RAW == 0 and EB % HL == 0 and (MOD_STEP * SB) % RAW == 0
PADW = 127
DR = 7

CONSTS = {}
_at = 0
for _name, _n in (("ident", P), ("ones", P), ("before", P), ("slots", T * P), ("experts", E), ("sel", 4 * P),
                  ("ropec", 2 * DH), ("ropes", 2 * DH), ("mask0", 2 * 3 * P), ("ahead", P), ("behind", P),
                  ("is_ahead", P), ("is_behind", P), ("decay_at", 2 * P), ("kcol", 2), ("cmask", GRID_W)):
    CONSTS[_name] = (_at, _n)
    _at += _n
NCONST = _at


def constants():
    c = np.zeros((P, NCONST), np.float32)

    def put(name, a):
        o, n = CONSTS[name]
        c[:, o:o + n] = np.asarray(a, np.float64).reshape(P, n)

    i = np.arange(P)
    put("ident", np.eye(P))
    put("ones", np.ones((P, P)))
    put("before", i[:, None] < i[None, :])
    put("slots", np.tile(np.arange(T * P), (P, 1)))
    put("experts", np.tile(np.arange(E), (P, 1)))
    sel = np.zeros((4, 32, 4, P))
    for m, rows in enumerate(((0, 2, 4), (1, 3, 4), (0, 2, 4, 5), (1, 3, 4, 5))):
        for r in rows:
            sel[:, r, m] = 1
    put("sel", sel.reshape(P, 4 * P))
    nf = DH // 4
    inv = 10000.0 ** (-np.arange(nf, dtype=np.float32) / np.float32(nf))
    t = np.arange(2 * P)
    ang = np.stack([(t // GRID_W)[:, None] * inv, (t % GRID_W)[:, None] * inv], 1).astype(np.float32)
    cos, sin = np.cos(ang), np.sin(ang)
    put("ropec", np.concatenate([cos, cos], -1).reshape(2, P, DH).transpose(1, 0, 2))
    put("ropes", np.concatenate([-sin, sin], -1).reshape(2, P, DH).transpose(1, 0, 2))
    m0 = np.zeros((P, 2, 3 * P))
    m0[:, 0, 2 * P:] = np.where(i[None, :] + P - i[:, None] <= P, 0, NEG)
    m0[:, 1, P:2 * P] = np.where(i[:, None] + P - i[None, :] <= P, 0, NEG)
    put("mask0", m0)
    d = i[None, :] - i[:, None]
    put("ahead", np.maximum(d, 0))
    put("behind", np.maximum(-d, 0))
    put("is_ahead", d >= 0)
    put("is_behind", d <= 0)
    put("decay_at", np.tile(np.concatenate([i + 1, P - i]), (P, 1)))
    put("kcol", np.stack([P - 1 - i, i], 1))
    cq = i % GRID_W
    ck = np.arange(GRID_W)
    start = np.clip(cq - NB_COLS // 2, 0, GRID_W - NB_COLS)
    ok = (ck[None] >= start[:, None]) & (ck[None] < start[:, None] + NB_COLS)
    put("cmask", np.where(ok, 0, NEG))
    return c


def build(nc, a, outs):
    (x_prompt, x_sample, cache_a_k, cache_a_v, st_f, st_b, cache_c_k, cache_c_v, c_in, c_ctx, mod_w, mod_b,
     norm1_g, norm2_g, final_g, w_in, w_out0, sink, lg_f, lg_b, w_gu, w_down, w_qkv, w_out1, rpb, w_router,
     moe_gu, moe_down, const) = a
    y_prompt, y_sample, new_a_k, new_a_v, new_f, new_b, new_c_k, new_c_v = outs

    mods = nc.dram_tensor("mods_scratch", [4, MOD_CH * 512], F32).ap()
    padded = nc.dram_tensor("rpb_scratch", [C_HEADS * DR, PADW], F32).ap()

    with ExitStack() as ctx:
        def sem(name):
            return ctx.enter_context(nc.semaphore(name))

        top = [0]

        def sb(name, shape, dt=F32, at=None):
            n = 4 * int(np.prod(shape[1:]))
            n = (n + 31) // 32 * 32
            o = top[0] if at is None else at
            h = nc.alloc_sbuf_tensor_at(name, shape, dt, offset=o)
            if at is None:
                top[0] = o + n
            return h

        first = ctx.enter_context(nc.sbuf_tensor("first", [P, 8], F32))
        top[0] = (nc.sbuf_base + 63) // 32 * 32
        x = sb("x", [P, T, D])
        keep = sb("keep", [P, CONSTS["ropec"][0]])
        rawb = sb("rawb", [P, RAW, BLK])
        whi = sb("whi", [P, HL, BLK], F32R)
        wlo = sb("wlo", [P, HL, BLK], F32R)
        hT_hi = sb("hT_hi", [P, KD, T * P], F32R)
        hT_lo = sb("hT_lo", [P, KD, T * P], F32R)
        mrow = sb("mrow", [P, D])
        gate = sb("gate", [P, 2, D])
        gbc = sb("gbc", [P, D])
        st = sb("st", [P, 64])
        comb = sb("comb", [P, T, 1 + E])
        posm = sb("posm", [P, T, E + 1])
        counts = sb("counts", [1, E], I32)
        region = top[0]
        top[0] = region
        h = sb("h", [P, T, D])
        act_at = top[0]
        acc = sb("acc", [P, T, D])
        fT_hi = sb("fT_hi", [P, DB, T * P], F32R)
        fT_lo = sb("fT_lo", [P, DB, T * P], F32R)
        sg_at = top[0]
        sg = sb("sg", [P, T, FS])
        ohT_more = sb("ohT_more", [P, T - 1, T * P], F32R, at=sg_at)
        oh = sb("oh", [P, T, T * P])
        ohT = sb("ohT", [P, T * P], F32R)
        ff_top = top[0]
        top[0] = act_at + 12 * 1024
        wr = sb("wr", [P, KD, E])
        wr_hi = sb("wr_hi", [P, KD, E], F32R)
        wr_lo = sb("wr_lo", [P, KD, E], F32R)
        logits = sb("logits", [P, T, E])
        best = sb("best", [P, T, 8])
        best_i = sb("best_i", [P, T, 8], U32)
        best_f = sb("best_f", [P, T, 8])
        m1 = sb("m1", [P, T, E])
        m2 = sb("m2", [P, T, E])
        msk = sb("msk", [P, T, E])
        rt = sb("rt", [P, 8, T])
        top[0] = act_at
        crow = sb("crow", [16, P])
        ccol = sb("ccol", [P, 16])
        cs4 = sb("cs4", [P, KD, P], F32R)
        mst = sb("mst", [4, MOD_STEP, 512])
        padrow = sb("padrow", [C_HEADS * DR, PADW])
        top[0] = region
        s_sc = sb("s_sc", [P, 2, 3 * P])
        s_p = sb("s_p", [P, 2, 3 * P])
        s_pT = sb("s_pT", [P, 2, 3 * P])
        a_neg = sb("a_neg", [P, 2, 2])
        a_sum = sb("a_sum", [P, 2, 2])
        a_es = sb("a_es", [P, 2, 2])
        a_rec = sb("a_rec", [P, 2, 2])
        assert top[0] <= act_at
        top[0] = act_at
        kT = sb("kT", [P, 2, 4 * P])
        qT = sb("qT", [P, 2, T * P])
        shared = top[0]
        proj0 = sb("proj0", [P, T, IN_EVEN])
        more = sb("more", [P, NCONST - CONSTS["ropec"][0]])
        ck0 = sb("ck0", [P, A_KV])
        cv0 = sb("cv0", [P, A_KV])
        kdup = sb("kdup", [P, 4, 2 * A_KV])
        sinks = sb("sinks", [P, 2, A_HEADS])
        lg = sb("lg", [P, 3, 8])
        lgt = sb("lgt", [P, 3, 8])
        logd = sb("logd", [P, 3, 8])
        dm = sb("dm", [P, B_HEADS, P])
        dq = sb("dq", [P, 2, 4, P])
        kdec = sb("kdec", [P, 2, 8])
        cdec = sb("cdec", [P, 2, 4])
        S0 = sb("S0", [P, 2, 4, DH])
        SS = sb("SS", [P, 2, 4, DH])
        up = sb("up", [P, 2, 4, DH])
        gst = sb("gst", [P, 4, T, 8])
        kd_at = top[0]
        kd = sb("kd", [P, 4, B_W])
        rqT = sb("rqT", [P, 2, T * P])
        rkT = sb("rkT", [P, 2, T * P])
        rqd = sb("rqd", [P, 2, 2, 2 * P])
        rat = sb("rat", [P, 2, T * P])
        top0 = top[0]
        rot = sb("rot", [P, 2, 640], at=kd_at)
        dm2 = sb("dm2", [P, B_HEADS, P], at=kd_at + 8 * 1024)
        gn = sb("gn", [P, T, B_W], at=kd_at)
        gn2 = sb("gn2", [P, T, B_W], at=kd_at + 4 * T * B_W)
        tmp_w = sb("tmp_w", [P, T, D], at=region)
        top[0] = shared
        proj1 = sb("proj1", [P, T, 3 * C_W])
        ck1 = sb("ck1", [P, C_W])
        cv1 = sb("cv1", [P, C_W])
        bm = sb("bm", [P, 2, 2, 2, 3 * P])
        bmr = sb("bmr", [P, 2, 4, 4, GRID_W])
        cm = sb("cm", [P, GRID_W])
        assert max(ff_top, top0, top[0]) <= nc.sbuf_usable_end, (ff_top, top0, top[0], nc.sbuf_usable_end)

        ps = ctx.enter_context(nc.psum_tensor("ps", [P, 8, 512], F32))

        def cst(name):
            o, n = CONSTS[name]
            base = CONSTS["ropec"][0]
            return keep[:, o:o + n] if o < base else more[:, o - base:o - base + n]

        ident = cst("ident")

        w_loaded = [sem(f"w_loaded{i}") for i in range(RAW)]
        hi_done = sem("hi_done")
        lo_done = sem("lo_done")
        pe_used = sem("pe_used")
        x_in = sem("x_in")
        keep_in = sem("keep_in")
        more_in = sem("more_in")
        crow_in = sem("crow_in")
        g_in = sem("g_in")
        m_in = sem("m_in")
        ones_in = sem("ones_in")
        cc_t = sem("cc_t")
        cc_silu = sem("cc_silu")
        cs_zero = sem("cs_zero")
        cs_hi = sem("cs_hi")
        cs_lo = sem("cs_lo")
        mod_ev = sem("mod_ev")
        mst_free = sem("mst_free")
        mod_out = sem("mod_out")
        nsq = sem("nsq")
        nms = sem("nms")
        nsd = sem("nsd")
        nrs = sem("nrs")
        bc_ps = sem("bc_ps")
        h_rows = sem("h_rows")
        gate_ps = sem("gate_ps")
        gate_ev = sem("gate_ev")
        tin_ps = sem("tin_ps")
        tin_hi = sem("tin_hi")
        tin_lo = sem("tin_lo")
        gm_ev = sem("gm_ev")
        res_t = sem("res_t")
        x_upd = sem("x_upd")
        dch = sem("dch")
        ach = sem("ach")
        rope_done = sem("rope_done")
        at_trk = sem("at_trk")
        at_trq = sem("at_trq")
        at_kT = sem("at_kT")
        at_qT = sem("at_qT")
        at_s = sem("at_s")
        at_sc = sem("at_sc")
        at_m = sem("at_m")
        at_e = sem("at_e")
        at_pt = sem("at_pt")
        at_ptev = sem("at_ptev")
        at_o = sem("at_o")
        at_es = sem("at_es")
        at_zs = sem("at_zs")
        at_done = sem("at_done")
        kv_in = sem("kv_in")
        lg_in = sem("lg_in")
        s0_in = sem("s0_in")
        tb_a = sem("tb_a")
        tb_v = sem("tb_v")
        kd_v = sem("kd_v")
        kdup_v = sem("kdup_v")
        u_ps = sem("u_ps")
        up_ev = sem("up_ev")
        ss_v = sem("ss_v")
        r_tr = sem("r_tr")
        r_q = sem("r_q")
        r_qd = sem("r_qd")
        r_at_ps = sem("r_at_ps")
        r_at_v = sem("r_at_v")
        r_o = sem("r_o")
        gn_v = sem("gn_v")
        gn_a = sem("gn_a")
        mix_done = sem("mix_done")
        pad_z = sem("pad_z")
        pad_in = sem("pad_in")
        pad_out = sem("pad_out")
        cm_in = sem("cm_in")
        bm_z = sem("bm_z")
        bm_in = [sem("bm_in0"), sem("bm_in1")]
        bm_ok = sem("bm_ok")
        c1_in = sem("c1_in")
        sg_a = sem("sg_a")
        gu_v = sem("gu_v")
        ft_ps = sem("ft_ps")
        ft_hi = sem("ft_hi")
        ft_lo = sem("ft_lo")
        y_hi = sem("y_hi")
        y_lo = sem("y_lo")
        wr_in = sem("wr_in")
        wr_v = sem("wr_v")
        lo_ps = sem("lo_ps")
        rt_v = sem("rt_v")
        rt_a = sem("rt_a")
        pos_ps = sem("pos_ps")
        routed = sem("routed")
        acc_z = sem("acc_z")
        oh_v = sem("oh_v")
        ga_ps = sem("ga_ps")
        ga_hi = sem("ga_hi")
        ga_lo = sem("ga_lo")
        oht_ps = sem("oht_ps")
        oht_ev = sem("oht_ev")
        sc_ps = sem("sc_ps")
        sc_v = sem("sc_v")
        stored = sem("stored")
        stored_sp = sem("stored_sp")

        def slot_h(b):
            return (b if b < B_MOE else b - B_MOE) % HL

        def slot_r(b):
            return (b if b < B_MOE else b - B_MOE) % RAW

        def conv_hi(act, b, n=None, loads=None):
            s, r = slot_r(b), slot_h(b)
            act.wait_ge(w_loaded[s], 16 * (b // RAW + 1) if loads is None else loads)
            act.wait_ge(pe_used, (b if n is None else n) + 1)
            nc.scalar.activation(whi[:, r, :], rawb[:, s, :], ACT.Copy).then_inc(hi_done, 1)

        def conv_lo(dve, b, n=None, loads=None):
            s, r = slot_r(b), slot_h(b)
            dve.wait_ge(hi_done, (b if n is None else n) + 1)
            nc.vector.tensor_tensor(wlo[:, r, :], rawb[:, s, :], whi[:, r, :].bitcast(F32),
                                    ALU.subtract).then_inc(lo_done, 1)

        class Ahead:

            def __init__(self, eng, conv, start):
                self.eng, self.conv, self.b = eng, conv, start

            def to(self, end):
                while self.b < end:
                    self.conv(self.eng, self.b)
                    self.b += 1

        class Chain:

            def __init__(self, eng, s):
                self.eng, self.s, self.n = eng, s, 0

            def __call__(self, ins):
                self.n += 1
                ins.then_inc(self.s, 1)
                self.eng.wait_ge(self.s, self.n)

        def mm3(out, l_hi, l_lo, r_hi, r_lo, start, stop):
            nc.tensor.matmul(out, l_hi, r_hi, start=start, stop=False)
            nc.tensor.matmul(out, l_hi, r_lo, start=False, stop=False)
            return nc.tensor.matmul(out, l_lo, r_hi, start=False, stop=stop)

        def wblk(buf, b, cols):
            return buf[:, slot_h(b), :].rearrange("p (k n) -> p k n", n=cols)

        def tiles_of(ap):
            return ap.rearrange("(t p) d -> p t d", p=P)

        def kn(w):
            return w.rearrange("(k p) n -> p k n", p=P)

        def chunks(b0, ncols):
            out = []
            b = b0
            for o in range(0, ncols, 512):
                n = min(512, ncols - o)
                k = KD * n // BLK
                out.append((b, k, o, n))
                b += k
            return out

        IN_CH = chunks(B_IN, IN_EVEN)
        QKV_CH = chunks(B_QKV, 3 * C_W)
        OUT_CH = [chunks(B_OUT0, D), chunks(B_OUT1, D)]
        BEFORE = [sum(b % RAW == s for b in range(B_MOE)) for s in range(RAW)]

        def y_of(buf, i=0):
            end = DB * T * P - i * D
            return buf[:, :, :].rearrange("p a n -> p (a n)")[:, end - D:end]

        def turned(i):
            return ohT[:, :] if i == 0 else ohT_more[:, i - 1, :]

        G_END = {ph[2] + ph[3]: ph[0] for ph in FF_PH if ph[1] == 0}
        U_END = {ph[2] + ph[3]: ph[0] for ph in FF_PH if ph[1] == 1}
        TURN = {ph[2] + ph[3] - 1: ph[0] - 1 for ph in FF_PH if ph[1] == 0 and ph[0]}
        TURN[GB + 3] = NS - 1
        WIDTH = {ph[0]: ph[5] for ph in FF_PH}
        Y_LAST = 1
        SCATTER = {b: i for i, b in enumerate((4, 5, 6, 7, 9, 10))}
        OH_TURN = {GB + 5 + 2 * t: t for t in range(T)}
        ONE_HOT = GB + 10
        GATHER = {GB + 12: 0, GB + 14: 1}

        def down_bank(nt, t):
            return 2 * t if nt == T else 4 * (t + T - 1 - nt) if nt > 1 else 4

        def sc_inc(nt, i):
            return 1 if i < 6 * nt - 1 else 6 * (T - nt) + 1

        def ga_inc(nt, half):
            return 1 + 2 * (T - nt) if half == 0 else 1

        def y_at(nt, e, t):
            return e * T + (T + 1 - nt) + (t + 1)

        GM_DONE = [0, T * len(IN_CH)]

        block = ctx.enter_context(nc.Block())

        @block.sync
        def _(sp):
            def load(b, src, n=None):
                sp.wait_ge(lo_done, (b if n is None else n) + 1)
                view = rawb[:, slot_r(b), :]
                if len(src.shape) == 3:
                    view = view.rearrange("p (k n) -> p k n", n=src.shape[2])
                sp.dma_start(view, src).then_inc(w_loaded[slot_r(b)], 16)

            def load_chunks(ch, w):
                for b, k, o, n in ch:
                    rows = BLK // n
                    for i in range(k):
                        load(b + i, kn(w)[:, i * rows:(i + 1) * rows, o:o + n])

            def load_ff(b0, gu, down, n0=None):
                guv = kn(gu)
                for s, g, j, k, o, n in FF_PH:
                    rows = BLK // n
                    for i in range(k):
                        load(b0 + j + i, guv[:, i * rows:(i + 1) * rows, g * FF + o:g * FF + o + n],
                             None if n0 is None else n0 + (j + i))
                for j in range(DB):
                    load(b0 + GB + j, down[j * P:(j + 1) * P, :], None if n0 is None else n0 + (GB + j))

            mw = mod_w.rearrange("l (k p) n -> p k l n", p=P)
            with sp.Fori(0, MOD_CH // MOD_STEP) as it:
                for c in range(MOD_STEP):
                    for i in range(SB):
                        j = c * SB + i
                        lay = it // (MOD_CH // MOD_STEP // 2)
                        col = (it % (MOD_CH // MOD_STEP // 2)) * (MOD_STEP * 512) + c * 512
                        sp.wait_ge(lo_done, it * (MOD_STEP * SB) + (j + 1))
                        sp.dma_start(rawb[:, j % RAW, :].rearrange("p (k n) -> p k n", n=512),
                                     mw[:, 2 * i:2 * i + 2, bass.ds(lay, 1), bass.ds(col, 512)]
                                     .rearrange("p k l n -> p k (l n)")).then_inc(w_loaded[j % RAW], 16)
            load_chunks(IN_CH, w_in[0])
            load_chunks(OUT_CH[0], w_out0[0])
            load_ff(B_FFN, w_gu[0], w_down[0])
            load_chunks(QKV_CH, w_qkv[0])
            load_chunks(OUT_CH[1], w_out1[0])
            sp.wait_ge(lo_done, B_MOE + RAW)
            with sp.Fori(0, E) as e:
                load_ff(B_MOE, moe_gu[0, bass.ds(e, 1)].rearrange("e d n -> (e d) n"),
                        moe_down[0, bass.ds(e, 1)].rearrange("e d n -> (e d) n"), n0=e * EB + B_MOE)


        @block.gpsimd
        def _(pool):
            pool.dma_start(crow[0:8, :], c_ctx.rearrange("(k p) -> k p", p=P)).then_inc(crow_in, 16)
            pool.dma_start(crow[8:16, :], c_in[0].rearrange("(k p) -> k p", p=P)).then_inc(crow_in, 16)
            nkeep = CONSTS["ropec"][0]
            pool.dma_start(keep[:, :], const[:, 0:nkeep]).then_inc(keep_in, 16)
            nc.gpsimd.memset(padrow[:, :], 0.0).then_inc(pad_z, 1)
            pool.dma_start(x[:, 0, :], x_prompt[0]).then_inc(x_in, 16)
            pool.dma_start(x[:, 1:3, :], tiles_of(x_sample[0])).then_inc(x_in, 16)
            o1 = CONSTS["ones"][0]
            for q in range(3):
                pool.dma_start(mrow[32 * q + 5:32 * q + 6, :].rearrange("p (a b) -> p a b", b=P),
                               const[0:8, o1:o1 + P].unsqueeze(0)).then_inc(ones_in, 16)
            pool.dma_start(more[:, :], const[:, nkeep:NCONST]).then_inc(more_in, 16)
            pool.dma_start(ck0[:, :], cache_a_k[0, 0].rearrange("t h d -> t (h d)")).then_inc(kv_in, 16)
            pool.dma_start(cv0[:, :], cache_a_v[0, 0].rearrange("t h d -> t (h d)")).then_inc(kv_in, 16)
            pool.dma_start(sinks[:, 0, :], sink[0].partition_broadcast(P)).then_inc(kv_in, 16)
            for d, src in enumerate((lg_f, lg_b)):
                pool.dma_start(lg[:, 1 + d, :], src[0].partition_broadcast(P)).then_inc(lg_in, 16)
                for u in range(2):
                    pool.dma_start(lg[DH * u:DH * (u + 1), 0, 4 * d:4 * d + 4],
                                   src[0].rearrange("(i u) -> u i", u=2)[u].partition_broadcast(DH),
                                   allow_slow_non_contiguous=True).then_inc(lg_in, 16)
            for d, src in enumerate((st_f, st_b)):
                for u in range(2):
                    pool.dma_start(S0[DH * u:DH * (u + 1), d, :, :],
                                   src[0, 0].rearrange("(i u) k v -> u k i v", u=2)[u]).then_inc(s0_in, 16)
            pool.wait_ge(pad_z, 1)
            pool.dma_start(padded, padrow[:, :]).then_inc(pad_out, 16)
            pool.wait_ge(pad_out, 16)
            pool.dma_start(padded.rearrange("(h r) c -> h r c", r=DR)[:, :, 48:48 + 2 * NB_COLS - 1],
                           rpb[0][:, NB_ROWS - 4:NB_ROWS + 3, :]).then_inc(pad_in, 16)

            with pool.Fori(0, MOD_CH // MOD_STEP) as it:
                pool.wait_ge(mod_ev, it * MOD_STEP + 2 * MOD_STEP)
                pool.dma_start(mods[:, bass.ds(it * (MOD_STEP * 512), MOD_STEP * 512)],
                               mst[:, :, :].rearrange("p a b -> p (a b)")).then_inc(mod_out, 16)
                pool.wait_ge(mod_out, it * 16 + 16)
                pool.sem_inc(mst_free, 1)

            def norm_rows(n):
                lay, half = n // 2, n % 2
                if n:
                    pool.wait_ge(gate_ps, n)
                    pool.wait_ge(h_rows, T * n)
                else:
                    pool.wait_ge(mod_out, 16 * (MOD_CH // MOD_STEP))
                g = (norm1_g, norm2_g)[half]
                pool.dma_start(gbc[:, :], g[lay].partition_broadcast(P)).then_inc(g_in, 16)
                for q in range(3):
                    c0 = (3 * half + q) * D
                    pool.dma_start(mrow[32 * q:32 * q + 4, :], mods[:, lay * 6 * D + c0:lay * 6 * D + c0 + D])\
                        .then_inc(m_in, 16)
                    pool.dma_start(mrow[32 * q + 4:32 * q + 5, :], mod_b[lay:lay + 1, c0:c0 + D]).then_inc(m_in, 16)

            norm_rows(0)
            norm_rows(1)
            pool.wait_ge(gm_ev, GM_DONE[1])
            pool.dma_start(new_a_k[0, 0].rearrange("t h d -> t (h d)"), proj0[:, 0, O_KA:O_KA + A_KV]).then_inc(stored, 16)
            pool.dma_start(new_a_v[0, 0].rearrange("t h d -> t (h d)"), proj0[:, 0, O_VA:O_VA + A_KV]).then_inc(stored, 16)
            pool.wait_ge(up_ev, 2)
            for d, dst in enumerate((new_f, new_b)):
                for u in range(2):
                    pool.dma_start(dst[0, 0].rearrange("(i u) k v -> u k i v", u=2)[u],
                                   up[DH * u:DH * (u + 1), d, :, :]).then_inc(stored, 16)
            norm_rows(2)
            pool.wait_ge(x_upd, 12)
            pool.dma_start(ck1[:, :], cache_c_k[0, 0].rearrange("t h d -> t (h d)")).then_inc(c1_in, 16)
            pool.dma_start(cv1[:, :], cache_c_v[0, 0].rearrange("t h d -> t (h d)")).then_inc(c1_in, 16)
            oc = CONSTS["cmask"][0]
            pool.dma_start(cm[:, :], const[:, oc:oc + GRID_W]).then_inc(cm_in, 16)
            for r in range(2):
                nc.gpsimd.memset(bm[:, r, :, :, 0:P], 0.0).then_inc(bm_z, 1)
            pool.wait_ge(pad_in, 16)
            pool.wait_ge(cm_in, 16)

            def bias_load(i):
                if i >= 2:
                    pool.wait_ge(bm_ok, i - 1)
                for qt in range(2):
                    for rq in range(2):
                        for u in range(2):
                            row = (2 * i + u) * DR + 3 - (2 * qt + rq)
                            src = bass.AP(padded.tensor, row * PADW, [[1, GRID_W], [PADW, 4], [1, GRID_W]])
                            pool.dma_start(bmr[GRID_W * rq:GRID_W * (rq + 1), i % 2, 2 * qt + u, :, :], src)\
                                .then_inc(bm_in[i % 2], 16)

            bias_load(0)
            for i in range(8):
                if i < 7:
                    bias_load(i + 1)
                pool.wait_ge(bm_in[i % 2], 128 * (i // 2 + 1))
                if i >= 2:
                    pool.wait_ge(at_sc, 24 + 6 * (i - 1))
                v = bm[:, i % 2, :, :, P:].rearrange("p a b (k c) -> p (a b) k c", c=GRID_W)
                m = cm[:, :].unsqueeze(1).unsqueeze(1).to_broadcast([P, 4, 4, GRID_W])
                nc.gpsimd.tensor_tensor(v, bmr[:, i % 2, :, :, ::-1], m, ALU.add).then_inc(bm_ok, 1)
            pool.dma_start(new_c_k[0, 0].rearrange("t h d -> t (h d)"), proj1[:, 0, C_W:2 * C_W]).then_inc(stored, 16)
            pool.dma_start(new_c_v[0, 0].rearrange("t h d -> t (h d)"), proj1[:, 0, 2 * C_W:]).then_inc(stored, 16)
            norm_rows(3)
            pool.wait_ge(stored, 16 * 8)
            pool.wait_ge(x_upd, 18)
            pool.dma_start(wr[:, :, :], kn(w_router[0]), allow_slow_non_contiguous=True).then_inc(wr_in, 16)
            nc.gpsimd.memset(acc[:, :, :], 0.0).then_inc(acc_z, 1)
            pool.wait_ge(h_rows, 12)
            pool.dma_start(gbc[:, :], final_g.partition_broadcast(P)).then_inc(g_in, 16)
            for t in range(T):
                pool.wait_ge(h_rows, 13 + t)
                dst = y_prompt[0] if t == 0 else y_sample[0, (t - 1) * P:t * P, :]
                pool.dma_start(dst, h[:, t, :]).then_inc(stored, 16)
            pool.wait_ge(stored, 16 * 11)

        @block.tensor
        def _(pe):
            def norm_bc(n):
                pe.wait_ge(m_in, 96 * (n + 1))
                if n:
                    pe.wait_ge(x_upd, 6 * n)
                for kind in range(2):
                    for part, m in ((1, 2 + kind), (0, kind)):
                        for half in range(2):
                            q = 32 * part
                            mm = nc.tensor.matmul(ps[:, 4 * kind + 2 * (1 - part) + half, :],
                                                  cst("sel")[q:q + 6, m * P:(m + 1) * P],
                                                  mrow[q:q + 6, 512 * half:512 * (half + 1)], start=True, stop=True)
                    mm.then_inc(bc_ps, 1)

            def norm_gate(n):
                for kind in range(2):
                    for half in range(2):
                        mm = nc.tensor.matmul(ps[:, 4 + 2 * kind + half, :], cst("sel")[64:70, kind * P:(kind + 1) * P],
                                              mrow[64:70, 512 * half:512 * (half + 1)], start=True, stop=True)
                mm.then_inc(gate_ps, 1)

            def turn_in(n, src, ready):
                for t in range(T):
                    ready(t)
                    if t == 2:
                        pe.wait_ge(tin_lo, 6 * n + 2)
                    for kh in range(2):
                        for k in range(4):
                            mm = nc.tensor.transpose(ps[:, (2 * t) % 4 + kh, k * P:(k + 1) * P],
                                                     src(t, 4 * kh + k), ident)
                        mm.then_inc(tin_ps, 1)

            def norm(n, turn):
                norm_bc(n)
                turn_in(turn, lambda t, k: h[:, t, k * P:(k + 1) * P], lambda t: pe.wait_ge(h_rows, T * n + t + 1))
                norm_gate(n)
                pe.wait_ge(tin_lo, 6 * (turn + 1))
                pe.wait_ge(gate_ev, n + 1)

            def dense(ch, base):
                for c, (b, nb, o, n) in enumerate(ch):
                    rows = BLK // n
                    for i in range(nb):
                        pe.wait_ge(lo_done, b + i + 1 + RAW)
                        for kk in range(rows):
                            k = i * rows + kk
                            for t in range(T):
                                idx = T * c + t
                                if k == 0 and idx >= 6 and base is not None:
                                    pe.wait_ge(gm_ev, base + idx - 5)
                                mm = mm3(ps[:, idx % 6, 0:n], hT_hi[:, k, t * P:(t + 1) * P],
                                         hT_lo[:, k, t * P:(t + 1) * P], wblk(whi, b + i, n)[:, kk, :],
                                         wblk(wlo, b + i, n)[:, kk, :], k == 0, k == KD - 1)
                        mm.then_inc(pe_used, 1)

            def attention(lay):
                npair, u0, p0, m0 = (4, 0, 0, 0) if lay == 0 else (8, 24, 4, 12)
                proj = proj0 if lay == 0 else proj1

                def prep(i):
                    if lay == 1 or i % 2 == 0:
                        ki = i // 2 if lay == 0 else 2 + i
                        if ki:
                            pe.wait_ge(at_kT, ki)
                        for c in range(4):
                            if lay == 0:
                                src = kdup[:, c, P * ki:P * (ki + 1)]
                            else:
                                src = (ck1[:, P * i:P * (i + 1)], proj[:, 1, C_W + P * i:C_W + P * (i + 1)],
                                       proj[:, 2, C_W + P * i:C_W + P * (i + 1)],
                                       proj[:, 0, C_W + P * i:C_W + P * (i + 1)])[c]
                            mm = nc.tensor.transpose(ps[:, 4, c * P:(c + 1) * P], src, ident)
                        mm.then_inc(at_trk, 1)
                    if p0 + i:
                        pe.wait_ge(at_qT, p0 + i)
                    for t in range(T):
                        mm = nc.tensor.transpose(ps[:, 5, t * P:(t + 1) * P], proj[:, t, P * i:P * (i + 1)], ident)
                    mm.then_inc(at_trq, 1)

                def unit(n):
                    return n // 6, n % 6 // 2, n % 2

                def scores(n):
                    i, t, u = unit(n)
                    g = u0 + n
                    if n % 6 == 0:
                        pe.wait_ge(at_qT, p0 + i + 1)
                        pe.wait_ge(at_kT, i // 2 + 1 if lay == 0 else 2 + i + 1)
                    if g >= 2:
                        pe.wait_ge(at_sc, g - 1)
                    sl = (i // 2) % 2 if lay == 0 else i % 2
                    r = slice(DH * u, DH * (u + 1))
                    lo, hi = (3 * P, 4 * P) if t == 0 else (0, 3 * P)
                    nc.tensor.matmul(ps[:, g % 2, 0:hi - lo], qT[r, i % 2, t * P:(t + 1) * P], kT[r, sl, lo:hi],
                                     start=True, stop=True).then_inc(at_s, 1)

                def turn_p(n):
                    g = u0 + n
                    nk = 1 if unit(n)[1] == 0 else 3
                    pe.wait_ge(at_e, g + 1)
                    if g >= 2:
                        pe.wait_ge(at_ptev, g - 1)
                    for c in range(nk):
                        mm = nc.tensor.transpose(ps[:, 2 + g % 2, c * P:(c + 1) * P],
                                                 s_p[:, g % 2, c * P:(c + 1) * P], ident)
                    mm.then_inc(at_pt, 1)

                def values(n):
                    i, t, u = unit(n)
                    g, m = u0 + n, m0 + 3 * i + t
                    head = 2 * i + u
                    pe.wait_ge(at_ptev, g + 1)
                    if u == 0 and m >= 2:
                        pe.wait_ge(at_done, m - 1)
                    if lay == 0:
                        o = DH * (head // 4)
                        vs = [proj[:, 0, O_VA + o:O_VA + o + DH]] if t == 0 else \
                             [cv0[:, o:o + DH]] + [proj[:, c, O_VA + o:O_VA + o + DH] for c in (1, 2)]
                    else:
                        o = DH * head
                        vs = [proj[:, 0, 2 * C_W + o:2 * C_W + o + DH]] if t == 0 else \
                             [cv1[:, o:o + DH]] + [proj[:, c, 2 * C_W + o:2 * C_W + o + DH] for c in (1, 2)]
                    for c, v in enumerate(vs):
                        mm = nc.tensor.matmul(ps[:, 6 + m % 2, DH * u:DH * (u + 1)], s_pT[:, g % 2, c * P:(c + 1) * P],
                                              v, start=(c == 0), stop=(c == len(vs) - 1))
                    if u == 1:
                        mm.then_inc(at_o, 1)

                N = 6 * npair
                prep(0)
                for n in range(N + 2):
                    if n < N:
                        scores(n)
                    if 1 <= n <= N:
                        turn_p(n - 1)
                    if n >= 2:
                        values(n - 2)
                    if n % 6 == 3 and n // 6 + 1 < npair:
                        prep(n // 6 + 1)

            def retention():
                pe.wait_ge(at_done, 12)
                pe.wait_ge(kd_v, 4)
                for z, t in enumerate((0, 1, 0, 2)):
                    for head in range(8):
                        i, u = head // 2, head % 2
                        mm = nc.tensor.matmul(ps[DH * u:DH * (u + 1), z, i * DH:(i + 1) * DH],
                                              kd[:, z, head * DH:(head + 1) * DH],
                                              proj0[:, t, O_VR + head * DH:O_VR + (head + 1) * DH], start=True, stop=True)
                    mm.then_inc(u_ps, 1)

                def turn(i):
                    if i:
                        pe.wait_ge(r_q, 2 * i)
                        pe.wait_ge(r_qd, i)
                    for o, bank in ((O_QR, 0), (O_KR, 1)):
                        for t in range(T):
                            mm = nc.tensor.transpose(ps[:, bank, t * P:(t + 1) * P],
                                                     proj0[:, t, o + P * i:o + P * (i + 1)], ident)
                    mm.then_inc(r_tr, 1)

                def att(j):
                    i, u = j // 2, j % 2
                    r = slice(DH * u, DH * (u + 1))
                    if u == 0:
                        pe.wait_ge(r_q, 2 * (i + 1))
                    if j >= 2:
                        pe.wait_ge(r_at_v, j - 1)
                    for t in range(T):
                        mm = nc.tensor.matmul(ps[:, 2 + j % 2, t * P:(t + 1) * P], rkT[r, i % 2, t * P:(t + 1) * P],
                                              rqT[r, i % 2, t * P:(t + 1) * P], start=True, stop=True)
                    mm.then_inc(r_at_ps, 1)

                def out(j):
                    i, u = j // 2, j % 2
                    r = slice(DH * u, DH * (u + 1))
                    pe.wait_ge(r_at_v, j + 1)
                    if u == 0:
                        pe.wait_ge(r_qd, i + 1)
                    for t in range(T):
                        o = ps[:, 5 + t, DH * j:DH * (j + 1)]
                        mm = nc.tensor.matmul(o, rat[:, j % 2, t * P:(t + 1) * P],
                                              proj0[:, t, O_VR + DH * j:O_VR + DH * (j + 1)], start=True, stop=(t == 0))
                        if t:
                            sf, sb_ = (S0, SS) if t == 1 else (SS, S0)
                            c = (t - 1) * P
                            if t == 1 and j:
                                pe.wait_ge(r_o, j)
                            nc.tensor.matmul(o, rqd[r, i % 2, 0, c:c + P], sf[r, 0, i, :], start=False, stop=False)
                            mm = nc.tensor.matmul(o, rqd[r, i % 2, 1, c:c + P], sb_[r, 1, i, :], start=False, stop=True)
                    mm.then_inc(r_o, 1)

                pe.wait_ge(up_ev, 2)
                pe.wait_ge(ss_v, 2)
                turn(0)
                for j in range(9):
                    if j < 8:
                        att(j)
                        if j % 2 == 1 and j < 7:
                            turn(j // 2 + 1)
                    if j >= 1:
                        out(j - 1)

            def feed(nt, b0, n0, u, between=None):
                def at(v):
                    return v if u is None else u * (T * NS) + v

                def inc(t):
                    return 1 if t < nt - 1 else T - nt + 1

                def begin(b):
                    if between is not None:
                        between(b)
                    if b in TURN:
                        turn(TURN[b])
                    pe.wait_ge(lo_done, b0 + b + 1 + RAW if n0 is None else n0 + (b + 1 + RAW))

                def turn(s):
                    for t in range(nt):
                        q = s * nt + t
                        pe.wait_ge(gu_v, at(T * s + t + 1))
                        if q < 2 and between is not None:
                            pe.wait_ge(sc_v, (u - 1) * 18 + 6)
                        if q >= 2:
                            ls, lt = divmod(q - 2, nt)
                            pe.wait_ge(ft_lo, at(T * ls + lt + 1))
                        for c in range(WIDTH[s] // P):
                            mm = nc.tensor.transpose(ps[:, 6 + q % 2, c * P:(c + 1) * P], sg[:, t, c * P:(c + 1) * P], ident)
                        mm.then_inc(ft_ps, inc(t))

                for s, g, j, nb, o, n in FF_PH:
                    rows = BLK // n
                    for i in range(nb):
                        begin(j + i)
                        for kk in range(rows):
                            k = i * rows + kk
                            for t in range(nt):
                                if k == 0 and s:
                                    pe.wait_ge(gu_v if g else sg_a, at(T * (s - 1) + t + 1))
                                mm = mm3(ps[:, nt * g + t, 0:n], hT_hi[:, k, t * P:(t + 1) * P],
                                         hT_lo[:, k, t * P:(t + 1) * P], wblk(whi, b0 + j + i, n)[:, kk, :],
                                         wblk(wlo, b0 + j + i, n)[:, kk, :], k == 0, k == KD - 1)
                        mm.then_inc(pe_used, 1)
                for j in range(DB):
                    begin(GB + j)
                    w_hi, w_lo = (wblk(w, b0 + GB + j, 512) for w in (whi, wlo))
                    for t in range(nt):
                        if j == 0:
                            if nt == T:
                                pe.wait_ge(gu_v, at(T * NS))
                            pe.wait_ge(sg_a, at(T * NS))
                        if j % 4 == 0:
                            pe.wait_ge(ft_lo, at(T * (j // 4) + t + 1))
                        for half in range(2):
                            mm = mm3(ps[:, down_bank(nt, t) + half, :], fT_hi[:, j, t * P:(t + 1) * P],
                                     fT_lo[:, j, t * P:(t + 1) * P], w_hi[:, half, :], w_lo[:, half, :],
                                     j == 0, j == DB - 1)
                    mm.then_inc(pe_used, 1)

            def gather(t, half):
                for c in range(4):
                    k = 4 * half + c
                    for m in range(T):
                        mm = nc.tensor.matmul(ps[:, 6 + half, c * P:(c + 1) * P], h[:, m, k * P:(k + 1) * P],
                                              oh[:, m, t * P:(t + 1) * P], start=(m == 0), stop=(m == T - 1))
                return mm

            def scatter(i, m, half):
                o = ps[:, 6 + half, :]
                yc = slice(512 * half, 512 * (half + 1))
                nc.tensor.matmul(o, turned(i)[:, m * P:(m + 1) * P], y_of(fT_hi, i)[:, yc], start=True, stop=False)
                return nc.tensor.matmul(o, turned(i)[:, m * P:(m + 1) * P], y_of(fT_lo, i)[:, yc], start=False, stop=True)

            def scatter_last(nt, e, i):
                if i == 0:
                    pe.wait_ge(y_lo, y_at(nt, e, -1))
                pe.wait_ge(sc_v, e * 18 + max(i - 1, 0))
                scatter(0, i // 2, i % 2).then_inc(sc_ps, sc_inc(nt, i))

            def expert(nt, e):
                if nt > 1:
                    pe.wait_ge(sc_v, e * 18)
                for i in range(2 * (nt - 1)):
                    pe.wait_ge(ga_lo, e * 6 + (i + 1))
                    gather(1 + i // 2, i % 2).then_inc(ga_ps, 1)
                pe.wait_ge(ga_lo, e * 6 + 2 * nt)

                def between(b):
                    if b in SCATTER:
                        scatter_last(nt, e, SCATTER[b])
                    t = OH_TURN.get(b, nt)
                    if t < nt:
                        pe.wait_ge(ft_lo, (e + 1) * (T * NS) + T * NS)
                        if t > 1:
                            pe.wait_ge(oht_ev, e * T + (t - 1))
                        for m in range(T):
                            mm = nc.tensor.transpose(ps[:, 6 + t % 2, m * P:(m + 1) * P], oh[:, m, t * P:(t + 1) * P], ident)
                        mm.then_inc(oht_ps, 1 if t < nt - 1 else T - nt + 1)
                    if b in GATHER:
                        pe.wait_ge(oht_ev, e * T + T)
                        pe.wait_ge(oh_v, e + 2)
                        gather(0, GATHER[b]).then_inc(ga_ps, ga_inc(nt, GATHER[b]))

                feed(nt, B_MOE, e * EB + B_MOE, e + 1, between)
                for t in range(nt - 1):
                    pe.wait_ge(y_lo, y_at(nt, e, t))
                    for m in range(T):
                        for half in range(2):
                            i = 6 + 6 * t + 2 * m + half
                            if i < 8:
                                pe.wait_ge(ga_lo, e * 6 + (7 + half))
                            else:
                                pe.wait_ge(sc_v, e * 18 + (i - 1))
                            scatter(nt - 1 - t, m, half).then_inc(sc_ps, sc_inc(nt, i))

            pe.wait_ge(crow_in, 32)
            pe.wait_ge(keep_in, 16)
            nc.tensor.transpose(ps[:, 6, 0:16], crow[:, :], ident[0:16, 0:16]).then_inc(cc_t, 1)
            pe.wait_ge(cs_lo, 1)
            with pe.Fori(0, MOD_CH // MOD_STEP) as it:
                for c in range(MOD_STEP):
                    for i in range(SB):
                        j = c * SB + i
                        pe.wait_ge(lo_done, it * (MOD_STEP * SB) + (j + 1 + RAW))
                        if i == 0:
                            pe.wait_ge(mod_ev, it * MOD_STEP + (c + 1))
                        for kk in range(2):
                            k = 2 * i + kk
                            nc.tensor.matmul(ps[:, c, :], cs4[:, k, :], wblk(whi, j, 512)[:, kk, :],
                                             start=(k == 0), stop=False)
                            mm = nc.tensor.matmul(ps[:, c, :], cs4[:, k, :], wblk(wlo, j, 512)[:, kk, :],
                                                  start=False, stop=(k == KD - 1))
                        mm.then_inc(pe_used, 1)
            pe.wait_ge(mod_ev, MOD_CH + MOD_STEP)
            pe.wait_ge(ones_in, 48)
            norm(0, 0)
            dense(IN_CH, 0)
            pe.wait_ge(gm_ev, GM_DONE[1])
            pe.wait_ge(rope_done, 2)
            pe.wait_ge(kdup_v, 4)
            pe.wait_ge(kv_in, 48)
            attention(0)
            retention()
            pe.wait_ge(at_done, 12)
            turn_in(1, lambda t, k: proj0[:, t, P * k:P * (k + 1)] if k < 4 else
                    proj0[:, t, O_QR + P * (k - 4):O_QR + P * (k - 3)], lambda t: pe.wait_ge(mix_done, t + 1))
            pe.wait_ge(tin_lo, 12)
            dense(OUT_CH[0], None)
            norm(1, 2)
            feed(T, B_FFN, None, None)
            norm(2, 3)
            dense(QKV_CH, GM_DONE[1])
            pe.wait_ge(gm_ev, GM_DONE[1] + T * len(QKV_CH))
            pe.wait_ge(c1_in, 32)
            attention(1)
            turn_in(4, lambda t, k: proj1[:, t, P * k:P * (k + 1)], lambda t: pe.wait_ge(at_done, 36))
            pe.wait_ge(tin_lo, 30)
            dense(OUT_CH[1], None)
            norm(3, 5)
            pe.wait_ge(wr_v, 2)
            for t in range(T):
                for k in range(KD):
                    mm = mm3(ps[:, t, 0:E], hT_hi[:, k, t * P:(t + 1) * P], hT_lo[:, k, t * P:(t + 1) * P],
                             wr_hi[:, k, :], wr_lo[:, k, :], k == 0, k == KD - 1)
                mm.then_inc(lo_ps, 1)
            pe.wait_ge(rt_v, 2)
            for t in range(T):
                for m in range(t + 1):
                    mm = nc.tensor.matmul(ps[:, 3 + t, 0:E], cst("before") if m == t else cst("ones"), msk[:, m, :],
                                          start=(m == 0), stop=(m == t))
            for m in range(T):
                mm = nc.tensor.matmul(ps[:, 6, 0:E], cst("ones"), msk[:, m, :], start=(m == 0), stop=(m == T - 1))
            mm.then_inc(pos_ps, 1)
            pe.wait_ge(routed, 1)
            pe.wait_ge(oh_v, 1)
            for half in range(2):
                gather(0, half).then_inc(ga_ps, 1)
            with pe.Fori(0, E) as e:
                n_tok = pe.value_load(counts[0:1, bass.ds(e, 1)], min_val=0, max_val=T * P)
                with pe.If(n_tok < P + 1):
                    expert(1, e)
                with pe.Else():
                    with pe.If(n_tok < 2 * P + 1):
                        expert(2, e)
                    with pe.Else():
                        expert(3, e)
                    pe.nop()
            for i in range(6):
                scatter_last(T, E, i)

        @block.scalar
        def _(act):
            chain = Chain(act, ach)

            def norm_stats(n):
                for t in range(T):
                    if n == 0 and t == 0:
                        act.wait_ge(x_in, 32)
                    elif n < 4 and t == 0:
                        act.wait_ge(x_upd, 6 * n)
                    elif n == 4:
                        act.wait_ge(x_upd, 18 + t + 1)
                    nc.scalar.activation(h[:, t, :], x[:, t, :], ACT.Square, accum_out=st[:, t:t + 1]).then_inc(nsq, 1)
                act.wait_ge(nms, n + 1)
                nc.scalar.activation(st[:, 6:9], st[:, 3:6], ACT.Sqrt).then_inc(nsd, 1)

            def turn_in(n):
                for t in range(T):
                    for kh in range(2):
                        act.wait_ge(tin_ps, 6 * n + 2 * t + kh + 1)
                        nc.scalar.activation(hT_hi[:, 4 * kh:4 * kh + 4, t * P:(t + 1) * P],
                                             ps[:, (2 * t) % 4 + kh, :].rearrange("p (k n) -> p k n", n=P), ACT.Copy)\
                            .then_inc(tin_hi, 1)

            def norm(n, turn):
                norm_stats(n)
                turn_in(turn)
                act.wait_ge(gate_ps, n + 1)
                nc.scalar.activation(gate[:, :, :], ps[:, 4:8, :].rearrange("p (a b) n -> p a (b n)", a=2), ACT.Copy)\
                    .then_inc(gate_ev, 1)

            def dense(ch, base, proj, extra=None):
                for c, (b, nb, o, n) in enumerate(ch):
                    ahead.to(min(b + nb + HL, B_MOE))
                    if proj is None:
                        continue
                    for t in range(T):
                        idx = T * c + t
                        act.wait_ge(pe_used, b + nb + HL)
                        nc.scalar.activation(proj[:, t, o:o + n], ps[:, idx % 6, 0:n], ACT.Copy).then_inc(gm_ev, 1)
                    if extra is not None and c == 1:
                        extra()

            def tables():
                act.wait_ge(tb_v, 1)
                chain(nc.scalar.activation(lgt[:, :, :], lgt[:, :, :], ACT.Exp, scale=-1.0))
                nc.scalar.activation(lgt[:, :, :], lgt[:, :, :], ACT.Ln, bias=1.0).then_inc(tb_a, 1)
                act.wait_ge(tb_v, 2)
                for hd in range(8):
                    nc.scalar.activation(dm[:, hd, :], cst("ahead"), ACT.Exp, scale=logd[:, 1, hd:hd + 1])
                    nc.scalar.activation(dm2[:, hd, :], cst("behind"), ACT.Exp, scale=logd[:, 2, hd:hd + 1])
                for d in range(2):
                    for i in range(4):
                        nc.scalar.activation(dq[:, d, i, :], cst("decay_at")[:, d * P:(d + 1) * P], ACT.Exp,
                                             scale=logd[:, 0, 4 * d + i:4 * d + i + 1])
                nc.scalar.activation(cdec[:, :, :], logd[:, 0, :].rearrange("p (a b) -> p a b", a=2), ACT.Exp,
                                     scale=float(P))
                nc.scalar.activation(kdec[:, :, :], kdec[:, :, :], ACT.Exp).then_inc(tb_a, 1)

            def attention(lay):
                npair, u0, p0, m0 = (4, 0, 0, 0) if lay == 0 else (8, 24, 4, 12)

                def prep(i):
                    if lay == 1 or i % 2 == 0:
                        ki = i // 2 if lay == 0 else 2 + i
                        sl = ki % 2 if lay == 0 else i % 2
                        act.wait_ge(at_trk, ki + 1)
                        nc.scalar.activation(kT[:, sl, :], ps[:, 4, :], ACT.Copy).then_inc(at_kT, 1)
                    act.wait_ge(at_trq, p0 + i + 1)
                    nc.scalar.activation(qT[:, i % 2, :], ps[:, 5, 0:T * P], ACT.Copy).then_inc(at_qT, 1)

                def exps(n):
                    t, u, g = n % 6 // 2, n % 2, u0 + n
                    m = m0 + n // 2
                    w = P if t == 0 else 3 * P
                    act.wait_ge(at_m, g + 1)
                    if g >= 2:
                        act.wait_ge(at_pt, g - 1)
                    if u == 0 and m >= 2:
                        act.wait_ge(at_done, m - 1)
                    nc.scalar.activation(s_p[:, g % 2, 0:w], s_sc[:, g % 2, 0:w], ACT.Exp, bias=a_neg[:, m % 2, u:u + 1],
                                         accum_out=a_sum[:, m % 2, u:u + 1]).then_inc(at_e, 1)

                def evac(n):
                    g = u0 + n
                    w = P if n % 6 // 2 == 0 else 3 * P
                    act.wait_ge(at_pt, g + 1)
                    nc.scalar.activation(s_pT[:, g % 2, 0:w], ps[:, 2 + g % 2, 0:w], ACT.Copy).then_inc(at_ptev, 1)

                N = 6 * npair
                prep(0)
                for n in range(N + 1):
                    if n < N:
                        exps(n)
                        if lay == 0 and n % 2 == 1:
                            m = n // 2
                            act.wait_ge(at_zs, m + 1)
                            nc.scalar.activation(a_es[:, m % 2, :], a_es[:, m % 2, :], ACT.Exp).then_inc(at_es, 1)
                    if n >= 1:
                        evac(n - 1)
                    if n % 6 == 3 and n // 6 + 1 < npair:
                        prep(n // 6 + 1)

            def retention():
                act.wait_ge(u_ps, 3)
                for d, z in ((0, 0), (1, 2)):
                    nc.scalar.activation(up[:, d, :, :], ps[:, z, 0:4 * DH].rearrange("p (a b) -> p a b", b=DH), ACT.Copy)\
                        .then_inc(up_ev, 1)
                for i in range(4):
                    act.wait_ge(r_tr, i + 1)
                    nc.scalar.activation(rqT[:, i % 2, :], ps[:, 0, 0:T * P], ACT.Copy).then_inc(r_q, 1)
                    nc.scalar.activation(rkT[:, i % 2, :], ps[:, 1, 0:T * P], ACT.Copy, scale=SCALE).then_inc(r_q, 1)
                for t in range(T):
                    nc.scalar.activation(proj0[:, t, O_GR:], proj0[:, t, O_GR:], ACT.Silu).then_inc(gn_a, 1)
                act.wait_ge(gn_v, 1)
                nc.scalar.activation(gst[:, 2, :, :], gst[:, 1, :, :], ACT.Sqrt).then_inc(gn_a, 1)

            def feed(nt, b0, n0, u, conv, between=None):
                def at(v):
                    return v if u is None else u * (T * NS) + v

                def inc(t):
                    return 1 if t < nt - 1 else T - nt + 1

                for b in range(EB):
                    conv(b + HL)
                    if b in TURN:
                        s, n = TURN[b], WIDTH[TURN[b]]
                        for t in range(nt):
                            act.wait_ge(ft_ps, at(T * s + t + 1))
                            nc.scalar.activation(fT_hi[:, 4 * s:4 * s + n // P, t * P:(t + 1) * P],
                                                 ps[:, 6 + (s * nt + t) % 2, 0:n].rearrange("p (c m) -> p c m", m=P),
                                                 ACT.Copy).then_inc(ft_hi, inc(t))
                    if b in G_END:
                        s, n = G_END[b], WIDTH[G_END[b]]
                        act.wait_ge(pe_used, b0 + b + HL if n0 is None else n0 + (b + HL))
                        for t in range(nt):
                            nc.scalar.activation(sg[:, t, 0:n], ps[:, t, 0:n], ACT.Silu).then_inc(sg_a, inc(t))
                    if between is not None:
                        between(b)

            def loop_conv(e):
                done = [HL]

                def to(end, next_too=False):
                    while done[0] < (end if next_too else min(end, EB)):
                        j = done[0]
                        conv_hi(act, B_MOE + j, e * EB + (B_MOE + j),
                                (e * (EB // RAW) + (BEFORE[j % RAW] + j // RAW + 1)) * 16)
                        done[0] += 1
                return to

            def gathered(t, half, n, inc):
                act.wait_ge(ga_ps, n)
                nc.scalar.activation(hT_hi[:, 4 * half:4 * half + 4, t * P:(t + 1) * P],
                                     ps[:, 6 + half, :].rearrange("p (k n) -> p k n", n=P), ACT.Copy).then_inc(ga_hi, inc)

            def take_y(nt, e, t):
                own = t >= 0
                act.wait_ge(pe_used, e * EB + (B_MOE + HL + (EB if own else 0)))
                b = down_bank(nt, t) if own else 4
                nc.scalar.activation(y_of(fT_hi, nt - 1 - t if own else 0),
                                     ps[:, b:b + 2, :].rearrange("p a n -> p (a n)"), ACT.Copy)\
                    .then_inc(y_hi, 1 if own else T + 1 - nt)

            def expert(nt, e):
                conv = loop_conv(e)
                for i in range(2 * (nt - 1)):
                    gathered(1 + i // 2, i % 2, e * 6 + (i + 3), 1)

                def between(b):
                    if b == Y_LAST:
                        take_y(nt, e, -1)
                    t = OH_TURN.get(b, nt)
                    if t < nt:
                        act.wait_ge(oht_ps, e * T + (t + 1))
                        nc.scalar.activation(turned(nt - 1 - t), ps[:, 6 + t % 2, 0:T * P], ACT.Copy)\
                            .then_inc(oht_ev, 1 if t < nt - 1 else T - nt + 1)
                    if b in GATHER:
                        half = GATHER[b]
                        gathered(0, half, e * 6 + (7 + half), ga_inc(nt, half))

                feed(nt, B_MOE, e * EB + B_MOE, e + 1, conv, between)
                for t in range(nt - 1):
                    take_y(nt, e, t)
                with act.If(e < E - 1):
                    conv(EB + HL, next_too=True)

            act.wait_ge(cc_t, 1)
            nc.scalar.activation(ccol[:, :], ps[:, 6, 0:16], ACT.Silu).then_inc(cc_silu, 1)
            act.wait_ge(cc_silu, 1)
            act.wait_ge(cs_zero, 1)
            nc.scalar.activation(cs4[:, :, 0:2], ccol[:, :].rearrange("p (a k) -> p k a", a=2), ACT.Copy).then_inc(cs_hi, 1)
            with act.Fori(0, MOD_CH // MOD_STEP) as it:
                def conv(j):
                    conv_hi(act, j, it * (MOD_STEP * SB) + j, (it * (MOD_STEP * SB // RAW) + (j // RAW + 1)) * 16)

                j = 0
                for c in range(MOD_STEP):
                    while j < min((c + 1) * SB + HL, MOD_STEP * SB):
                        conv(j)
                        j += 1
                    act.wait_ge(pe_used, it * (MOD_STEP * SB) + ((c + 1) * SB + HL))
                    if c == 0:
                        act.wait_ge(mst_free, it + 1)
                    nc.scalar.activation(mst[:, c, :], ps[0:4, c, :], ACT.Copy).then_inc(mod_ev, 1)
            ahead = Ahead(act, conv_hi, B_IN)
            norm(0, 0)
            dense(IN_CH, 0, proj0, tables)
            attention(0)
            retention()
            turn_in(1)
            dense(OUT_CH[0], None, None)
            norm(1, 2)
            act.wait_ge(stored, 16 * 6)
            feed(T, B_FFN, None, None, lambda end: ahead.to(min(B_FFN + end, B_MOE)))
            ahead.to(B_QKV + HL)
            norm(2, 3)
            dense(QKV_CH, GM_DONE[1], proj1)
            attention(1)
            turn_in(4)
            dense(OUT_CH[1], None, None)
            norm(3, 5)
            act.wait_ge(wr_in, 16)
            nc.scalar.activation(wr_hi[:, :, :], wr[:, :, :], ACT.Copy).then_inc(wr_v, 1)
            act.wait_ge(rt_v, 1)
            nc.scalar.activation(rt[:, 1, :], rt[:, 0, :], ACT.Exp).then_inc(rt_a, 1)
            act.wait_ge(pe_used, B_MOE + HL)
            for j in range(HL):
                conv_hi(act, B_MOE + j, None, (BEFORE[j] + 1) * 16)
            act.wait_ge(routed, 1)
            for half in range(2):
                gathered(0, half, half + 1, 1)
            with act.Fori(0, E) as e:
                n_tok = act.value_load(counts[0:1, bass.ds(e, 1)], min_val=0, max_val=T * P)
                with act.If(n_tok < P + 1):
                    expert(1, e)
                with act.Else():
                    with act.If(n_tok < 2 * P + 1):
                        expert(2, e)
                    with act.Else():
                        expert(3, e)
                    act.nop()
            take_y(T, E, -1)
            norm_stats(4)

        @block.vector
        def _(dve):
            chain = Chain(dve, dch)

            def norm_rows(n):
                dve.wait_ge(nsq, T * (n + 1))
                nc.vector.tensor_scalar(st[:, 3:6], st[:, 0:3], 1.0 / D, EPS, ALU.mult, ALU.add).then_inc(nms, 1)
                dve.wait_ge(nsd, n + 1)
                chain(nc.vector.reciprocal(st[:, 9:12], st[:, 6:9]))
                dve.wait_ge(g_in, 16 * (n + 1))
                for t in range(T):
                    ins = nc.vector.scalar_tensor_tensor(out=h[:, t, :], in0=x[:, t, :], scalar=st[:, 9 + t:10 + t],
                                                         in1=gbc[:, :], op0=ALU.mult, op1=ALU.mult)
                    if n == 4:
                        ins.then_inc(h_rows, 1)
                        continue
                    chain(ins)
                    kind = min(t, 1)
                    dve.wait_ge(bc_ps, 2 * n + kind + 1)
                    chain(nc.vector.tensor_tensor(h[:, t, :], h[:, t, :], ps[:, 4 * kind:4 * kind + 2, :]
                                                  .rearrange("p a n -> p (a n)"), ALU.mult))
                    nc.vector.tensor_tensor(h[:, t, :], h[:, t, :], ps[:, 4 * kind + 2:4 * kind + 4, :]
                                            .rearrange("p a n -> p (a n)"), ALU.add).then_inc(h_rows, 1)

            def turn_in(n):
                for t in range(T):
                    for kh in range(2):
                        dve.wait_ge(tin_hi, 6 * n + 2 * t + kh + 1)
                        sl = (slice(None), slice(4 * kh, 4 * kh + 4), slice(t * P, (t + 1) * P))
                        nc.vector.tensor_tensor(hT_lo[sl], ps[:, (2 * t) % 4 + kh, :].rearrange("p (k n) -> p k n", n=P),
                                                hT_hi[sl].bitcast(F32), ALU.subtract).then_inc(tin_lo, 1)

            def norm(n, turn):
                norm_rows(n)
                turn_in(turn)

            def dense(ch, extra=None):
                for c, (b, nb, o, n) in enumerate(ch):
                    ahead.to(min(b + nb + HL, B_MOE))
                    if extra is not None and c == 1:
                        extra()

            def residual(ch, n):
                dve.wait_ge(gate_ev, n + 1)
                for c, (b, nb, o, w) in enumerate(ch):
                    for t in range(T):
                        idx = T * c + t
                        dve.wait_ge(pe_used, b + nb + HL)
                        add_to_x(t, slice(o, o + w), ps[:, idx, 0:w])

            def add_to_x(t, cols, src):
                chain(nc.vector.tensor_tensor(tmp_w[:, t, cols], src, gate[:, min(t, 1), cols], ALU.mult))
                nc.vector.tensor_tensor(x[:, t, cols], x[:, t, cols], tmp_w[:, t, cols], ALU.add).then_inc(x_upd, 1)

            def tables():
                dve.wait_ge(lg_in, 96)
                dve.wait_ge(more_in, 16)
                nc.vector.scalar_tensor_tensor(out=lgt[:, :, :], in0=lg[:, :, :], scalar=-1.0, in1=lg[:, :, :],
                                               op0=ALU.mult, op1=ALU.max).then_inc(tb_v, 1)
                chain(nc.vector.tensor_scalar(logd[:, :, :], lg[:, :, :], 0.0, None, ALU.min))
                dve.wait_ge(tb_a, 1)
                chain(nc.vector.tensor_tensor(logd[:, :, :], logd[:, :, :], lgt[:, :, :], ALU.subtract))
                for d in range(2):
                    ins = nc.vector.tensor_scalar(kdec[:, d, :], logd[:, 1 + d, :], cst("kcol")[:, d:d + 1], None, ALU.mult)
                ins.then_inc(tb_v, 1)
                dve.wait_ge(tb_a, 2)

                def over_heads(name):
                    return cst(name).unsqueeze(1).to_broadcast([P, B_HEADS, P])

                chain(nc.vector.tensor_tensor(dm[:, :, :], dm[:, :, :], over_heads("is_ahead"), ALU.mult))
                chain(nc.vector.tensor_tensor(dm2[:, :, :], dm2[:, :, :], over_heads("is_behind"), ALU.mult))
                chain(nc.vector.tensor_tensor(dm[:, :, :], dm[:, :, :], dm2[:, :, :], ALU.add))
                chain(nc.vector.tensor_scalar(kdec[:, :, :], kdec[:, :, :], SCALE, None, ALU.mult))
                dve.wait_ge(kv_in, 48)
                chain(nc.vector.tensor_scalar(sinks[:, 1, :], sinks[:, 0, :], -1.0, None, ALU.mult))

            def rotary():
                dve.wait_ge(gm_ev, GM_DONE[1])
                nh = (A_Q + A_KV) // DH
                for t in (1, 2):
                    v = proj0[:, t, 0:nh * DH].rearrange("p (n d) -> p n d", d=DH)
                    cos = cst("ropec").rearrange("p (t d) -> p t d", t=2)[:, t - 1].unsqueeze(1).to_broadcast([P, nh, DH])
                    chain(nc.vector.tensor_tensor(rot[:, 0, :].rearrange("p (n d) -> p n d", d=DH), v, cos, ALU.mult))
                    v4 = proj0[:, t, 0:nh * DH].rearrange("p (n a b) -> p n a b", a=4, b=DH // 4)
                    r4 = rot[:, 1, :].rearrange("p (n a b) -> p n a b", a=4, b=DH // 4)
                    s4 = cst("ropes").rearrange("p (t a b) -> p t a b", t=2, a=4)[:, t - 1]
                    for q in range(2):
                        sn = s4[:, q::2, :].unsqueeze(1).to_broadcast([P, nh, 2, DH // 4])
                        chain(nc.vector.tensor_tensor(r4[:, :, q::2, :], v4[:, :, 1 - q::2, :], sn, ALU.mult))
                    nc.vector.tensor_tensor(proj0[:, t, 0:nh * DH], rot[:, 0, :], rot[:, 1, :], ALU.add).then_inc(rope_done, 1)
                    dve.wait_ge(rope_done, t)
                for c, src in enumerate((ck0[:, :], proj0[:, 1, O_KA:O_VA], proj0[:, 2, O_KA:O_VA], proj0[:, 0, O_KA:O_VA])):
                    s3 = src.rearrange("p (g d) -> p g d", g=2)
                    nc.vector.tensor_copy(kdup[:, c, :].rearrange("p (g u d) -> p g u d", g=2, u=2),
                                          s3.unsqueeze(2).to_broadcast([P, 2, 2, DH])).then_inc(kdup_v, 1)

            def attention(lay):
                npair, u0, m0 = (4, 0, 0) if lay == 0 else (8, 24, 12)
                proj = proj0 if lay == 0 else proj1

                def scaled(n):
                    i, t, u = n // 6, n % 6 // 2, n % 2
                    g, m = u0 + n, m0 + n // 2
                    w = P if t == 0 else 3 * P
                    dve.wait_ge(at_s, g + 1)
                    if g >= 2:
                        dve.wait_ge(at_e, g - 1)
                    if t == 0:
                        nc.vector.tensor_scalar(s_sc[:, g % 2, 0:w], ps[:, g % 2, 0:w], SCALE, None, ALU.mult)\
                            .then_inc(at_sc, 1)
                    else:
                        if lay == 1 and t == 1 and u == 0:
                            dve.wait_ge(bm_ok, i + 1)
                        mask = cst("mask0").rearrange("p (t n) -> p t n", t=2)[:, t - 1] if lay == 0 else \
                            bm[:, i % 2, t - 1, u, :]
                        nc.vector.scalar_tensor_tensor(out=s_sc[:, g % 2, :], in0=ps[:, g % 2, 0:w], scalar=SCALE,
                                                       in1=mask, op0=ALU.mult, op1=ALU.add).then_inc(at_sc, 1)
                    dve.wait_ge(at_sc, g + 1)
                    ins = nc.vector.reduce_max(a_neg[:, m % 2, u:u + 1], s_sc[:, g % 2, 0:w], AX, negate=True)
                    if lay == 0:
                        chain(ins)
                        hd = 2 * i + u
                        ins = nc.vector.tensor_tensor(a_neg[:, m % 2, u:u + 1], a_neg[:, m % 2, u:u + 1],
                                                      sinks[:, 1, hd:hd + 1], ALU.min)
                    ins.then_inc(at_m, 1)
                    if lay == 0 and u == 1:
                        dve.wait_ge(at_m, g + 1)
                        nc.vector.tensor_tensor(a_es[:, m % 2, :], a_neg[:, m % 2, :], sinks[:, 0, 2 * i:2 * i + 2],
                                                ALU.add).then_inc(at_zs, 1)

                def finish(k):
                    i, t, m = k // 3, k % 3, m0 + k
                    tot = a_sum[:, m % 2, :]
                    if lay == 0:
                        dve.wait_ge(at_es, k + 1)
                        chain(nc.vector.tensor_tensor(a_rec[:, m % 2, :], tot, a_es[:, m % 2, :], ALU.add))
                        tot = a_rec[:, m % 2, :]
                    dve.wait_ge(at_o, m + 1)
                    chain(nc.vector.reciprocal(a_rec[:, m % 2, :], tot))
                    nc.vector.tensor_tensor(proj[:, t, P * i:P * (i + 1)].rearrange("p (u d) -> p u d", u=2),
                                            ps[:, 6 + m % 2, 0:P].rearrange("p (u d) -> p u d", u=2),
                                            a_rec[:, m % 2, :].unsqueeze(2).to_broadcast([P, 2, DH]), ALU.mult)\
                        .then_inc(at_done, 1)

                N = 6 * npair
                for n in range(N + 2):
                    if n < N:
                        scaled(n)
                    if n % 2 == 1 and n >= 3:
                        finish((n - 3) // 2)

            def retention():
                for z, (d, t) in enumerate(((0, 0), (0, 1), (1, 0), (1, 2))):
                    nc.vector.tensor_tensor(kd[:, z, :].rearrange("p (n d) -> p n d", d=DH),
                                            proj0[:, t, O_KR:O_VR].rearrange("p (n d) -> p n d", d=DH),
                                            kdec[:, d, :].unsqueeze(2).to_broadcast([P, 8, DH]), ALU.mult).then_inc(kd_v, 1)
                dve.wait_ge(s0_in, 64)
                chain(nc.vector.tensor_tensor(SS[:, :, :, :].rearrange("p a b d -> p (a b) d"),
                                              S0[:, :, :, :].rearrange("p a b d -> p (a b) d"),
                                              cdec[:, :, :].rearrange("p a b -> p (a b)").unsqueeze(2)
                                              .to_broadcast([P, 8, DH]), ALU.mult))
                dve.wait_ge(u_ps, 4)
                for d, z in ((0, 1), (1, 3)):
                    nc.vector.tensor_tensor(SS[:, d, :, :], SS[:, d, :, :],
                                            ps[:, z, 0:4 * DH].rearrange("p (a b) -> p a b", b=DH), ALU.add).then_inc(ss_v, 1)

                def queries(i):
                    dve.wait_ge(r_q, 2 * i + 2)
                    for d in range(2):
                        ins = nc.vector.tensor_tensor(rqd[:, i % 2, d, :].rearrange("p (t n) -> p t n", t=2),
                                                      ps[:, 0, P:3 * P].rearrange("p (t n) -> p t n", t=2),
                                                      dq[:, d, i, :].unsqueeze(1).to_broadcast([P, 2, P]), ALU.mult)
                    ins.then_inc(r_qd, 1)

                queries(0)
                for j in range(8):
                    dve.wait_ge(r_at_ps, j + 1)
                    nc.vector.tensor_tensor(rat[:, j % 2, :].rearrange("p (t n) -> p t n", t=T),
                                            ps[:, 2 + j % 2, 0:T * P].rearrange("p (t n) -> p t n", t=T),
                                            dm[:, j, :].unsqueeze(1).to_broadcast([P, T, P]), ALU.mult).then_inc(r_at_v, 1)
                    if j % 2 == 1 and j < 7:
                        queries(j // 2 + 1)
                dve.wait_ge(r_o, 8)

                def heads(ap):
                    return ap.rearrange("p (n d) -> p n d", d=DH)

                for t in range(T):
                    chain(nc.vector.tensor_reduce(gst[:, 0, t, :], heads(ps[:, 5 + t, :]), AX, ALU.add))
                chain(nc.vector.tensor_scalar(gst[:, 0, :, :], gst[:, 0, :, :], 1.0 / DH, None, ALU.mult))
                for t in range(T):
                    mean = gst[:, 0, t, :].unsqueeze(2).to_broadcast([P, 8, DH])
                    chain(nc.vector.tensor_tensor(heads(gn[:, t, :]), heads(ps[:, 5 + t, :]), mean, ALU.subtract))
                chain(nc.vector.tensor_tensor(gn2[:, :, :], gn[:, :, :], gn[:, :, :], ALU.mult))
                for t in range(T):
                    chain(nc.vector.tensor_reduce(gst[:, 1, t, :], heads(gn2[:, t, :]), AX, ALU.add))
                nc.vector.tensor_scalar(gst[:, 1, :, :], gst[:, 1, :, :], 1.0 / DH, EPS, ALU.mult, ALU.add).then_inc(gn_v, 1)
                dve.wait_ge(gn_a, 4)
                chain(nc.vector.reciprocal(gst[:, 3, :, :], gst[:, 2, :, :]))
                for t in range(T):
                    rs = gst[:, 3, t, :].unsqueeze(2).to_broadcast([P, 8, DH])
                    chain(nc.vector.tensor_tensor(heads(gn[:, t, :]), heads(gn[:, t, :]), rs, ALU.mult))
                    nc.vector.tensor_tensor(proj0[:, t, O_QR:O_KR], gn[:, t, :], proj0[:, t, O_GR:], ALU.mult)\
                        .then_inc(mix_done, 1)

            def feed(nt, n0, u, conv, between=None):
                def at(v):
                    return v if u is None else u * (T * NS) + v

                def inc(t):
                    return 1 if t < nt - 1 else T - nt + 1

                for b in range(EB):
                    conv(b + HL)
                    if b in TURN:
                        s, n = TURN[b], WIDTH[TURN[b]]
                        for t in range(nt):
                            dve.wait_ge(ft_hi, at(T * s + t + 1))
                            sl = (slice(None), slice(4 * s, 4 * s + n // P), slice(t * P, (t + 1) * P))
                            nc.vector.tensor_tensor(fT_lo[sl], ps[:, 6 + (s * nt + t) % 2, 0:n]
                                                    .rearrange("p (c m) -> p c m", m=P), fT_hi[sl].bitcast(F32),
                                                    ALU.subtract).then_inc(ft_lo, inc(t))
                    if b in U_END:
                        s, n = U_END[b], WIDTH[U_END[b]]
                        dve.wait_ge(pe_used, n0 + (b + HL))
                        for t in range(nt):
                            dve.wait_ge(sg_a, at(T * s + t + 1))
                            nc.vector.tensor_tensor(sg[:, t, 0:n], sg[:, t, 0:n], ps[:, nt + t, 0:n], ALU.mult)\
                                .then_inc(gu_v, inc(t))
                    if between is not None:
                        between(b)

            def loop_conv(e):
                done = [HL]

                def to(end, next_too=False):
                    while done[0] < (end if next_too else min(end, EB)):
                        conv_lo(dve, B_MOE + done[0], e * EB + (B_MOE + done[0]))
                        done[0] += 1
                return to

            def one_hot(e):
                for m in range(T):
                    ins = nc.vector.tensor_scalar(oh[:, m, :], cst("slots"), posm[:, m, bass.ds(e, 1)], None, ALU.is_equal)
                ins.then_inc(oh_v, 1)

            def gathered(t, half, n, inc):
                dve.wait_ge(ga_hi, n)
                sl = (slice(None), slice(4 * half, 4 * half + 4), slice(t * P, (t + 1) * P))
                nc.vector.tensor_tensor(hT_lo[sl], ps[:, 6 + half, :].rearrange("p (k n) -> p k n", n=P),
                                        hT_hi[sl].bitcast(F32), ALU.subtract).then_inc(ga_lo, inc)

            def scattered(nt, e, i, m, half, col):
                dve.wait_ge(sc_ps, e * 18 + (i + 1))
                cols = slice(512 * half, 512 * (half + 1))
                nc.vector.scalar_tensor_tensor(out=acc[:, m, cols], in0=ps[:, 6 + half, :],
                                               scalar=comb[:, m, bass.ds(col, 1)], in1=acc[:, m, cols],
                                               op0=ALU.mult, op1=ALU.add).then_inc(sc_v, sc_inc(nt, i))

            def split_y(nt, e, t):
                own = t >= 0
                i, b = (nt - 1 - t, down_bank(nt, t)) if own else (0, 4)
                dve.wait_ge(y_hi, y_at(nt, e, t))
                nc.vector.tensor_tensor(y_of(fT_lo, i), ps[:, b:b + 2, :].rearrange("p a n -> p (a n)"),
                                        y_of(fT_hi, i).bitcast(F32), ALU.subtract).then_inc(y_lo, 1 if own else T + 1 - nt)

            def expert(nt, e):
                conv = loop_conv(e)
                for i in range(2 * (nt - 1)):
                    gathered(1 + i // 2, i % 2, e * 6 + (i + 3), 1)

                def between(b):
                    if b == Y_LAST:
                        split_y(nt, e, -1)
                    if b in SCATTER:
                        i = SCATTER[b]
                        scattered(nt, e, i, i // 2, i % 2, e)
                    if b == ONE_HOT:
                        dve.wait_ge(oht_ev, e * T + T)
                        one_hot(e + 1)
                    if b in GATHER:
                        half = GATHER[b]
                        gathered(0, half, e * 6 + (7 + half), ga_inc(nt, half))

                feed(nt, e * EB + B_MOE, e + 1, conv, between)
                for t in range(nt - 1):
                    split_y(nt, e, t)
                    for m in range(T):
                        for half in range(2):
                            scattered(nt, e, 6 + 6 * t + 2 * m + half, m, half, e + 1)
                with dve.If(e < E - 1):
                    conv(EB + HL, next_too=True)

            def route():
                dve.wait_ge(wr_v, 1)
                nc.vector.tensor_tensor(wr_lo[:, :, :], wr[:, :, :], wr_hi[:, :, :].bitcast(F32), ALU.subtract).then_inc(wr_v, 1)
                for t in range(T):
                    dve.wait_ge(lo_ps, t + 1)
                    chain(nc.vector.tensor_copy(logits[:, t, :], ps[:, t, 0:E]))
                    chain(nc.vector.max(best[:, t, :], logits[:, t, :]))
                    chain(nc.vector.max_index(best_i[:, t, :], best[:, t, :], logits[:, t, :]))
                chain(nc.vector.tensor_copy(best_f[:, :, :], best_i[:, :, :]))
                nc.vector.tensor_tensor(rt[:, 0, :], best[:, :, 1], best[:, :, 0], ALU.subtract).then_inc(rt_v, 1)
                for t in range(T):
                    chain(nc.vector.tensor_scalar(m1[:, t, :], cst("experts"), best_f[:, t, 0:1], None, ALU.is_equal))
                    chain(nc.vector.tensor_scalar(m2[:, t, :], cst("experts"), best_f[:, t, 1:2], None, ALU.is_equal))
                nc.vector.tensor_tensor(msk[:, :, :], m1[:, :, :], m2[:, :, :], ALU.add).then_inc(rt_v, 1)
                dve.wait_ge(rt_a, 1)
                chain(nc.vector.tensor_scalar(rt[:, 2, :], rt[:, 1, :], 1.0, None, ALU.add))
                chain(nc.vector.reciprocal(rt[:, 3, :], rt[:, 2, :]))
                chain(nc.vector.tensor_tensor(rt[:, 4, :], rt[:, 1, :], rt[:, 3, :], ALU.mult))
                for t in range(T):
                    chain(nc.vector.tensor_scalar(m1[:, t, :], m1[:, t, :], rt[:, 3, t:t + 1], None, ALU.mult))
                    chain(nc.vector.scalar_tensor_tensor(out=comb[:, t, 1:], in0=m2[:, t, :], scalar=rt[:, 4, t:t + 1],
                                                         in1=m1[:, t, :], op0=ALU.mult, op1=ALU.add))
                dve.wait_ge(pos_ps, 1)
                dve.wait_ge(rt_v, 2)
                for t in range(T):
                    chain(nc.vector.scalar_tensor_tensor(out=posm[:, t, 0:E], in0=ps[:, 3 + t, 0:E], scalar=1.0,
                                                         in1=msk[:, t, :], op0=ALU.add, op1=ALU.mult))
                chain(nc.vector.tensor_scalar(posm[:, :, :], posm[:, :, :], -1.0, None, ALU.add))
                nc.vector.memset(comb[:, :, 0:1], 0.0)
                dve.wait_ge(acc_z, 1)
                chain(nc.vector.tensor_copy(counts[:, :], ps[0:1, 6, 0:E]))
                chain(nc.vector.memset(ohT[:, :].bitcast(F32), 0.0))
                nc.vector.memset(first[:, 1:2], 0.0).then_inc(routed, 1)

            nc.vector.memset(first[:, 0:1], 0.0).then_inc(lo_done, RAW)
            nc.vector.memset(first[:, 1:2], 0.0).then_inc(pe_used, HL)
            nc.vector.memset(first[:, 2:3], 0.0).then_inc(mst_free, 1)
            nc.vector.memset(first[:, 3:4], 0.0).then_inc(mod_ev, MOD_STEP)
            nc.vector.memset(cs4[:, :, :].bitcast(F32), 0.0).then_inc(cs_zero, 1)
            dve.wait_ge(cs_hi, 1)
            nc.vector.tensor_tensor(cs4[:, :, 2:4], ccol[:, :].rearrange("p (a k) -> p k a", a=2),
                                    cs4[:, :, 0:2].bitcast(F32), ALU.subtract).then_inc(cs_lo, 1)
            with dve.Fori(0, MOD_CH // MOD_STEP) as it:
                for j in range(MOD_STEP * SB):
                    conv_lo(dve, j, it * (MOD_STEP * SB) + j)
            ahead = Ahead(dve, conv_lo, B_IN)
            norm(0, 0)
            dense(IN_CH, tables)
            rotary()
            attention(0)
            retention()
            turn_in(1)
            dense(OUT_CH[0])
            residual(OUT_CH[0], 0)
            norm(1, 2)
            dve.wait_ge(stored, 16 * 6)
            feed(T, B_FFN, None, lambda end: ahead.to(min(B_FFN + end, B_MOE)))
            ahead.to(B_QKV + HL)
            dve.wait_ge(gate_ev, 2)
            for t in range(T):
                for half in range(2):
                    dve.wait_ge(pe_used, B_FFN + EB + HL)
                    add_to_x(t, slice(512 * half, 512 * (half + 1)), ps[:, 2 * t + half, :])
            norm(2, 3)
            dense(QKV_CH)
            attention(1)
            turn_in(4)
            dense(OUT_CH[1])
            residual(OUT_CH[1], 2)
            norm(3, 5)
            nc.vector.memset(posm[:, :, E:], 0.0)
            route()
            one_hot(0)
            for j in range(HL):
                conv_lo(dve, B_MOE + j)
            for half in range(2):
                gathered(0, half, half + 1, 1)
            with dve.Fori(0, E) as e:
                n_tok = dve.value_load(counts[0:1, bass.ds(e, 1)], min_val=0, max_val=T * P)
                with dve.If(n_tok < P + 1):
                    expert(1, e)
                with dve.Else():
                    with dve.If(n_tok < 2 * P + 1):
                        expert(2, e)
                    with dve.Else():
                        expert(3, e)
                    dve.nop()
            split_y(T, E, -1)
            for i in range(6):
                scattered(T, E, i, i // 2, i % 2, E)
            dve.wait_ge(gate_ev, 4)
            dve.wait_ge(sc_v, E * 18 + 6)
            for t in range(T):
                chain(nc.vector.tensor_tensor(acc[:, t, :], acc[:, t, :], gate[:, min(t, 1), :], ALU.mult))
                nc.vector.tensor_tensor(x[:, t, :], x[:, t, :], acc[:, t, :], ALU.add).then_inc(x_upd, 1)
            norm_rows(4)


_INS = ['x_prompt', 'x_sample', 'cache_a_k', 'cache_a_v', 'state_ret_fwd', 'state_ret_bwd', 'cache_c_k',
        'cache_c_v', 'c', 'c_ctx', 'mod_w', 'mod_b', 'norm1_g', 'norm2_g', 'final_g', 'ev_w_in', 'ev_w_out',
        'ev_sink', 'ev_ret_logit_fwd', 'ev_ret_logit_bwd', 'ev_ffn_w_gu', 'ev_ffn_w_down', 'od_w_qkv',
        'od_w_out', 'od_rpb', 'od_w_router', 'od_moe_w_gu', 'od_moe_w_down']
_OUTS = [(1, 128, 1024), (1, 256, 1024), (1, 1, 128, 2, 64), (1, 1, 128, 2, 64), (1, 1, 8, 64, 64),
         (1, 1, 8, 64, 64), (1, 1, 128, 16, 64), (1, 1, 128, 16, 64)]


def kernel(**inputs):
    import concourse.bacc as _bacc
    from concourse.bass_utils import run_bass_kernel_spmd as _run

    nc = _bacc.Bacc("TRN2", target_bir_lowering=False, num_devices=1)
    arrays, args = {}, []
    for name in _INS:
        a = inputs[name]
        arrays[f"in_{name}"] = np.ascontiguousarray(a[..., ::-1] if name == "od_rpb" else a)
    arrays["constants"] = constants()
    for name, a in arrays.items():
        args.append(nc.dram_tensor(name, a.shape, mybir.dt.from_np(a.dtype), kind="ExternalInput").ap())
    outs = [nc.dram_tensor(f"out_{i}", shape, F32, kind="ExternalOutput").ap() for i, shape in enumerate(_OUTS)]
    build(nc, args, outs)
    r = _run(nc, [arrays], core_ids=[0])
    return tuple(r.results[0][f"out_{i}"] for i in range(len(_OUTS)))
```

```python
from contextlib import ExitStack

import numpy as np

import concourse.bass as bass
from concourse import mybir

F32 = mybir.dt.float32
F32R = mybir.dt.float32r
I32 = mybir.dt.int32
U32 = mybir.dt.uint32
ALU = mybir.AluOpType
ACT = mybir.ActivationFunctionType
AX = mybir.AxisListType.X

P = 128
D = 1024
KD = D // P
T = 3
DH = 64
GRID_W = 64
A_HEADS, A_KV_HEADS, B_HEADS, C_HEADS = 8, 2, 8, 16
A_Q, A_KV, B_W = A_HEADS * DH, A_KV_HEADS * DH, B_HEADS * DH
NB_ROWS, NB_COLS = 8, 16
C_W = C_HEADS * DH
IN_EVEN = A_Q + 2 * A_KV + 4 * B_W
O_QA, O_KA, O_VA = 0, A_Q, A_Q + A_KV
O_QR = O_VA + A_KV
O_KR, O_VR, O_GR = O_QR + B_W, O_QR + 2 * B_W, O_QR + 3 * B_W
FF = 2816
E = 8
EPS = 1e-6
NEG = -1e30
SCALE = DH ** -0.5

RAW = 6
HL = 3
BLK = 1024
SB = 4
FS = 512
NS = -(-FF // FS)
FF_PH = []
for _s in range(NS):
    for _g in range(2):
        _n = min(FS, FF - _s * FS)
        _j = FF_PH[-1][2] + FF_PH[-1][3] if FF_PH else 0
        FF_PH.append((_s, _g, _j, KD * _n // BLK, _s * FS, _n))
GB = FF_PH[-1][2] + FF_PH[-1][3]
DB = FF // P
EB = GB + DB
MOD_CH, MOD_STEP = 12, 3
B_MOD0 = 0
B_MOD1 = B_MOD0 + MOD_CH * SB
MOD_EARLY, MOD_PER = 2, 2
IN_BLOCKS = IN_EVEN * KD // BLK
B_OUT0 = B_MOD1 + MOD_CH * SB + IN_BLOCKS
N_MOD1, N_IN = [B_MOD1 + b for b in range(MOD_EARLY * SB)], []
while len(N_MOD1) + len(N_IN) < MOD_CH * SB + IN_BLOCKS:
    N_IN.append(B_MOD1 + len(N_MOD1) + len(N_IN))
    for _ in range(min(MOD_PER, MOD_CH * SB - len(N_MOD1))):
        N_MOD1.append(B_MOD1 + len(N_MOD1) + len(N_IN))
assert len(N_IN) == IN_BLOCKS and SB % MOD_PER == 0
B_FFN = B_OUT0 + 2 * SB
B_QKV = B_FFN + EB
B_OUT1 = B_QKV + 6 * SB
B_MOE = B_OUT1 + 2 * SB
assert IN_EVEN % 512 == 256 and EB % RAW == 0 and EB % HL == 0 and (MOD_STEP * SB) % RAW == 0
PADW = 127
DR = 7

CONSTS = {}
_at = 0
for _name, _n in (("ident", P), ("ones", P), ("before", P), ("slots", T * P), ("experts", E), ("sel", 4 * P),
                  ("ropec", 2 * DH), ("ropes", 2 * DH), ("mask0", 2 * 3 * P), ("ahead", P), ("behind", P),
                  ("is_ahead", P), ("is_behind", P), ("decay_at", 2 * P), ("kcol", 2), ("cmask", GRID_W)):
    CONSTS[_name] = (_at, _n)
    _at += _n
NCONST = _at


def constants():
    c = np.zeros((P, NCONST), np.float32)

    def put(name, a):
        o, n = CONSTS[name]
        c[:, o:o + n] = np.asarray(a, np.float64).reshape(P, n)

    i = np.arange(P)
    put("ident", np.eye(P))
    put("ones", np.ones((P, P)))
    put("before", i[:, None] < i[None, :])
    put("slots", np.tile(np.arange(T * P), (P, 1)))
    put("experts", np.tile(np.arange(E), (P, 1)))
    sel = np.zeros((4, 32, 4, P))
    for m, rows in enumerate(((0, 2, 4), (1, 3, 4), (0, 2, 4, 5), (1, 3, 4, 5))):
        for r in rows:
            sel[:, r, m] = 1
    put("sel", sel.reshape(P, 4 * P))
    nf = DH // 4
    inv = 10000.0 ** (-np.arange(nf, dtype=np.float32) / np.float32(nf))
    t = np.arange(2 * P)
    ang = np.stack([(t // GRID_W)[:, None] * inv, (t % GRID_W)[:, None] * inv], 1).astype(np.float32)
    cos, sin = np.cos(ang), np.sin(ang)
    put("ropec", np.concatenate([cos, cos], -1).reshape(2, P, DH).transpose(1, 0, 2))
    put("ropes", np.concatenate([-sin, sin], -1).reshape(2, P, DH).transpose(1, 0, 2))
    m0 = np.zeros((P, 2, 3 * P))
    m0[:, 0, 2 * P:] = np.where(i[None, :] + P - i[:, None] <= P, 0, NEG)
    m0[:, 1, P:2 * P] = np.where(i[:, None] + P - i[None, :] <= P, 0, NEG)
    put("mask0", m0)
    d = i[None, :] - i[:, None]
    put("ahead", np.maximum(d, 0))
    put("behind", np.maximum(-d, 0))
    put("is_ahead", d >= 0)
    put("is_behind", d <= 0)
    put("decay_at", np.tile(np.concatenate([i + 1, P - i]), (P, 1)))
    put("kcol", np.stack([P - 1 - i, i], 1))
    cq = i % GRID_W
    ck = np.arange(GRID_W)
    start = np.clip(cq - NB_COLS // 2, 0, GRID_W - NB_COLS)
    ok = (ck[None] >= start[:, None]) & (ck[None] < start[:, None] + NB_COLS)
    put("cmask", np.where(ok, 0, NEG))
    return c


def build(nc, a, outs):
    (x_prompt, x_sample, cache_a_k, cache_a_v, st_f, st_b, cache_c_k, cache_c_v, c_in, c_ctx, mod_w, mod_b,
     norm1_g, norm2_g, final_g, w_in, w_out0, sink, lg_f, lg_b, w_gu, w_down, w_qkv, w_out1, rpb, w_router,
     moe_gu, moe_down, const) = a
    y_prompt, y_sample, new_a_k, new_a_v, new_f, new_b, new_c_k, new_c_v = outs

    mods = nc.dram_tensor("mods_scratch", [4, 2 * MOD_CH * 512], F32).ap()
    padded = nc.dram_tensor("rpb_scratch", [C_HEADS * DR, PADW], F32).ap()

    with ExitStack() as ctx:
        def sem(name):
            return ctx.enter_context(nc.semaphore(name))

        top = [0]

        def sb(name, shape, dt=F32, at=None):
            n = 4 * int(np.prod(shape[1:]))
            n = (n + 31) // 32 * 32
            o = top[0] if at is None else at
            h = nc.alloc_sbuf_tensor_at(name, shape, dt, offset=o)
            if at is None:
                top[0] = o + n
            return h

        first = ctx.enter_context(nc.sbuf_tensor("first", [P, 8], F32))
        top[0] = (nc.sbuf_base + 63) // 32 * 32
        x = sb("x", [P, T, D])
        keep = sb("keep", [P, CONSTS["ropec"][0]])
        rawb = sb("rawb", [P, RAW, BLK])
        whi = sb("whi", [P, HL, BLK], F32R)
        wlo = sb("wlo", [P, HL, BLK], F32R)
        hT_hi = sb("hT_hi", [P, KD, T * P], F32R)
        hT_lo = sb("hT_lo", [P, KD, T * P], F32R)
        mrow = sb("mrow", [P, D])
        gate = sb("gate", [P, 2, D])
        gbc = sb("gbc", [P, D])
        st = sb("st", [P, 64])
        comb = sb("comb", [P, T, 1 + E])
        posm = sb("posm", [P, T, E + 1])
        counts = sb("counts", [1, E], I32)
        region = top[0]
        top[0] = region
        h = sb("h", [P, T, D])
        act_at = top[0]
        acc = sb("acc", [P, T, D])
        fT_hi = sb("fT_hi", [P, DB, T * P], F32R)
        fT_lo = sb("fT_lo", [P, DB, T * P], F32R)
        sg_at = top[0]
        sg = sb("sg", [P, T, FS])
        ohT_more = sb("ohT_more", [P, T - 1, T * P], F32R, at=sg_at)
        oh = sb("oh", [P, T, T * P])
        ohT = sb("ohT", [P, T * P], F32R)
        ff_top = top[0]
        top[0] = act_at + 12 * 1024
        wr = sb("wr", [P, KD, E])
        wr_hi = sb("wr_hi", [P, KD, E], F32R)
        wr_lo = sb("wr_lo", [P, KD, E], F32R)
        logits = sb("logits", [P, T, E])
        best = sb("best", [P, T, 8])
        best_i = sb("best_i", [P, T, 8], U32)
        best_f = sb("best_f", [P, T, 8])
        m1 = sb("m1", [P, T, E])
        m2 = sb("m2", [P, T, E])
        msk = sb("msk", [P, T, E])
        rt = sb("rt", [P, 8, T])
        top[0] = act_at
        crow = sb("crow", [16, P])
        ccol = sb("ccol", [P, 16])
        padrow = sb("padrow", [C_HEADS * DR, PADW])
        mst_at = act_at + 10 * 1024
        mst = sb("mst", [4, MOD_STEP, 512], at=mst_at)
        top[0] = act_at
        mr_hi = sb("mr_hi", [P, D], F32R)
        mr_lo = sb("mr_lo", [P, D], F32R)
        sel_r = sb("sel_r", [P, 4 * P], F32R)
        top[0] = region
        s_sc = sb("s_sc", [P, 2, 3 * P])
        s_p = sb("s_p", [P, 2, 3 * P])
        s_pT = sb("s_pT", [P, 2, 3 * P])
        a_neg = sb("a_neg", [P, 3, 2])
        a_sum = sb("a_sum", [P, 3, 2])
        a_es = sb("a_es", [P, 3, 2])
        a_rec = sb("a_rec", [P, 3, 2])
        mst1 = sb("mst1", [4, 512])
        assert top[0] <= act_at
        top[0] = act_at
        kT = sb("kT", [P, 2, 4 * P])
        qT = sb("qT", [P, 2, T * P])
        shared = top[0]
        proj0 = sb("proj0", [P, T, IN_EVEN])
        more = sb("more", [P, NCONST - CONSTS["ropec"][0]])
        ck0 = sb("ck0", [P, A_KV])
        cv0 = sb("cv0", [P, A_KV])
        kdup = sb("kdup", [P, 4, 2 * A_KV])
        sinks = sb("sinks", [P, 2, A_HEADS])
        lg = sb("lg", [P, 3, 8])
        lgt = sb("lgt", [P, 3, 8])
        logd = sb("logd", [P, 3, 8])
        dm = sb("dm", [P, B_HEADS, P])
        dq = sb("dq", [P, 2, 4, P])
        kdec = sb("kdec", [P, 2, 8])
        cdec = sb("cdec", [P, 2, 4])
        S0 = sb("S0", [P, 2, 4, DH])
        SS = sb("SS", [P, 2, 4, DH])
        up = sb("up", [P, 2, 4, DH])
        gst = sb("gst", [P, 4, T, 8])
        kd_at = top[0]
        kd = sb("kd", [P, 4, B_W])
        rqT = sb("rqT", [P, 2, T * P])
        rkT = sb("rkT", [P, 2, T * P])
        rqd = sb("rqd", [P, 2, 2, 2 * P])
        rat = sb("rat", [P, 2, T * P])
        cs4 = sb("cs4", [P, 4 * KD + P], F32R)
        top0 = top[0]
        rot = sb("rot", [P, 2, 640], at=kd_at)
        dm2 = sb("dm2", [P, B_HEADS, P], at=kd_at + 8 * 1024)
        gn = sb("gn", [P, T, B_W], at=kd_at)
        gn2 = sb("gn2", [P, T, B_W], at=kd_at + 4 * T * B_W)
        tmp_w = sb("tmp_w", [P, T, D], at=region)
        top[0] = shared
        proj1 = sb("proj1", [P, T, 3 * C_W])
        ck1 = sb("ck1", [P, C_W])
        cv1 = sb("cv1", [P, C_W])
        bm = sb("bm", [P, 2, 2, 2, 3 * P])
        bmr = sb("bmr", [P, 2, 4, 4, GRID_W])
        cm = sb("cm", [P, GRID_W])
        assert max(ff_top, top0, top[0]) <= nc.sbuf_usable_end, (ff_top, top0, top[0], nc.sbuf_usable_end)

        ps = ctx.enter_context(nc.psum_tensor("ps", [P, 8, 512], F32))

        def cst(name):
            o, n = CONSTS[name]
            base = CONSTS["ropec"][0]
            return keep[:, o:o + n] if o < base else more[:, o - base:o - base + n]

        ident = cst("ident")
        cs_by_k = cs4[:, 0:4 * KD].rearrange("p (k c) -> p k c", c=4)

        w_loaded = [sem(f"w_loaded{i}") for i in range(RAW)]
        hi_done = sem("hi_done")
        lo_done = sem("lo_done")
        pe_used = sem("pe_used")
        x_in = sem("x_in")
        keep_in = sem("keep_in")
        more_in = sem("more_in")
        crow_in = sem("crow_in")
        g_in = sem("g_in")
        m_in = sem("m_in")
        mg_v = sem("mg_v")
        mr_z = sem("mr_z")
        mr_h = sem("mr_h")
        mr_l = sem("mr_l")
        ones_in = sem("ones_in")
        cc_t = sem("cc_t")
        cc_silu = sem("cc_silu")
        cs_zero = sem("cs_zero")
        cs_hi = sem("cs_hi")
        cs_lo = sem("cs_lo")
        mod_ev = sem("mod_ev")
        mst_free = sem("mst_free")
        mod_out = sem("mod_out")
        nsq = sem("nsq")
        nms = sem("nms")
        nsd = sem("nsd")
        nrs = sem("nrs")
        bc_ps = sem("bc_ps")
        h_rows = sem("h_rows")
        gate_ps = sem("gate_ps")
        gate_ev = sem("gate_ev")
        tin_ps = sem("tin_ps")
        tin_hi = sem("tin_hi")
        tin_lo = sem("tin_lo")
        gm_ev = sem("gm_ev")
        res_t = sem("res_t")
        x_upd = sem("x_upd")
        dch = sem("dch")
        ach = sem("ach")
        rope_done = sem("rope_done")
        at_trk = sem("at_trk")
        at_trq = sem("at_trq")
        at_kT = sem("at_kT")
        at_qT = sem("at_qT")
        at_s = sem("at_s")
        at_sc = sem("at_sc")
        at_m = sem("at_m")
        at_e = sem("at_e")
        at_pt = sem("at_pt")
        at_ptev = sem("at_ptev")
        at_o = sem("at_o")
        at_es = sem("at_es")
        at_zs = sem("at_zs")
        at_done = sem("at_done")
        kv_in = sem("kv_in")
        lg_in = sem("lg_in")
        s0_in = sem("s0_in")
        tb_a = sem("tb_a")
        tb_v = sem("tb_v")
        kd_v = sem("kd_v")
        kdup_v = sem("kdup_v")
        u_ps = sem("u_ps")
        up_ev = sem("up_ev")
        ss_v = sem("ss_v")
        r_tr = sem("r_tr")
        r_q = sem("r_q")
        r_qd = sem("r_qd")
        r_at_ps = sem("r_at_ps")
        r_at_v = sem("r_at_v")
        r_o = sem("r_o")
        gn_v = sem("gn_v")
        gn_a = sem("gn_a")
        mix_done = sem("mix_done")
        pad_z = sem("pad_z")
        pad_in = sem("pad_in")
        pad_out = sem("pad_out")
        cm_in = sem("cm_in")
        bm_z = sem("bm_z")
        bm_in = [sem("bm_in0"), sem("bm_in1")]
        bm_ok = sem("bm_ok")
        c1_in = sem("c1_in")
        sg_a = sem("sg_a")
        gu_v = sem("gu_v")
        ft_ps = sem("ft_ps")
        ft_hi = sem("ft_hi")
        ft_lo = sem("ft_lo")
        y_hi = sem("y_hi")
        y_lo = sem("y_lo")
        wr_in = sem("wr_in")
        wr_v = sem("wr_v")
        lo_ps = sem("lo_ps")
        rt_v = sem("rt_v")
        rt_a = sem("rt_a")
        pos_ps = sem("pos_ps")
        routed = sem("routed")
        acc_z = sem("acc_z")
        oh_v = sem("oh_v")
        ga_ps = sem("ga_ps")
        ga_hi = sem("ga_hi")
        ga_lo = sem("ga_lo")
        oht_ps = sem("oht_ps")
        oht_ev = sem("oht_ev")
        sc_ps = sem("sc_ps")
        sc_v = sem("sc_v")
        stored = sem("stored")
        stored_sp = sem("stored_sp")

        def slot_h(b):
            return (b if b < B_MOE else b - B_MOE) % HL

        def slot_r(b):
            return (b if b < B_MOE else b - B_MOE) % RAW

        def conv_hi(act, b, n=None, loads=None):
            s, r = slot_r(b), slot_h(b)
            act.wait_ge(w_loaded[s], 16 * (b // RAW + 1) if loads is None else loads)
            act.wait_ge(pe_used, (b if n is None else n) + 1)
            nc.scalar.activation(whi[:, r, :], rawb[:, s, :], ACT.Copy).then_inc(hi_done, 1)

        def conv_lo(dve, b, n=None, loads=None):
            s, r = slot_r(b), slot_h(b)
            dve.wait_ge(hi_done, (b if n is None else n) + 1)
            nc.vector.tensor_tensor(wlo[:, r, :], rawb[:, s, :], whi[:, r, :].bitcast(F32),
                                    ALU.subtract).then_inc(lo_done, 1)

        class Ahead:

            def __init__(self, eng, conv, start):
                self.eng, self.conv, self.b = eng, conv, start

            def to(self, end):
                while self.b < end:
                    self.conv(self.eng, self.b)
                    self.b += 1

        class Chain:

            def __init__(self, eng, s):
                self.eng, self.s, self.n = eng, s, 0

            def __call__(self, ins):
                self.n += 1
                ins.then_inc(self.s, 1)
                self.eng.wait_ge(self.s, self.n)

        def mm3(out, l_hi, l_lo, r_hi, r_lo, start, stop):
            nc.tensor.matmul(out, l_hi, r_hi, start=start, stop=False)
            nc.tensor.matmul(out, l_hi, r_lo, start=False, stop=False)
            return nc.tensor.matmul(out, l_lo, r_hi, start=False, stop=stop)

        def wblk(buf, b, cols):
            return buf[:, slot_h(b), :].rearrange("p (k n) -> p k n", n=cols)

        def tiles_of(ap):
            return ap.rearrange("(t p) d -> p t d", p=P)

        def kn(w):
            return w.rearrange("(k p) n -> p k n", p=P)

        def chunks(numbers, ncols):
            out, at = [], 0
            for o in range(0, ncols, 512):
                n = min(512, ncols - o)
                k = KD * n // BLK
                out.append((numbers[at:at + k], o, n))
                at += k
            return out

        IN_CH = chunks(N_IN, IN_EVEN)
        QKV_CH = chunks(range(B_QKV, B_OUT1), 3 * C_W)
        OUT_CH = [chunks(range(B_OUT0, B_FFN), D), chunks(range(B_OUT1, B_MOE), D)]

        def mod_behind(b):
            return [i for i, m in enumerate(N_MOD1) if b < m <= b + MOD_PER and b + 1 in N_MOD1] if b in N_IN else []

        def mod_bank(c):
            return 4 + c if c < MOD_EARLY else 6 + c % 2

        def mod_buf(c):
            return mst[:, c, :] if c < MOD_EARLY else mst1[:, :]

        BEFORE = [sum(b % RAW == s for b in range(B_MOE)) for s in range(RAW)]

        def y_of(buf, i=0):
            end = DB * T * P - i * D
            return buf[:, :, :].rearrange("p a n -> p (a n)")[:, end - D:end]

        def turned(i):
            return ohT[:, :] if i == 0 else ohT_more[:, i - 1, :]

        G_END = {ph[2] + ph[3]: ph[0] for ph in FF_PH if ph[1] == 0}
        U_END = {ph[2] + ph[3]: ph[0] for ph in FF_PH if ph[1] == 1}
        TURN = {ph[2] + ph[3] - 1: ph[0] - 1 for ph in FF_PH if ph[1] == 0 and ph[0]}
        TURN[GB + 3] = NS - 1

        def turned_at(b, nt):
            return [(TURN[b], t) for t in range(min(nt, 2)) if b in TURN] + \
                   [(TURN[b - 1], 2) for _ in range(nt - 2) if b - 1 in TURN]

        WIDTH = {ph[0]: ph[5] for ph in FF_PH}
        Y_LAST = 1
        SCATTER = {b: i for i, b in enumerate((4, 6, 8, 13, 15, 17))}
        OH_TURN = {GB + 5 + 2 * t: t for t in range(T)}
        ONE_HOT = GB + 10
        GATHER = {GB + 12: 0, GB + 14: 1}

        def down_bank(nt, t):
            return 2 * t if nt == T else 4 * (t + T - 1 - nt) if nt > 1 else 4

        def sc_inc(nt, i):
            return 1 if i < 6 * nt - 1 else 6 * (T - nt) + 1

        def ga_inc(nt, half):
            return 1 + 2 * (T - nt) if half == 0 else 1

        def y_at(nt, e, t):
            return e * T + (T + 1 - nt) + (t + 1)

        GM_DONE = [0, T * len(IN_CH)]

        block = ctx.enter_context(nc.Block())

        @block.sync
        def _(sp):
            def load(b, src, n=None):
                sp.wait_ge(lo_done, (b if n is None else n) + 1)
                view = rawb[:, slot_r(b), :]
                if len(src.shape) == 3:
                    view = view.rearrange("p (k n) -> p k n", n=src.shape[2])
                sp.dma_start(view, src).then_inc(w_loaded[slot_r(b)], 16)

            def load_mod1(b):
                c, i = b // SB, b % SB
                load(N_MOD1[b], kn(mod_w[1])[:, 2 * i:2 * i + 2, 512 * c:512 * (c + 1)])

            def load_chunks(ch, w):
                for bs, o, n in ch:
                    rows = BLK // n
                    for i, b in enumerate(bs):
                        load(b, kn(w)[:, i * rows:(i + 1) * rows, o:o + n])
                        for m in mod_behind(b):
                            load_mod1(m)

            def load_ff(b0, gu, down, n0=None):
                guv = kn(gu)
                for s, g, j, k, o, n in FF_PH:
                    rows = BLK // n
                    for i in range(k):
                        load(b0 + j + i, guv[:, i * rows:(i + 1) * rows, g * FF + o:g * FF + o + n],
                             None if n0 is None else n0 + (j + i))
                for j in range(DB):
                    load(b0 + GB + j, down[j * P:(j + 1) * P, :], None if n0 is None else n0 + (GB + j))

            mw = kn(mod_w[0])
            with sp.Fori(0, MOD_CH // MOD_STEP) as it:
                for c in range(MOD_STEP):
                    for i in range(SB):
                        j = c * SB + i
                        col = it * (MOD_STEP * 512) + c * 512
                        sp.wait_ge(lo_done, it * (MOD_STEP * SB) + (j + 1))
                        sp.dma_start(rawb[:, j % RAW, :].rearrange("p (k n) -> p k n", n=512),
                                     mw[:, 2 * i:2 * i + 2, bass.ds(col, 512)]).then_inc(w_loaded[j % RAW], 16)
            for b in range(MOD_EARLY * SB):
                load_mod1(b)
            load_chunks(IN_CH, w_in[0])
            load_chunks(OUT_CH[0], w_out0[0])
            load_ff(B_FFN, w_gu[0], w_down[0])
            load_chunks(QKV_CH, w_qkv[0])
            load_chunks(OUT_CH[1], w_out1[0])
            sp.wait_ge(lo_done, B_MOE + RAW)
            with sp.Fori(0, E) as e:
                load_ff(B_MOE, moe_gu[0, bass.ds(e, 1)].rearrange("e d n -> (e d) n"),
                        moe_down[0, bass.ds(e, 1)].rearrange("e d n -> (e d) n"), n0=e * EB + B_MOE)


        @block.gpsimd
        def _(pool):
            pool.dma_start(crow[0:8, :], c_ctx.rearrange("(k p) -> k p", p=P)).then_inc(crow_in, 16)
            pool.dma_start(crow[8:16, :], c_in[0].rearrange("(k p) -> k p", p=P)).then_inc(crow_in, 16)
            nkeep = CONSTS["ropec"][0]
            pool.dma_start(keep[:, :], const[:, 0:nkeep]).then_inc(keep_in, 16)
            nc.gpsimd.memset(padrow[:, :], 0.0).then_inc(pad_z, 1)
            pool.dma_start(x[:, 0, :], x_prompt[0]).then_inc(x_in, 16)
            pool.dma_start(x[:, 1:3, :], tiles_of(x_sample[0])).then_inc(x_in, 16)
            o1 = CONSTS["ones"][0]
            pool.wait_ge(mr_z, 1)
            for q in range(3):
                pool.dma_start(mrow[32 * q + 5:32 * q + 6, :].rearrange("p (a b) -> p a b", b=P),
                               const[0:8, o1:o1 + P].unsqueeze(0)).then_inc(ones_in, 16)
            pool.dma_start(more[:, :], const[:, nkeep:NCONST]).then_inc(more_in, 16)
            pool.dma_start(ck0[:, :], cache_a_k[0, 0].rearrange("t h d -> t (h d)")).then_inc(kv_in, 16)
            pool.dma_start(cv0[:, :], cache_a_v[0, 0].rearrange("t h d -> t (h d)")).then_inc(kv_in, 16)
            pool.dma_start(sinks[:, 0, :], sink[0].partition_broadcast(P)).then_inc(kv_in, 16)
            for d, src in enumerate((lg_f, lg_b)):
                pool.dma_start(lg[:, 1 + d, :], src[0].partition_broadcast(P)).then_inc(lg_in, 16)
                for u in range(2):
                    pool.dma_start(lg[DH * u:DH * (u + 1), 0, 4 * d:4 * d + 4],
                                   src[0].rearrange("(i u) -> u i", u=2)[u].partition_broadcast(DH),
                                   allow_slow_non_contiguous=True).then_inc(lg_in, 16)
            for d, src in enumerate((st_f, st_b)):
                for u in range(2):
                    pool.dma_start(S0[DH * u:DH * (u + 1), d, :, :],
                                   src[0, 0].rearrange("(i u) k v -> u k i v", u=2)[u]).then_inc(s0_in, 16)
            pool.wait_ge(pad_z, 1)
            pool.dma_start(padded, padrow[:, :]).then_inc(pad_out, 16)
            pool.wait_ge(pad_out, 16)
            pool.dma_start(padded.rearrange("(h r) c -> h r c", r=DR)[:, :, 48:48 + 2 * NB_COLS - 1],
                           rpb[0][:, NB_ROWS - 4:NB_ROWS + 3, :]).then_inc(pad_in, 16)

            def norm_rows(n):
                lay, half = n // 2, n % 2
                if n:
                    pool.wait_ge(mr_l, n)
                g = (norm1_g, norm2_g)[half]
                pool.dma_start(gbc[:, :], g[lay].partition_broadcast(P)).then_inc(g_in, 16)
                for q in range(3):
                    c0 = lay * 6 * D + (3 * half + q) * D
                    pool.dma_start(mrow[32 * q + 4:32 * q + 5, :], mod_b[lay:lay + 1, c0 - lay * 6 * D:c0 - lay * 6 * D + D])\
                        .then_inc(m_in, 16)
                if n:
                    norm_mods(n)

            def mod_store(c):
                pool.wait_ge(mod_ev, MOD_STEP + MOD_CH + c + 1)
                o = (MOD_CH + c) * 512
                pool.dma_start(mods[:, o:o + 512], mod_buf(c)).then_inc(mod_out, 16)
                pool.wait_ge(mod_out, 16 * (MOD_CH // MOD_STEP + c + 1))

            def norm_mods(n):
                for q in range(3):
                    c0 = (n // 2) * 6 * D + (3 * (n % 2) + q) * D
                    pool.dma_start(mrow[32 * q:32 * q + 4, :], mods[:, c0:c0 + D]).then_inc(m_in, 16)

            norm_rows(0)
            with pool.Fori(0, MOD_CH // MOD_STEP) as it:
                pool.wait_ge(mod_ev, it * MOD_STEP + 2 * MOD_STEP)
                pool.dma_start(mods[:, bass.ds(it * (MOD_STEP * 512), MOD_STEP * 512)],
                               mst[:, :, :].rearrange("p a b -> p (a b)")).then_inc(mod_out, 16)
                pool.wait_ge(mod_out, it * 16 + 16)
                pool.sem_inc(mst_free, 1)

            pool.wait_ge(mod_out, 16 * (MOD_CH // MOD_STEP))
            norm_mods(0)
            for c in range(MOD_EARLY):
                mod_store(c)
            norm_rows(1)
            for c in range(MOD_EARLY, MOD_CH):
                mod_store(c)
            pool.wait_ge(gm_ev, GM_DONE[1])
            pool.dma_start(new_a_k[0, 0].rearrange("t h d -> t (h d)"), proj0[:, 0, O_KA:O_KA + A_KV]).then_inc(stored, 16)
            pool.dma_start(new_a_v[0, 0].rearrange("t h d -> t (h d)"), proj0[:, 0, O_VA:O_VA + A_KV]).then_inc(stored, 16)
            pool.wait_ge(up_ev, 2)
            for d, dst in enumerate((new_f, new_b)):
                for u in range(2):
                    pool.dma_start(dst[0, 0].rearrange("(i u) k v -> u k i v", u=2)[u],
                                   up[DH * u:DH * (u + 1), d, :, :]).then_inc(stored, 16)
            norm_rows(2)
            pool.wait_ge(x_upd, 12)
            pool.dma_start(ck1[:, :], cache_c_k[0, 0].rearrange("t h d -> t (h d)")).then_inc(c1_in, 16)
            pool.dma_start(cv1[:, :], cache_c_v[0, 0].rearrange("t h d -> t (h d)")).then_inc(c1_in, 16)
            oc = CONSTS["cmask"][0]
            pool.dma_start(cm[:, :], const[:, oc:oc + GRID_W]).then_inc(cm_in, 16)
            for r in range(2):
                nc.gpsimd.memset(bm[:, r, :, :, 0:P], 0.0).then_inc(bm_z, 1)
            pool.wait_ge(pad_in, 16)
            pool.wait_ge(cm_in, 16)

            def bias_load(i):
                if i >= 2:
                    pool.wait_ge(bm_ok, i - 1)
                for qt in range(2):
                    for rq in range(2):
                        for u in range(2):
                            row = (2 * i + u) * DR + 3 - (2 * qt + rq)
                            src = bass.AP(padded.tensor, row * PADW, [[1, GRID_W], [PADW, 4], [1, GRID_W]])
                            pool.dma_start(bmr[GRID_W * rq:GRID_W * (rq + 1), i % 2, 2 * qt + u, :, :], src)\
                                .then_inc(bm_in[i % 2], 16)

            bias_load(0)
            for i in range(8):
                if i < 7:
                    bias_load(i + 1)
                pool.wait_ge(bm_in[i % 2], 128 * (i // 2 + 1))
                if i >= 2:
                    pool.wait_ge(at_sc, 24 + 6 * (i - 1))
                v = bm[:, i % 2, :, :, P:].rearrange("p a b (k c) -> p (a b) k c", c=GRID_W)
                m = cm[:, :].unsqueeze(1).unsqueeze(1).to_broadcast([P, 4, 4, GRID_W])
                nc.gpsimd.tensor_tensor(v, bmr[:, i % 2, :, :, ::-1], m, ALU.add).then_inc(bm_ok, 1)
            pool.dma_start(new_c_k[0, 0].rearrange("t h d -> t (h d)"), proj1[:, 0, C_W:2 * C_W]).then_inc(stored, 16)
            pool.dma_start(new_c_v[0, 0].rearrange("t h d -> t (h d)"), proj1[:, 0, 2 * C_W:]).then_inc(stored, 16)
            norm_rows(3)
            pool.wait_ge(stored, 16 * 8)
            pool.wait_ge(x_upd, 18)
            pool.dma_start(wr[:, :, :], kn(w_router[0]), allow_slow_non_contiguous=True).then_inc(wr_in, 16)
            pool.wait_ge(gate_ps, 4)
            nc.gpsimd.memset(acc[:, :, :], 0.0).then_inc(acc_z, 1)
            pool.wait_ge(h_rows, 12)
            pool.dma_start(gbc[:, :], final_g.partition_broadcast(P)).then_inc(g_in, 16)
            for t in range(T):
                pool.wait_ge(h_rows, 13 + t)
                dst = y_prompt[0] if t == 0 else y_sample[0, (t - 1) * P:t * P, :]
                pool.dma_start(dst, h[:, t, :]).then_inc(stored, 16)
            pool.wait_ge(stored, 16 * 11)

        @block.tensor
        def _(pe):
            def rows_bc(b, q, m, half):
                for part in (mr_hi, mr_lo):
                    mm = nc.tensor.matmul(ps[:, b, :], sel_r[q:q + 6, m * P:(m + 1) * P],
                                          part[q:q + 6, 512 * half:512 * (half + 1)], start=(part is mr_hi),
                                          stop=(part is mr_lo))
                return mm

            def norm_bc(n):
                pe.wait_ge(mr_l, n + 1)
                for kind, part in ((1, 0), (0, 1), (0, 0), (1, 1)):
                    q, m = (96, 2 + kind) if part else (0, kind)
                    for half in range(2):
                        b = 4 * kind + 2 * (1 - part) + half
                        if n and b < 6:
                            pe.wait_ge(x_upd, 6 * (n - 1) + b + 1)
                        mm = rows_bc(b, q, m, half)
                    if kind == part:
                        mm.then_inc(bc_ps, 1)

            def norm_gate(n):
                for kind in range(2):
                    for half in range(2):
                        mm = rows_bc(4 + 2 * kind + half, 64, kind, half)
                mm.then_inc(gate_ps, 1)

            def turn_in(n, src, ready):
                for t in range(T):
                    ready(t)
                    if t == 2:
                        pe.wait_ge(tin_lo, 6 * n + 2)
                    for kh in range(2):
                        for k in range(4):
                            mm = nc.tensor.transpose(ps[:, (2 * t) % 4 + kh, k * P:(k + 1) * P],
                                                     src(t, 4 * kh + k), ident)
                        mm.then_inc(tin_ps, 1)

            def norm(n, turn):
                norm_bc(n)
                turn_in(turn, lambda t, k: h[:, t, k * P:(k + 1) * P], lambda t: pe.wait_ge(h_rows, T * n + t + 1))
                norm_gate(n)
                pe.wait_ge(tin_lo, 6 * (turn + 1))

            def mod1(b):
                c, i = b // SB, b % SB
                pe.wait_ge(lo_done, N_MOD1[b] + 1 + RAW)
                if i == 0 and c >= MOD_EARLY + 2:
                    pe.wait_ge(mod_ev, MOD_STEP + MOD_CH + c - 1)
                elif i == 0 and c >= MOD_EARLY:
                    pe.wait_ge(gate_ev, 1)
                for kk in range(2):
                    k = 2 * i + kk
                    nc.tensor.matmul(ps[:, mod_bank(c), :], cs4[:, 4 * k:4 * k + P], wblk(whi, N_MOD1[b], 512)[:, kk, :],
                                     start=(k == 0), stop=False)
                    mm = nc.tensor.matmul(ps[:, mod_bank(c), :], cs4[:, 4 * k:4 * k + P],
                                          wblk(wlo, N_MOD1[b], 512)[:, kk, :], start=False, stop=(k == KD - 1))
                mm.then_inc(pe_used, 1)

            def dense(ch, base, gates=None):
                for c, (bs, o, n) in enumerate(ch):
                    if c == 1 and gates is not None:
                        pe.wait_ge(gate_ev, gates)
                    rows = BLK // n
                    for i, b in enumerate(bs):
                        pe.wait_ge(lo_done, b + 1 + RAW)
                        for kk in range(rows):
                            k = i * rows + kk
                            for t in range(T):
                                idx = T * c + t
                                if k == 0 and idx >= 6 and base is not None:
                                    pe.wait_ge(gm_ev, base + idx - 5)
                                mm = mm3(ps[:, idx % 6, 0:n], hT_hi[:, k, t * P:(t + 1) * P],
                                         hT_lo[:, k, t * P:(t + 1) * P], wblk(whi, b, n)[:, kk, :],
                                         wblk(wlo, b, n)[:, kk, :], k == 0, k == KD - 1)
                        mm.then_inc(pe_used, 1)
                        for m in mod_behind(b):
                            mod1(m)

            def attention(lay):
                npair, u0, p0, m0 = (4, 0, 0, 0) if lay == 0 else (8, 24, 4, 12)
                proj = proj0 if lay == 0 else proj1

                def prep(i):
                    if lay == 1 or i % 2 == 0:
                        ki = i // 2 if lay == 0 else 2 + i
                        if ki:
                            pe.wait_ge(at_kT, ki)
                        for c in range(4):
                            if lay == 0:
                                src = kdup[:, c, P * ki:P * (ki + 1)]
                            else:
                                src = (ck1[:, P * i:P * (i + 1)], proj[:, 1, C_W + P * i:C_W + P * (i + 1)],
                                       proj[:, 2, C_W + P * i:C_W + P * (i + 1)],
                                       proj[:, 0, C_W + P * i:C_W + P * (i + 1)])[c]
                            mm = nc.tensor.transpose(ps[:, 4, c * P:(c + 1) * P], src, ident)
                        mm.then_inc(at_trk, 1)
                    if p0 + i:
                        pe.wait_ge(at_qT, p0 + i)
                    for t in range(T):
                        mm = nc.tensor.transpose(ps[:, 5, t * P:(t + 1) * P], proj[:, t, P * i:P * (i + 1)], ident)
                    mm.then_inc(at_trq, 1)

                def unit(n):
                    return n // 6, n % 6 // 2, n % 2

                def scores(n):
                    i, t, u = unit(n)
                    g = u0 + n
                    if n % 6 == 0:
                        pe.wait_ge(at_qT, p0 + i + 1)
                        pe.wait_ge(at_kT, i // 2 + 1 if lay == 0 else 2 + i + 1)
                    if g >= 2:
                        pe.wait_ge(at_sc, g - 1)
                    sl = (i // 2) % 2 if lay == 0 else i % 2
                    r = slice(DH * u, DH * (u + 1))
                    lo, hi = (3 * P, 4 * P) if t == 0 else (0, 3 * P)
                    nc.tensor.matmul(ps[:, g % 2, 0:hi - lo], qT[r, i % 2, t * P:(t + 1) * P], kT[r, sl, lo:hi],
                                     start=True, stop=True).then_inc(at_s, 1)

                def turn_p(n):
                    g = u0 + n
                    nk = 1 if unit(n)[1] == 0 else 3
                    pe.wait_ge(at_e, g + 1)
                    if g >= 2:
                        pe.wait_ge(at_ptev, g - 1)
                    for c in range(nk):
                        mm = nc.tensor.transpose(ps[:, 2 + g % 2, c * P:(c + 1) * P],
                                                 s_p[:, g % 2, c * P:(c + 1) * P], ident)
                    mm.then_inc(at_pt, 1)

                def values(n):
                    i, t, u = unit(n)
                    g, m = u0 + n, m0 + 3 * i + t
                    head = 2 * i + u
                    pe.wait_ge(at_ptev, g + 1)
                    if u == 0 and m >= 2:
                        pe.wait_ge(at_done, m - 1)
                    if lay == 0:
                        o = DH * (head // 4)
                        vs = [proj[:, 0, O_VA + o:O_VA + o + DH]] if t == 0 else \
                             [cv0[:, o:o + DH]] + [proj[:, c, O_VA + o:O_VA + o + DH] for c in (1, 2)]
                    else:
                        o = DH * head
                        vs = [proj[:, 0, 2 * C_W + o:2 * C_W + o + DH]] if t == 0 else \
                             [cv1[:, o:o + DH]] + [proj[:, c, 2 * C_W + o:2 * C_W + o + DH] for c in (1, 2)]
                    for c, v in enumerate(vs):
                        mm = nc.tensor.matmul(ps[:, 6 + m % 2, DH * u:DH * (u + 1)], s_pT[:, g % 2, c * P:(c + 1) * P],
                                              v, start=(c == 0), stop=(c == len(vs) - 1))
                    if u == 1:
                        mm.then_inc(at_o, 1)

                N = 6 * npair
                prep(0)
                for n in range(N + 3):
                    if n < N:
                        scores(n)
                    if 2 <= n <= N + 1:
                        turn_p(n - 2)
                    if n >= 3:
                        values(n - 3)
                    if n % 6 == 3 and n // 6 + 1 < npair:
                        prep(n // 6 + 1)

            def retention():
                pe.wait_ge(at_done, 12)
                pe.wait_ge(kd_v, 4)
                for z, t in enumerate((0, 1, 0, 2)):
                    for head in range(8):
                        i, u = head // 2, head % 2
                        mm = nc.tensor.matmul(ps[DH * u:DH * (u + 1), z, i * DH:(i + 1) * DH],
                                              kd[:, z, head * DH:(head + 1) * DH],
                                              proj0[:, t, O_VR + head * DH:O_VR + (head + 1) * DH], start=True, stop=True)
                    mm.then_inc(u_ps, 1)

                def turn(i):
                    if i:
                        pe.wait_ge(r_q, 2 * i)
                        pe.wait_ge(r_qd, i)
                    for o, bank in ((O_QR, 0), (O_KR, 1)):
                        for t in range(T):
                            mm = nc.tensor.transpose(ps[:, bank, t * P:(t + 1) * P],
                                                     proj0[:, t, o + P * i:o + P * (i + 1)], ident)
                    mm.then_inc(r_tr, 1)

                def att(j):
                    i, u = j // 2, j % 2
                    r = slice(DH * u, DH * (u + 1))
                    if u == 0:
                        pe.wait_ge(r_q, 2 * (i + 1))
                    if j >= 2:
                        pe.wait_ge(r_at_v, j - 1)
                    for t in range(T):
                        mm = nc.tensor.matmul(ps[:, 2 + j % 2, t * P:(t + 1) * P], rkT[r, i % 2, t * P:(t + 1) * P],
                                              rqT[r, i % 2, t * P:(t + 1) * P], start=True, stop=True)
                    mm.then_inc(r_at_ps, 1)

                def out(j):
                    i, u = j // 2, j % 2
                    r = slice(DH * u, DH * (u + 1))
                    pe.wait_ge(r_at_v, j + 1)
                    if u == 0:
                        pe.wait_ge(r_qd, i + 1)
                    for t in range(T):
                        o = ps[:, 5 + t, DH * j:DH * (j + 1)]
                        mm = nc.tensor.matmul(o, rat[:, j % 2, t * P:(t + 1) * P],
                                              proj0[:, t, O_VR + DH * j:O_VR + DH * (j + 1)], start=True, stop=(t == 0))
                        if t:
                            sf, sb_ = (S0, SS) if t == 1 else (SS, S0)
                            c = (t - 1) * P
                            if t == 1 and j:
                                pe.wait_ge(r_o, j)
                            nc.tensor.matmul(o, rqd[r, i % 2, 0, c:c + P], sf[r, 0, i, :], start=False, stop=False)
                            mm = nc.tensor.matmul(o, rqd[r, i % 2, 1, c:c + P], sb_[r, 1, i, :], start=False, stop=True)
                    mm.then_inc(r_o, 1)

                pe.wait_ge(up_ev, 2)
                pe.wait_ge(ss_v, 2)
                turn(0)
                for j in range(9):
                    if j < 8:
                        att(j)
                        if j % 2 == 1 and j < 7:
                            turn(j // 2 + 1)
                    if j >= 1:
                        out(j - 1)

            def feed(nt, b0, n0, u, between=None):
                def at(v):
                    return v if u is None else u * (T * NS) + v

                def inc(t):
                    return 1 if t < nt - 1 else T - nt + 1

                def begin(b):
                    if between is not None:
                        between(b)
                    for s, t in turned_at(b, nt):
                        turn(s, t)
                    pe.wait_ge(lo_done, b0 + b + 1 + RAW if n0 is None else n0 + (b + 1 + RAW))

                def turn(s, t):
                    q = s * nt + t
                    pe.wait_ge(gu_v, at(T * s + t + 1))
                    if s < 2 and between is not None:
                        pe.wait_ge(sc_v, (u - 1) * 18 + 3 * (s + 1))
                    if q >= 2:
                        ls, lt = divmod(q - 2, nt)
                        pe.wait_ge(ft_lo, at(T * ls + lt + 1))
                    for c in range(WIDTH[s] // P):
                        mm = nc.tensor.transpose(ps[:, 6 + q % 2, c * P:(c + 1) * P], sg[:, t, c * P:(c + 1) * P], ident)
                    mm.then_inc(ft_ps, inc(t))

                for s, g, j, nb, o, n in FF_PH:
                    rows = BLK // n
                    if g and not s and between is None:
                        pe.wait_ge(gate_ev, 2)
                    for i in range(nb):
                        begin(j + i)
                        for kk in range(rows):
                            k = i * rows + kk
                            for t in range(nt):
                                if k == 0 and s:
                                    pe.wait_ge(gu_v if g else sg_a, at(T * (s - 1) + t + 1))
                                mm = mm3(ps[:, nt * g + t, 0:n], hT_hi[:, k, t * P:(t + 1) * P],
                                         hT_lo[:, k, t * P:(t + 1) * P], wblk(whi, b0 + j + i, n)[:, kk, :],
                                         wblk(wlo, b0 + j + i, n)[:, kk, :], k == 0, k == KD - 1)
                        mm.then_inc(pe_used, 1)
                for j in range(DB):
                    begin(GB + j)
                    w_hi, w_lo = (wblk(w, b0 + GB + j, 512) for w in (whi, wlo))
                    for t in range(nt):
                        if j == 0:
                            pe.wait_ge(sg_a, at(T * NS))
                            if nt == T and t:
                                pe.wait_ge(gu_v, at(T * (NS - 1) + 2 * t - 1))
                        if j % 4 == 0:
                            pe.wait_ge(ft_lo, at(T * (j // 4) + t + 1))
                        for half in range(2):
                            mm = mm3(ps[:, down_bank(nt, t) + half, :], fT_hi[:, j, t * P:(t + 1) * P],
                                     fT_lo[:, j, t * P:(t + 1) * P], w_hi[:, half, :], w_lo[:, half, :],
                                     j == 0, j == DB - 1)
                    mm.then_inc(pe_used, 1)

            def gather(t, half):
                for c in range(4):
                    k = 4 * half + c
                    for m in range(T):
                        mm = nc.tensor.matmul(ps[:, 6 + half, c * P:(c + 1) * P], h[:, m, k * P:(k + 1) * P],
                                              oh[:, m, t * P:(t + 1) * P], start=(m == 0), stop=(m == T - 1))
                return mm

            def scatter(i, m, half):
                o = ps[:, 6 + half, :]
                yc = slice(512 * half, 512 * (half + 1))
                nc.tensor.matmul(o, turned(i)[:, m * P:(m + 1) * P], y_of(fT_hi, i)[:, yc], start=True, stop=False)
                return nc.tensor.matmul(o, turned(i)[:, m * P:(m + 1) * P], y_of(fT_lo, i)[:, yc], start=False, stop=True)

            def scatter_last(nt, e, i, within=True):
                if i == 0:
                    pe.wait_ge(y_lo, y_at(nt, e, -1))
                if i == 3 and within:
                    pe.wait_ge(ft_lo, (e + 1) * (T * NS) + T)
                pe.wait_ge(sc_v, e * 18 + max(i - 1, 0))
                scatter(0, i // 2, i % 2).then_inc(sc_ps, sc_inc(nt, i))

            def expert(nt, e):
                if nt > 1:
                    pe.wait_ge(sc_v, e * 18)
                for i in range(2 * (nt - 1)):
                    pe.wait_ge(ga_lo, e * 6 + (i + 1))
                    gather(1 + i // 2, i % 2).then_inc(ga_ps, 1)
                pe.wait_ge(ga_lo, e * 6 + 2 * nt)

                def between(b):
                    if b in SCATTER:
                        scatter_last(nt, e, SCATTER[b])
                    t = OH_TURN.get(b, nt)
                    if t < nt:
                        pe.wait_ge(ft_lo, (e + 1) * (T * NS) + T * NS)
                        if t > 1:
                            pe.wait_ge(oht_ev, e * T + (t - 1))
                        for m in range(T):
                            mm = nc.tensor.transpose(ps[:, 6 + t % 2, m * P:(m + 1) * P], oh[:, m, t * P:(t + 1) * P], ident)
                        mm.then_inc(oht_ps, 1 if t < nt - 1 else T - nt + 1)
                    if b in GATHER:
                        pe.wait_ge(oht_ev, e * T + T)
                        pe.wait_ge(oh_v, e + 2)
                        gather(0, GATHER[b]).then_inc(ga_ps, ga_inc(nt, GATHER[b]))

                feed(nt, B_MOE, e * EB + B_MOE, e + 1, between)
                for t in range(nt - 1):
                    pe.wait_ge(y_lo, y_at(nt, e, t))
                    for m in range(T):
                        for half in range(2):
                            i = 6 + 6 * t + 2 * m + half
                            if i < 8:
                                pe.wait_ge(ga_lo, e * 6 + (7 + half))
                            else:
                                pe.wait_ge(sc_v, e * 18 + (i - 1))
                            scatter(nt - 1 - t, m, half).then_inc(sc_ps, sc_inc(nt, i))

            pe.wait_ge(crow_in, 32)
            pe.wait_ge(keep_in, 16)
            nc.tensor.transpose(ps[:, 6, 0:16], crow[:, :], ident[0:16, 0:16]).then_inc(cc_t, 1)
            pe.wait_ge(cs_lo, 1)
            with pe.Fori(0, MOD_CH // MOD_STEP) as it:
                for c in range(MOD_STEP):
                    for i in range(SB):
                        j = c * SB + i
                        pe.wait_ge(lo_done, it * (MOD_STEP * SB) + (j + 1 + RAW))
                        if i == 0:
                            pe.wait_ge(mod_ev, it * MOD_STEP + (c + 1))
                        for kk in range(2):
                            k = 2 * i + kk
                            nc.tensor.matmul(ps[:, c, :], cs4[:, 4 * k:4 * k + P], wblk(whi, j, 512)[:, kk, :],
                                             start=(k == 0), stop=False)
                            mm = nc.tensor.matmul(ps[:, c, :], cs4[:, 4 * k:4 * k + P], wblk(wlo, j, 512)[:, kk, :],
                                                  start=False, stop=(k == KD - 1))
                        mm.then_inc(pe_used, 1)
            for b in range(MOD_EARLY * SB):
                mod1(b)
            pe.wait_ge(mod_ev, MOD_STEP + MOD_CH + MOD_EARLY)
            norm(0, 0)
            dense(IN_CH, 0, 1)
            pe.wait_ge(gm_ev, GM_DONE[1])
            pe.wait_ge(rope_done, 2)
            pe.wait_ge(kdup_v, 4)
            pe.wait_ge(kv_in, 48)
            attention(0)
            retention()
            pe.wait_ge(at_done, 12)
            turn_in(1, lambda t, k: proj0[:, t, P * k:P * (k + 1)] if k < 4 else
                    proj0[:, t, O_QR + P * (k - 4):O_QR + P * (k - 3)], lambda t: pe.wait_ge(mix_done, t + 1))
            pe.wait_ge(tin_lo, 12)
            dense(OUT_CH[0], None)
            norm(1, 2)
            feed(T, B_FFN, None, None)
            norm(2, 3)
            dense(QKV_CH, GM_DONE[1], 3)
            pe.wait_ge(gm_ev, GM_DONE[1] + T * len(QKV_CH))
            pe.wait_ge(c1_in, 32)
            attention(1)
            turn_in(4, lambda t, k: proj1[:, t, P * k:P * (k + 1)], lambda t: pe.wait_ge(at_done, 36))
            pe.wait_ge(tin_lo, 30)
            dense(OUT_CH[1], None)
            norm(3, 5)
            pe.wait_ge(wr_v, 2)
            for t in range(T):
                for k in range(KD):
                    mm = mm3(ps[:, t, 0:E], hT_hi[:, k, t * P:(t + 1) * P], hT_lo[:, k, t * P:(t + 1) * P],
                             wr_hi[:, k, :], wr_lo[:, k, :], k == 0, k == KD - 1)
                mm.then_inc(lo_ps, 1)
            pe.wait_ge(rt_v, 2)
            pe.wait_ge(gate_ev, 4)
            for t in range(T):
                for m in range(t + 1):
                    mm = nc.tensor.matmul(ps[:, 3 + t, 0:E], cst("before") if m == t else cst("ones"), msk[:, m, :],
                                          start=(m == 0), stop=(m == t))
            for m in range(T):
                mm = nc.tensor.matmul(ps[:, 6, 0:E], cst("ones"), msk[:, m, :], start=(m == 0), stop=(m == T - 1))
            mm.then_inc(pos_ps, 1)
            pe.wait_ge(routed, 1)
            pe.wait_ge(oh_v, 1)
            for half in range(2):
                gather(0, half).then_inc(ga_ps, 1)
            with pe.Fori(0, E) as e:
                n_tok = pe.value_load(counts[0:1, bass.ds(e, 1)], min_val=0, max_val=T * P)
                with pe.If(n_tok < P + 1):
                    expert(1, e)
                with pe.Else():
                    with pe.If(n_tok < 2 * P + 1):
                        expert(2, e)
                    with pe.Else():
                        expert(3, e)
                    pe.nop()
            for i in range(6):
                scatter_last(T, E, i, within=False)

        @block.scalar
        def _(act):
            chain = Chain(act, ach)

            def norm_stats(n):
                for t in range(T):
                    if n == 0 and t == 0:
                        act.wait_ge(x_in, 32)
                    elif n in (1, 2, 3):
                        act.wait_ge(x_upd, 6 * n - 4 + 2 * t if n == 2 else 6 * n - 2 + t)
                    elif n == 4:
                        act.wait_ge(x_upd, 18 + t + 1)
                    nc.scalar.activation(h[:, t, :], x[:, t, :], ACT.Square, accum_out=st[:, t:t + 1]).then_inc(nsq, 1)
                act.wait_ge(nms, n + 1)
                nc.scalar.activation(st[:, 6:9], st[:, 3:6], ACT.Sqrt).then_inc(nsd, 1)

            def split_rows(n):
                act.wait_ge(mg_v, n + 1)
                nc.scalar.activation(sel_r[:, :], cst("sel"), ACT.Copy)
                nc.scalar.activation(mr_hi[:, :], mrow[:, :], ACT.Copy).then_inc(mr_h, 1)

            def turn_in(n):
                for t in range(T):
                    for kh in range(2):
                        act.wait_ge(tin_ps, 6 * n + 2 * t + kh + 1)
                        nc.scalar.activation(hT_hi[:, 4 * kh:4 * kh + 4, t * P:(t + 1) * P],
                                             ps[:, (2 * t) % 4 + kh, :].rearrange("p (k n) -> p k n", n=P), ACT.Copy)\
                            .then_inc(tin_hi, 1)

            def norm(n, turn):
                norm_stats(n)
                turn_in(turn)
                act.wait_ge(gate_ps, n + 1)
                nc.scalar.activation(gate[:, :, :], ps[:, 4:8, :].rearrange("p (a b) n -> p a (b n)", a=2), ACT.Copy)\
                    .then_inc(gate_ev, 1)

            def mod1(b):
                ahead.to(N_MOD1[b] + 1 + HL)
                c = b // SB
                if b % SB == SB - 1:
                    act.wait_ge(pe_used, N_MOD1[b] + 1 + HL)
                    act.wait_ge(mod_out, 16 * (MOD_CH // MOD_STEP + (c if c >= MOD_EARLY else 0)))
                    nc.scalar.activation(mod_buf(c), ps[0:4, mod_bank(c), :], ACT.Copy).then_inc(mod_ev, 1)

            def dense(ch, base, proj, extra=None):
                for c, (bs, o, n) in enumerate(ch):
                    for b in bs:
                        ahead.to(min(b + HL + (b != ch[-1][0][-1]), B_MOE))
                        if b == bs[-1] and proj is not None:
                            for t in range(T):
                                idx = T * c + t
                                act.wait_ge(pe_used, b + 1 + HL)
                                nc.scalar.activation(proj[:, t, o:o + n], ps[:, idx % 6, 0:n], ACT.Copy).then_inc(gm_ev, 1)
                        ahead.to(min(b + 1 + HL, B_MOE))
                        for m in mod_behind(b):
                            mod1(m)
                    if extra is not None:
                        extra(c)

            def tables(c):
                if c == 0:
                    act.wait_ge(tb_v, 1)
                    chain(nc.scalar.activation(lgt[:, :, :], lgt[:, :, :], ACT.Exp, scale=-1.0))
                    nc.scalar.activation(lgt[:, :, :], lgt[:, :, :], ACT.Ln, bias=1.0).then_inc(tb_a, 1)
                if c == 1:
                    act.wait_ge(tb_v, 2)
                if 1 <= c <= 2:
                    for hd in range(4 * (c - 1), 4 * c):
                        nc.scalar.activation(dm[:, hd, :], cst("ahead"), ACT.Exp, scale=logd[:, 1, hd:hd + 1])
                        nc.scalar.activation(dm2[:, hd, :], cst("behind"), ACT.Exp, scale=logd[:, 2, hd:hd + 1])
                if c != 3:
                    return
                for d in range(2):
                    for i in range(4):
                        nc.scalar.activation(dq[:, d, i, :], cst("decay_at")[:, d * P:(d + 1) * P], ACT.Exp,
                                             scale=logd[:, 0, 4 * d + i:4 * d + i + 1])
                nc.scalar.activation(cdec[:, :, :], logd[:, 0, :].rearrange("p (a b) -> p a b", a=2), ACT.Exp,
                                     scale=float(P))
                nc.scalar.activation(kdec[:, :, :], kdec[:, :, :], ACT.Exp).then_inc(tb_a, 1)

            def attention(lay):
                npair, u0, p0, m0 = (4, 0, 0, 0) if lay == 0 else (8, 24, 4, 12)

                def prep(i):
                    if lay == 1 or i % 2 == 0:
                        ki = i // 2 if lay == 0 else 2 + i
                        sl = ki % 2 if lay == 0 else i % 2
                        act.wait_ge(at_trk, ki + 1)
                        nc.scalar.activation(kT[:, sl, :], ps[:, 4, :], ACT.Copy).then_inc(at_kT, 1)
                    act.wait_ge(at_trq, p0 + i + 1)
                    nc.scalar.activation(qT[:, i % 2, :], ps[:, 5, 0:T * P], ACT.Copy).then_inc(at_qT, 1)

                def exps(n):
                    t, u, g = n % 6 // 2, n % 2, u0 + n
                    m = m0 + n // 2
                    w = P if t == 0 else 3 * P
                    act.wait_ge(at_m, g + 1)
                    if g >= 2:
                        act.wait_ge(at_pt, g - 1)
                    if u == 0 and m >= 3:
                        act.wait_ge(at_done, m - 2)
                    nc.scalar.activation(s_p[:, g % 2, 0:w], s_sc[:, g % 2, 0:w], ACT.Exp, bias=a_neg[:, m % 3, u:u + 1],
                                         accum_out=a_sum[:, m % 3, u:u + 1]).then_inc(at_e, 1)

                def evac(n):
                    g = u0 + n
                    w = P if n % 6 // 2 == 0 else 3 * P
                    act.wait_ge(at_pt, g + 1)
                    nc.scalar.activation(s_pT[:, g % 2, 0:w], ps[:, 2 + g % 2, 0:w], ACT.Copy).then_inc(at_ptev, 1)

                N = 6 * npair
                prep(0)
                for n in range(N + 2):
                    if n >= 2:
                        evac(n - 2)
                    if n < N:
                        exps(n)
                        if lay == 0 and n % 2 == 1:
                            m = n // 2
                            act.wait_ge(at_zs, m + 1)
                            nc.scalar.activation(a_es[:, m % 3, :], a_es[:, m % 3, :], ACT.Exp).then_inc(at_es, 1)
                    if n % 6 == 3 and n // 6 + 1 < npair:
                        prep(n // 6 + 1)

            def retention():
                act.wait_ge(u_ps, 3)
                for d, z in ((0, 0), (1, 2)):
                    nc.scalar.activation(up[:, d, :, :], ps[:, z, 0:4 * DH].rearrange("p (a b) -> p a b", b=DH), ACT.Copy)\
                        .then_inc(up_ev, 1)
                for i in range(4):
                    act.wait_ge(r_tr, i + 1)
                    nc.scalar.activation(rqT[:, i % 2, :], ps[:, 0, 0:T * P], ACT.Copy).then_inc(r_q, 1)
                    nc.scalar.activation(rkT[:, i % 2, :], ps[:, 1, 0:T * P], ACT.Copy, scale=SCALE).then_inc(r_q, 1)
                for t in range(T):
                    nc.scalar.activation(proj0[:, t, O_GR:], proj0[:, t, O_GR:], ACT.Silu).then_inc(gn_a, 1)
                act.wait_ge(gn_v, 1)
                nc.scalar.activation(gst[:, 2, :, :], gst[:, 1, :, :], ACT.Sqrt).then_inc(gn_a, 1)

            def feed(nt, b0, n0, u, conv, between=None):
                def at(v):
                    return v if u is None else u * (T * NS) + v

                def inc(t):
                    return 1 if t < nt - 1 else T - nt + 1

                def turned(b):
                    for s, t in turned_at(b, nt):
                        n = WIDTH[s]
                        act.wait_ge(ft_ps, at(T * s + t + 1))
                        nc.scalar.activation(fT_hi[:, 4 * s:4 * s + n // P, t * P:(t + 1) * P],
                                             ps[:, 6 + (s * nt + t) % 2, 0:n].rearrange("p (c m) -> p c m", m=P),
                                             ACT.Copy).then_inc(ft_hi, inc(t))

                for b in range(EB):
                    if nt > 1:
                        turned(b)
                    conv(b + HL)
                    if nt == 1:
                        turned(b)
                    if b in G_END:
                        s, n = G_END[b], WIDTH[G_END[b]]
                        act.wait_ge(pe_used, b0 + b + HL if n0 is None else n0 + (b + HL))
                        for t in range(nt):
                            nc.scalar.activation(sg[:, t, 0:n], ps[:, t, 0:n], ACT.Silu).then_inc(sg_a, inc(t))
                    if between is not None:
                        between(b)

            def loop_conv(e):
                done = [HL]

                def to(end, next_too=False):
                    while done[0] < (end if next_too else min(end, EB)):
                        j = done[0]
                        conv_hi(act, B_MOE + j, e * EB + (B_MOE + j),
                                (e * (EB // RAW) + (BEFORE[j % RAW] + j // RAW + 1)) * 16)
                        done[0] += 1
                return to

            def gathered(t, half, n, inc):
                act.wait_ge(ga_ps, n)
                nc.scalar.activation(hT_hi[:, 4 * half:4 * half + 4, t * P:(t + 1) * P],
                                     ps[:, 6 + half, :].rearrange("p (k n) -> p k n", n=P), ACT.Copy).then_inc(ga_hi, inc)

            def take_y(nt, e, t):
                own = t >= 0
                act.wait_ge(pe_used, e * EB + (B_MOE + HL + (EB if own else 0)))
                b = down_bank(nt, t) if own else 4
                nc.scalar.activation(y_of(fT_hi, nt - 1 - t if own else 0),
                                     ps[:, b:b + 2, :].rearrange("p a n -> p (a n)"), ACT.Copy)\
                    .then_inc(y_hi, 1 if own else T + 1 - nt)

            def expert(nt, e):
                conv = loop_conv(e)
                for i in range(2 * (nt - 1)):
                    gathered(1 + i // 2, i % 2, e * 6 + (i + 3), 1)

                def between(b):
                    if b == Y_LAST:
                        take_y(nt, e, -1)
                    t = OH_TURN.get(b, nt)
                    if t < nt:
                        act.wait_ge(oht_ps, e * T + (t + 1))
                        nc.scalar.activation(turned(nt - 1 - t), ps[:, 6 + t % 2, 0:T * P], ACT.Copy)\
                            .then_inc(oht_ev, 1 if t < nt - 1 else T - nt + 1)
                    if b in GATHER:
                        half = GATHER[b]
                        gathered(0, half, e * 6 + (7 + half), ga_inc(nt, half))

                feed(nt, B_MOE, e * EB + B_MOE, e + 1, conv, between)
                for t in range(nt - 1):
                    take_y(nt, e, t)
                with act.If(e < E - 1):
                    conv(EB + HL, next_too=True)

            act.wait_ge(cc_t, 1)
            nc.scalar.activation(ccol[:, :], ps[:, 6, 0:16], ACT.Silu).then_inc(cc_silu, 1)
            act.wait_ge(cc_silu, 1)
            act.wait_ge(cs_zero, 1)
            nc.scalar.activation(cs_by_k[:, :, 0:2], ccol[:, :].rearrange("p (a k) -> p k a", a=2), ACT.Copy).then_inc(cs_hi, 1)
            with act.Fori(0, MOD_CH // MOD_STEP) as it:
                def conv(j):
                    conv_hi(act, j, it * (MOD_STEP * SB) + j, (it * (MOD_STEP * SB // RAW) + (j // RAW + 1)) * 16)

                j = 0
                for c in range(MOD_STEP):
                    while j < min((c + 1) * SB + HL, MOD_STEP * SB):
                        conv(j)
                        j += 1
                    act.wait_ge(pe_used, it * (MOD_STEP * SB) + ((c + 1) * SB + HL))
                    if c == 0:
                        act.wait_ge(mst_free, it + 1)
                    nc.scalar.activation(mst[:, c, :], ps[0:4, c, :], ACT.Copy).then_inc(mod_ev, 1)
            ahead = Ahead(act, conv_hi, B_MOD1)
            for b in range(MOD_EARLY * SB):
                mod1(b)
            split_rows(0)
            norm(0, 0)
            dense(IN_CH, 0, proj0, tables)
            attention(0)
            retention()
            turn_in(1)
            act.wait_ge(stored, 16 * 6)
            act.wait_ge(tin_ps, 12)
            split_rows(1)
            dense(OUT_CH[0], None, None)
            norm(1, 2)
            feed(T, B_FFN, None, None, lambda end: ahead.to(min(B_FFN + end, B_MOE)))
            split_rows(2)
            ahead.to(B_QKV + HL)
            norm(2, 3)
            dense(QKV_CH, GM_DONE[1], proj1)
            attention(1)
            turn_in(4)
            split_rows(3)
            dense(OUT_CH[1], None, None)
            norm(3, 5)
            act.wait_ge(wr_in, 16)
            nc.scalar.activation(wr_hi[:, :, :], wr[:, :, :], ACT.Copy).then_inc(wr_v, 1)
            act.wait_ge(rt_v, 1)
            nc.scalar.activation(rt[:, 1, :], rt[:, 0, :], ACT.Exp).then_inc(rt_a, 1)
            act.wait_ge(pe_used, B_MOE + HL)
            for j in range(HL):
                conv_hi(act, B_MOE + j, None, (BEFORE[j] + 1) * 16)
            act.wait_ge(routed, 1)
            for half in range(2):
                gathered(0, half, half + 1, 1)
            with act.Fori(0, E) as e:
                n_tok = act.value_load(counts[0:1, bass.ds(e, 1)], min_val=0, max_val=T * P)
                with act.If(n_tok < P + 1):
                    expert(1, e)
                with act.Else():
                    with act.If(n_tok < 2 * P + 1):
                        expert(2, e)
                    with act.Else():
                        expert(3, e)
                    act.nop()
            take_y(T, E, -1)
            norm_stats(4)

        @block.vector
        def _(dve):
            chain = Chain(dve, dch)

            def scale_rows(n):
                dve.wait_ge(g_in, 16 * (n + 1))
                dve.wait_ge(m_in, 96 * (n + 1))
                nc.vector.tensor_tensor(mrow[96:102, :], mrow[32:38, :], gbc[32:38, :], ALU.mult).then_inc(mg_v, 1)

            def split_rows(n):
                dve.wait_ge(mr_h, n + 1)
                nc.vector.tensor_tensor(mr_lo[:, :], mrow[:, :], mr_hi[:, :].bitcast(F32), ALU.subtract).then_inc(mr_l, 1)

            def norm_rows(n):
                dve.wait_ge(nsq, T * (n + 1))
                nc.vector.tensor_scalar(st[:, 3:6], st[:, 0:3], 1.0 / D, EPS, ALU.mult, ALU.add).then_inc(nms, 1)
                dve.wait_ge(nsd, n + 1)
                chain(nc.vector.reciprocal(st[:, 9:12], st[:, 6:9]))
                if n == 4:
                    dve.wait_ge(g_in, 16 * (n + 1))
                for t in range(T):
                    kind = min(t, 1)
                    if n < 4:
                        dve.wait_ge(bc_ps, 2 * n + kind + 1)
                    by = gbc[:, :] if n == 4 else ps[:, 4 * kind:4 * kind + 2, :].rearrange("p a n -> p (a n)")
                    ins = nc.vector.scalar_tensor_tensor(out=h[:, t, :], in0=x[:, t, :], scalar=st[:, 9 + t:10 + t],
                                                         in1=by, op0=ALU.mult, op1=ALU.mult)
                    if n == 4:
                        ins.then_inc(h_rows, 1)
                        continue
                    chain(ins)
                    nc.vector.tensor_tensor(h[:, t, :], h[:, t, :], ps[:, 4 * kind + 2:4 * kind + 4, :]
                                            .rearrange("p a n -> p (a n)"), ALU.add).then_inc(h_rows, 1)

            def turn_in(n):
                for t in range(T):
                    for kh in range(2):
                        dve.wait_ge(tin_hi, 6 * n + 2 * t + kh + 1)
                        sl = (slice(None), slice(4 * kh, 4 * kh + 4), slice(t * P, (t + 1) * P))
                        nc.vector.tensor_tensor(hT_lo[sl], ps[:, (2 * t) % 4 + kh, :].rearrange("p (k n) -> p k n", n=P),
                                                hT_hi[sl].bitcast(F32), ALU.subtract).then_inc(tin_lo, 1)

            def norm(n, turn):
                norm_rows(n)
                turn_in(turn)

            def dense(ch, extra=None, n=None):
                for c, (bs, o, w) in enumerate(ch):
                    last = min((N_MOD1[mod_behind(bs[-1])[-1]] if mod_behind(bs[-1]) else bs[-1]) + 1 + HL, B_MOE)
                    if n is not None:
                        ahead.to(min(bs[-1] + HL, B_MOE))
                        if c == 0:
                            dve.wait_ge(gate_ev, n + 1)
                        for t in range(T):
                            dve.wait_ge(pe_used, bs[-1] + 1 + HL)
                            add_to_x(t, slice(o, o + w), ps[:, T * c + t, 0:w])
                    ahead.to(last)
                    if extra is not None:
                        extra(c)

            def add_to_x(t, cols, src):
                chain(nc.vector.tensor_tensor(tmp_w[:, t, cols], src, gate[:, min(t, 1), cols], ALU.mult))
                nc.vector.tensor_tensor(x[:, t, cols], x[:, t, cols], tmp_w[:, t, cols], ALU.add).then_inc(x_upd, 1)

            def tables(c):
                if c == 0:
                    dve.wait_ge(lg_in, 96)
                    dve.wait_ge(more_in, 16)
                    nc.vector.scalar_tensor_tensor(out=lgt[:, :, :], in0=lg[:, :, :], scalar=-1.0, in1=lg[:, :, :],
                                                   op0=ALU.mult, op1=ALU.max).then_inc(tb_v, 1)
                    chain(nc.vector.tensor_scalar(logd[:, :, :], lg[:, :, :], 0.0, None, ALU.min))
                if c == 1:
                    dve.wait_ge(tb_a, 1)
                    chain(nc.vector.tensor_tensor(logd[:, :, :], logd[:, :, :], lgt[:, :, :], ALU.subtract))
                    for d in range(2):
                        ins = nc.vector.tensor_scalar(kdec[:, d, :], logd[:, 1 + d, :], cst("kcol")[:, d:d + 1], None,
                                                      ALU.mult)
                    ins.then_inc(tb_v, 1)
                if c in (2, 3):
                    rotary(c - 1)
                if c == 3:
                    double_keys()
                if c != 4:
                    return
                dve.wait_ge(tb_a, 2)

                def over_heads(name):
                    return cst(name).unsqueeze(1).to_broadcast([P, B_HEADS, P])

                chain(nc.vector.tensor_tensor(dm[:, :, :], dm[:, :, :], over_heads("is_ahead"), ALU.mult))
                chain(nc.vector.tensor_tensor(dm2[:, :, :], dm2[:, :, :], over_heads("is_behind"), ALU.mult))
                chain(nc.vector.tensor_tensor(dm[:, :, :], dm[:, :, :], dm2[:, :, :], ALU.add))
                chain(nc.vector.tensor_scalar(kdec[:, :, :], kdec[:, :, :], SCALE, None, ALU.mult))
                dve.wait_ge(kv_in, 48)
                chain(nc.vector.tensor_scalar(sinks[:, 1, :], sinks[:, 0, :], -1.0, None, ALU.mult))

            def rotary(t):
                dve.wait_ge(gm_ev, 2 * T)
                nh = (A_Q + A_KV) // DH
                v = proj0[:, t, 0:nh * DH].rearrange("p (n d) -> p n d", d=DH)
                cos = cst("ropec").rearrange("p (t d) -> p t d", t=2)[:, t - 1].unsqueeze(1).to_broadcast([P, nh, DH])
                chain(nc.vector.tensor_tensor(rot[:, 0, :].rearrange("p (n d) -> p n d", d=DH), v, cos, ALU.mult))
                v4 = proj0[:, t, 0:nh * DH].rearrange("p (n a b) -> p n a b", a=4, b=DH // 4)
                r4 = rot[:, 1, :].rearrange("p (n a b) -> p n a b", a=4, b=DH // 4)
                s4 = cst("ropes").rearrange("p (t a b) -> p t a b", t=2, a=4)[:, t - 1]
                for q in range(2):
                    sn = s4[:, q::2, :].unsqueeze(1).to_broadcast([P, nh, 2, DH // 4])
                    chain(nc.vector.tensor_tensor(r4[:, :, q::2, :], v4[:, :, 1 - q::2, :], sn, ALU.mult))
                nc.vector.tensor_tensor(proj0[:, t, 0:nh * DH], rot[:, 0, :], rot[:, 1, :], ALU.add).then_inc(rope_done, 1)
                dve.wait_ge(rope_done, t)

            def double_keys():
                dve.wait_ge(kv_in, 48)
                for c, src in enumerate((ck0[:, :], proj0[:, 1, O_KA:O_VA], proj0[:, 2, O_KA:O_VA], proj0[:, 0, O_KA:O_VA])):
                    s3 = src.rearrange("p (g d) -> p g d", g=2)
                    nc.vector.tensor_copy(kdup[:, c, :].rearrange("p (g u d) -> p g u d", g=2, u=2),
                                          s3.unsqueeze(2).to_broadcast([P, 2, 2, DH])).then_inc(kdup_v, 1)

            def attention(lay):
                npair, u0, m0 = (4, 0, 0) if lay == 0 else (8, 24, 12)
                proj = proj0 if lay == 0 else proj1

                def scaled(n):
                    i, t, u = n // 6, n % 6 // 2, n % 2
                    g, m = u0 + n, m0 + n // 2
                    w = P if t == 0 else 3 * P
                    dve.wait_ge(at_s, g + 1)
                    if g >= 2:
                        dve.wait_ge(at_e, g - 1)
                    if t == 0:
                        nc.vector.tensor_scalar(s_sc[:, g % 2, 0:w], ps[:, g % 2, 0:w], SCALE, None, ALU.mult)\
                            .then_inc(at_sc, 1)
                    else:
                        if lay == 1 and t == 1 and u == 0:
                            dve.wait_ge(bm_ok, i + 1)
                        mask = cst("mask0").rearrange("p (t n) -> p t n", t=2)[:, t - 1] if lay == 0 else \
                            bm[:, i % 2, t - 1, u, :]
                        nc.vector.scalar_tensor_tensor(out=s_sc[:, g % 2, :], in0=ps[:, g % 2, 0:w], scalar=SCALE,
                                                       in1=mask, op0=ALU.mult, op1=ALU.add).then_inc(at_sc, 1)
                    dve.wait_ge(at_sc, g + 1)
                    ins = nc.vector.reduce_max(a_neg[:, m % 3, u:u + 1], s_sc[:, g % 2, 0:w], AX, negate=True)
                    if lay == 0:
                        chain(ins)
                        hd = 2 * i + u
                        ins = nc.vector.tensor_tensor(a_neg[:, m % 3, u:u + 1], a_neg[:, m % 3, u:u + 1],
                                                      sinks[:, 1, hd:hd + 1], ALU.min)
                    ins.then_inc(at_m, 1)
                    if lay == 0 and u == 1:
                        dve.wait_ge(at_m, g + 1)
                        nc.vector.tensor_tensor(a_es[:, m % 3, :], a_neg[:, m % 3, :], sinks[:, 0, 2 * i:2 * i + 2],
                                                ALU.add).then_inc(at_zs, 1)

                def finish(k):
                    i, t, m = k // 3, k % 3, m0 + k
                    tot = a_sum[:, m % 3, :]
                    if lay == 0:
                        dve.wait_ge(at_es, k + 1)
                        chain(nc.vector.tensor_tensor(a_rec[:, m % 3, :], tot, a_es[:, m % 3, :], ALU.add))
                        tot = a_rec[:, m % 3, :]
                    dve.wait_ge(at_o, m + 1)
                    chain(nc.vector.reciprocal(a_rec[:, m % 3, :], tot))
                    nc.vector.tensor_tensor(proj[:, t, P * i:P * (i + 1)].rearrange("p (u d) -> p u d", u=2),
                                            ps[:, 6 + m % 2, 0:P].rearrange("p (u d) -> p u d", u=2),
                                            a_rec[:, m % 3, :].unsqueeze(2).to_broadcast([P, 2, DH]), ALU.mult)\
                        .then_inc(at_done, 1)

                N = 6 * npair
                for n in range(N + 3):
                    if n < N:
                        scaled(n)
                    if n % 2 == 0 and n >= 4:
                        finish((n - 4) // 2)

            def retention():
                for z, (d, t) in enumerate(((0, 0), (0, 1), (1, 0), (1, 2))):
                    nc.vector.tensor_tensor(kd[:, z, :].rearrange("p (n d) -> p n d", d=DH),
                                            proj0[:, t, O_KR:O_VR].rearrange("p (n d) -> p n d", d=DH),
                                            kdec[:, d, :].unsqueeze(2).to_broadcast([P, 8, DH]), ALU.mult).then_inc(kd_v, 1)
                dve.wait_ge(s0_in, 64)
                chain(nc.vector.tensor_tensor(SS[:, :, :, :].rearrange("p a b d -> p (a b) d"),
                                              S0[:, :, :, :].rearrange("p a b d -> p (a b) d"),
                                              cdec[:, :, :].rearrange("p a b -> p (a b)").unsqueeze(2)
                                              .to_broadcast([P, 8, DH]), ALU.mult))
                dve.wait_ge(u_ps, 4)
                for d, z in ((0, 1), (1, 3)):
                    nc.vector.tensor_tensor(SS[:, d, :, :], SS[:, d, :, :],
                                            ps[:, z, 0:4 * DH].rearrange("p (a b) -> p a b", b=DH), ALU.add).then_inc(ss_v, 1)

                def queries(i):
                    dve.wait_ge(r_q, 2 * i + 2)
                    for d in range(2):
                        ins = nc.vector.tensor_tensor(rqd[:, i % 2, d, :].rearrange("p (t n) -> p t n", t=2),
                                                      ps[:, 0, P:3 * P].rearrange("p (t n) -> p t n", t=2),
                                                      dq[:, d, i, :].unsqueeze(1).to_broadcast([P, 2, P]), ALU.mult)
                    ins.then_inc(r_qd, 1)

                queries(0)
                for j in range(8):
                    dve.wait_ge(r_at_ps, j + 1)
                    nc.vector.tensor_tensor(rat[:, j % 2, :].rearrange("p (t n) -> p t n", t=T),
                                            ps[:, 2 + j % 2, 0:T * P].rearrange("p (t n) -> p t n", t=T),
                                            dm[:, j, :].unsqueeze(1).to_broadcast([P, T, P]), ALU.mult).then_inc(r_at_v, 1)
                    if j % 2 == 1 and j < 7:
                        queries(j // 2 + 1)
                dve.wait_ge(r_o, 8)

                def heads(ap):
                    return ap.rearrange("p (n d) -> p n d", d=DH)

                for t in range(T):
                    chain(nc.vector.tensor_reduce(gst[:, 0, t, :], heads(ps[:, 5 + t, :]), AX, ALU.add))
                chain(nc.vector.tensor_scalar(gst[:, 0, :, :], gst[:, 0, :, :], 1.0 / DH, None, ALU.mult))
                for t in range(T):
                    mean = gst[:, 0, t, :].unsqueeze(2).to_broadcast([P, 8, DH])
                    chain(nc.vector.tensor_tensor(heads(gn[:, t, :]), heads(ps[:, 5 + t, :]), mean, ALU.subtract))
                chain(nc.vector.tensor_tensor(gn2[:, :, :], gn[:, :, :], gn[:, :, :], ALU.mult))
                for t in range(T):
                    chain(nc.vector.tensor_reduce(gst[:, 1, t, :], heads(gn2[:, t, :]), AX, ALU.add))
                nc.vector.tensor_scalar(gst[:, 1, :, :], gst[:, 1, :, :], 1.0 / DH, EPS, ALU.mult, ALU.add).then_inc(gn_v, 1)
                dve.wait_ge(gn_a, 4)
                chain(nc.vector.reciprocal(gst[:, 3, :, :], gst[:, 2, :, :]))
                for t in range(T):
                    rs = gst[:, 3, t, :].unsqueeze(2).to_broadcast([P, 8, DH])
                    chain(nc.vector.tensor_tensor(heads(gn[:, t, :]), heads(gn[:, t, :]), rs, ALU.mult))
                    nc.vector.tensor_tensor(proj0[:, t, O_QR:O_KR], gn[:, t, :], proj0[:, t, O_GR:], ALU.mult)\
                        .then_inc(mix_done, 1)

            def feed(nt, n0, u, conv, between=None):
                def at(v):
                    return v if u is None else u * (T * NS) + v

                def inc(t):
                    return 1 if t < nt - 1 else T - nt + 1

                def turned(b):
                    for s, t in turned_at(b, nt):
                        n = WIDTH[s]
                        dve.wait_ge(ft_hi, at(T * s + t + 1))
                        sl = (slice(None), slice(4 * s, 4 * s + n // P), slice(t * P, (t + 1) * P))
                        nc.vector.tensor_tensor(fT_lo[sl], ps[:, 6 + (s * nt + t) % 2, 0:n]
                                                .rearrange("p (c m) -> p c m", m=P), fT_hi[sl].bitcast(F32),
                                                ALU.subtract).then_inc(ft_lo, inc(t))

                def times_up(b):
                    s, n = U_END[b], WIDTH[U_END[b]]
                    dve.wait_ge(pe_used, n0 + (b + HL))
                    for t in range(nt):
                        dve.wait_ge(sg_a, at(T * s + t + 1))
                        nc.vector.tensor_tensor(sg[:, t, 0:n], sg[:, t, 0:n], ps[:, nt + t, 0:n], ALU.mult)\
                            .then_inc(gu_v, inc(t))

                for b in range(EB):
                    if nt > 1:
                        turned(b)
                    if b in U_END and nt > 1:
                        times_up(b)
                    conv(b + HL)
                    if nt == 1:
                        turned(b)
                    if b in U_END and nt == 1:
                        times_up(b)
                    if between is not None:
                        between(b)

            def loop_conv(e):
                done = [HL]

                def to(end, next_too=False):
                    while done[0] < (end if next_too else min(end, EB)):
                        conv_lo(dve, B_MOE + done[0], e * EB + (B_MOE + done[0]))
                        done[0] += 1
                return to

            def one_hot(e):
                for m in range(T):
                    ins = nc.vector.tensor_scalar(oh[:, m, :], cst("slots"), posm[:, m, bass.ds(e, 1)], None, ALU.is_equal)
                ins.then_inc(oh_v, 1)

            def gathered(t, half, n, inc):
                dve.wait_ge(ga_hi, n)
                sl = (slice(None), slice(4 * half, 4 * half + 4), slice(t * P, (t + 1) * P))
                nc.vector.tensor_tensor(hT_lo[sl], ps[:, 6 + half, :].rearrange("p (k n) -> p k n", n=P),
                                        hT_hi[sl].bitcast(F32), ALU.subtract).then_inc(ga_lo, inc)

            def scattered(nt, e, i, m, half, col):
                dve.wait_ge(sc_ps, e * 18 + (i + 1))
                cols = slice(512 * half, 512 * (half + 1))
                nc.vector.scalar_tensor_tensor(out=acc[:, m, cols], in0=ps[:, 6 + half, :],
                                               scalar=comb[:, m, bass.ds(col, 1)], in1=acc[:, m, cols],
                                               op0=ALU.mult, op1=ALU.add).then_inc(sc_v, sc_inc(nt, i))

            def split_y(nt, e, t):
                own = t >= 0
                i, b = (nt - 1 - t, down_bank(nt, t)) if own else (0, 4)
                dve.wait_ge(y_hi, y_at(nt, e, t))
                nc.vector.tensor_tensor(y_of(fT_lo, i), ps[:, b:b + 2, :].rearrange("p a n -> p (a n)"),
                                        y_of(fT_hi, i).bitcast(F32), ALU.subtract).then_inc(y_lo, 1 if own else T + 1 - nt)

            def expert(nt, e):
                conv = loop_conv(e)
                for i in range(2 * (nt - 1)):
                    gathered(1 + i // 2, i % 2, e * 6 + (i + 3), 1)

                def between(b):
                    if b == Y_LAST:
                        split_y(nt, e, -1)
                    if b in SCATTER:
                        i = SCATTER[b]
                        scattered(nt, e, i, i // 2, i % 2, e)
                    if b == ONE_HOT:
                        dve.wait_ge(oht_ev, e * T + T)
                        one_hot(e + 1)
                    if b in GATHER:
                        half = GATHER[b]
                        gathered(0, half, e * 6 + (7 + half), ga_inc(nt, half))

                feed(nt, e * EB + B_MOE, e + 1, conv, between)
                for t in range(nt - 1):
                    split_y(nt, e, t)
                    for m in range(T):
                        for half in range(2):
                            scattered(nt, e, 6 + 6 * t + 2 * m + half, m, half, e + 1)
                with dve.If(e < E - 1):
                    conv(EB + HL, next_too=True)

            def route():
                dve.wait_ge(wr_v, 1)
                nc.vector.tensor_tensor(wr_lo[:, :, :], wr[:, :, :], wr_hi[:, :, :].bitcast(F32), ALU.subtract).then_inc(wr_v, 1)
                for t in range(T):
                    dve.wait_ge(lo_ps, t + 1)
                    chain(nc.vector.tensor_copy(logits[:, t, :], ps[:, t, 0:E]))
                    chain(nc.vector.max(best[:, t, :], logits[:, t, :]))
                    chain(nc.vector.max_index(best_i[:, t, :], best[:, t, :], logits[:, t, :]))
                chain(nc.vector.tensor_copy(best_f[:, :, :], best_i[:, :, :]))
                nc.vector.tensor_tensor(rt[:, 0, :], best[:, :, 1], best[:, :, 0], ALU.subtract).then_inc(rt_v, 1)
                for t in range(T):
                    chain(nc.vector.tensor_scalar(m1[:, t, :], cst("experts"), best_f[:, t, 0:1], None, ALU.is_equal))
                    chain(nc.vector.tensor_scalar(m2[:, t, :], cst("experts"), best_f[:, t, 1:2], None, ALU.is_equal))
                nc.vector.tensor_tensor(msk[:, :, :], m1[:, :, :], m2[:, :, :], ALU.add).then_inc(rt_v, 1)
                dve.wait_ge(rt_a, 1)
                chain(nc.vector.tensor_scalar(rt[:, 2, :], rt[:, 1, :], 1.0, None, ALU.add))
                chain(nc.vector.reciprocal(rt[:, 3, :], rt[:, 2, :]))
                chain(nc.vector.tensor_tensor(rt[:, 4, :], rt[:, 1, :], rt[:, 3, :], ALU.mult))
                for t in range(T):
                    chain(nc.vector.tensor_scalar(m1[:, t, :], m1[:, t, :], rt[:, 3, t:t + 1], None, ALU.mult))
                    chain(nc.vector.scalar_tensor_tensor(out=comb[:, t, 1:], in0=m2[:, t, :], scalar=rt[:, 4, t:t + 1],
                                                         in1=m1[:, t, :], op0=ALU.mult, op1=ALU.add))
                dve.wait_ge(pos_ps, 1)
                dve.wait_ge(rt_v, 2)
                for t in range(T):
                    chain(nc.vector.scalar_tensor_tensor(out=posm[:, t, 0:E], in0=ps[:, 3 + t, 0:E], scalar=1.0,
                                                         in1=msk[:, t, :], op0=ALU.add, op1=ALU.mult))
                chain(nc.vector.tensor_scalar(posm[:, :, :], posm[:, :, :], -1.0, None, ALU.add))
                nc.vector.memset(comb[:, :, 0:1], 0.0)
                dve.wait_ge(acc_z, 1)
                chain(nc.vector.tensor_copy(counts[:, :], ps[0:1, 6, 0:E]))
                chain(nc.vector.memset(ohT[:, :].bitcast(F32), 0.0))
                nc.vector.memset(first[:, 1:2], 0.0).then_inc(routed, 1)

            nc.vector.memset(mrow[:, :], 0.0).then_inc(mr_z, 1)
            nc.vector.memset(first[:, 0:1], 0.0).then_inc(lo_done, RAW)
            nc.vector.memset(first[:, 1:2], 0.0).then_inc(pe_used, HL)
            nc.vector.memset(first[:, 2:3], 0.0).then_inc(mst_free, 1)
            nc.vector.memset(first[:, 3:4], 0.0).then_inc(mod_ev, MOD_STEP)
            nc.vector.memset(cs4[:, :].bitcast(F32), 0.0).then_inc(cs_zero, 1)
            dve.wait_ge(cs_hi, 1)
            nc.vector.tensor_tensor(cs_by_k[:, :, 2:4], ccol[:, :].rearrange("p (a k) -> p k a", a=2),
                                    cs_by_k[:, :, 0:2].bitcast(F32), ALU.subtract).then_inc(cs_lo, 1)
            with dve.Fori(0, MOD_CH // MOD_STEP) as it:
                for j in range(MOD_STEP * SB):
                    conv_lo(dve, j, it * (MOD_STEP * SB) + j)
            ahead = Ahead(dve, conv_lo, B_MOD1)
            ahead.to(N_MOD1[MOD_EARLY * SB - 1] + 1 + HL)
            dve.wait_ge(ones_in, 48)
            scale_rows(0)
            split_rows(0)
            norm(0, 0)
            dense(IN_CH, tables)
            attention(0)
            retention()
            turn_in(1)
            scale_rows(1)
            split_rows(1)
            dve.wait_ge(mod_out, 16 * (MOD_CH // MOD_STEP + MOD_CH))
            dense(OUT_CH[0], n=0)
            norm(1, 2)
            dve.wait_ge(stored, 16 * 6)
            scale_rows(2)
            feed(T, B_FFN, None, lambda end: ahead.to(min(B_FFN + end, B_MOE)))
            split_rows(2)
            ahead.to(B_QKV + HL - 1)
            dve.wait_ge(gate_ev, 2)
            for t in range(T):
                for half in range(2):
                    dve.wait_ge(pe_used, B_FFN + EB + HL)
                    add_to_x(t, slice(512 * half, 512 * (half + 1)), ps[:, 2 * t + half, :])
            ahead.to(B_QKV + HL)
            norm(2, 3)
            dense(QKV_CH)
            attention(1)
            turn_in(4)
            scale_rows(3)
            split_rows(3)
            dense(OUT_CH[1], n=2)
            norm(3, 5)
            nc.vector.memset(posm[:, :, E:], 0.0)
            route()
            one_hot(0)
            for j in range(HL):
                conv_lo(dve, B_MOE + j)
            for half in range(2):
                gathered(0, half, half + 1, 1)
            with dve.Fori(0, E) as e:
                n_tok = dve.value_load(counts[0:1, bass.ds(e, 1)], min_val=0, max_val=T * P)
                with dve.If(n_tok < P + 1):
                    expert(1, e)
                with dve.Else():
                    with dve.If(n_tok < 2 * P + 1):
                        expert(2, e)
                    with dve.Else():
                        expert(3, e)
                    dve.nop()
            split_y(T, E, -1)
            for i in range(6):
                scattered(T, E, i, i // 2, i % 2, E)
            dve.wait_ge(gate_ev, 4)
            dve.wait_ge(sc_v, E * 18 + 6)
            for t in range(T):
                chain(nc.vector.tensor_tensor(acc[:, t, :], acc[:, t, :], gate[:, min(t, 1), :], ALU.mult))
                nc.vector.tensor_tensor(x[:, t, :], x[:, t, :], acc[:, t, :], ALU.add).then_inc(x_upd, 1)
            norm_rows(4)


_INS = ['x_prompt', 'x_sample', 'cache_a_k', 'cache_a_v', 'state_ret_fwd', 'state_ret_bwd', 'cache_c_k',
        'cache_c_v', 'c', 'c_ctx', 'mod_w', 'mod_b', 'norm1_g', 'norm2_g', 'final_g', 'ev_w_in', 'ev_w_out',
        'ev_sink', 'ev_ret_logit_fwd', 'ev_ret_logit_bwd', 'ev_ffn_w_gu', 'ev_ffn_w_down', 'od_w_qkv',
        'od_w_out', 'od_rpb', 'od_w_router', 'od_moe_w_gu', 'od_moe_w_down']
_OUTS = [(1, 128, 1024), (1, 256, 1024), (1, 1, 128, 2, 64), (1, 1, 128, 2, 64), (1, 1, 8, 64, 64),
         (1, 1, 8, 64, 64), (1, 1, 128, 16, 64), (1, 1, 128, 16, 64)]


def kernel(**inputs):
    import concourse.bacc as _bacc
    from concourse.bass_utils import run_bass_kernel_spmd as _run

    nc = _bacc.Bacc("TRN2", target_bir_lowering=False, num_devices=1)
    arrays, args = {}, []
    for name in _INS:
        a = inputs[name]
        arrays[f"in_{name}"] = np.ascontiguousarray(a[..., ::-1] if name == "od_rpb" else a)
    arrays["constants"] = constants()
    for name, a in arrays.items():
        args.append(nc.dram_tensor(name, a.shape, mybir.dt.from_np(a.dtype), kind="ExternalInput").ap())
    outs = [nc.dram_tensor(f"out_{i}", shape, F32, kind="ExternalOutput").ap() for i, shape in enumerate(_OUTS)]
    build(nc, args, outs)
    r = _run(nc, [arrays], core_ids=[0])
    return tuple(r.results[0][f"out_{i}"] for i in range(len(_OUTS)))
```
